# Optimizing a Trainium2 kernel written in Bass

```python
import math
import jax, jax.numpy as jnp
from jax import lax
import numpy as np

D_MODEL = 1024
BATCH = 1
SEQ = 256
DEPTH = 1

EPS = 1e-5
NEG_INF = -1e30

A_HEADS = 8
A_HEAD_DIM = 64
A_WIDTH = A_HEADS * A_HEAD_DIM
A_PATTERNS = ((128, 1), (512, 4), (2048, 16))
A_QBLOCK = 64

B_HEADS = 8
B_NOPE = 64
B_ROPE = 32
B_V = 64
B_WIDTH = B_HEADS * B_V
Q_LORA = 256
KV_LORA = 128
ROPE_THETA = 10000.0
B_QBLOCK = 128

OFF_QA = 0
OFF_KA = OFF_QA + A_WIDTH
OFF_VA = OFF_KA + A_WIDTH
OFF_CQ = OFF_VA + A_WIDTH
OFF_CKV = OFF_CQ + Q_LORA
OFF_KR = OFF_CKV + KV_LORA
OFF_GA = OFF_KR + B_ROPE
OFF_GB = OFF_GA + D_MODEL
IN_COLS = OFF_GB + D_MODEL

N_EXPERTS = 32
TOP_K = 4
D_EXPERT = D_MODEL
SWIGLU_LIMIT = 7.0
SWIGLU_ALPHA = 1.702
MOE_BLOCK = 256

kernel_name = "hybrid_dilated_mla_moe_encoder"

def rmsnorm(x, g):
    xf = x.astype(jnp.float32)
    y = xf * lax.rsqrt(jnp.mean(xf * xf, axis=-1, keepdims=True) + EPS)
    return (y * g.astype(jnp.float32)).astype(x.dtype)

def alibi_slopes(n_heads):
    return 2.0 ** (-8.0 * (jnp.arange(n_heads, dtype=jnp.float32) + 1.0) / n_heads)

def dilated_pattern(q, k, v, window, dilation, slopes):
    B, S, H, Dh = q.shape
    hw = window // (2 * dilation)
    L = S // dilation
    nb = -(-L // A_QBLOCK)
    Lp = nb * A_QBLOCK
    W = A_QBLOCK + 2 * hw

    def strided(t):
        return t.reshape(B, L, dilation, H, Dh).transpose(0, 2, 1, 3, 4)

    qs = jnp.pad(strided(q), ((0, 0), (0, 0), (0, Lp - L), (0, 0), (0, 0)))
    kpad = ((0, 0), (0, 0), (hw, Lp - L + hw), (0, 0), (0, 0))
    ks = jnp.pad(strided(k), kpad)
    vs = jnp.pad(strided(v), kpad)
    qb = qs.reshape(B, dilation, nb, A_QBLOCK, H, Dh)
    kidx = jnp.arange(nb)[:, None] * A_QBLOCK + jnp.arange(W)[None, :]
    kb = ks[:, :, kidx]
    vb = vs[:, :, kidx]
    qpos = jnp.arange(nb)[:, None] * A_QBLOCK + jnp.arange(A_QBLOCK)[None, :]
    kpos = kidx - hw
    rel = kpos[:, None, :] - qpos[:, :, None]
    valid = (jnp.abs(rel) <= hw) & (kpos[:, None, :] >= 0) & (kpos[:, None, :] < L)
    dist = (jnp.abs(rel) * dilation).astype(jnp.float32)
    bias = -slopes[None, :, None, None] * dist[:, None, :, :]
    s = jnp.einsum('bdnqhe,bdnkhe->bdnhqk', qb, kb).astype(jnp.float32) * (A_HEAD_DIM ** -0.5)
    s = jnp.where(valid[:, None], s + bias, NEG_INF)
    m = jnp.max(s, axis=-1, keepdims=True)
    p = jnp.exp(s - m)
    l = jnp.sum(p, axis=-1)
    o = jnp.einsum('bdnhqk,bdnkhe->bdnqhe', (p / l[..., None]).astype(v.dtype), vb).astype(jnp.float32)
    lse = m[..., 0] + jnp.log(l)
    o = o.reshape(B, dilation, Lp, H, Dh)[:, :, :L].transpose(0, 2, 1, 3, 4).reshape(B, S, H, Dh)
    lse = lse.transpose(0, 1, 2, 4, 3).reshape(B, dilation, Lp, H)[:, :, :L]
    lse = lse.transpose(0, 2, 1, 3).reshape(B, S, H)
    return o, lse

def dilated_mixture(q, k, v):
    slopes = alibi_slopes(A_HEADS)
    outs, lses = [], []
    for window, dilation in A_PATTERNS:
        o, lse = dilated_pattern(q, k, v, window, dilation, slopes)
        outs.append(o)
        lses.append(lse)
    w = jax.nn.softmax(jnp.stack(lses, axis=0), axis=0)
    o = jnp.sum(w[..., None] * jnp.stack(outs, axis=0), axis=0)
    B, S = q.shape[0], q.shape[1]
    return o.reshape(B, S, A_WIDTH).astype(q.dtype)

def rope(x, cos, sin):
    xf = x.astype(jnp.float32)
    half = xf.shape[-1] // 2
    x1, x2 = xf[..., :half], xf[..., half:]
    return jnp.concatenate([x1 * cos - x2 * sin, x2 * cos + x1 * sin], axis=-1).astype(x.dtype)

def mla(c_q_raw, c_kv_raw, k_rope_raw, g_q, g_kv, w_uq, w_uk, w_uv):
    B, S, _ = c_q_raw.shape
    c_q = rmsnorm(c_q_raw, g_q)
    q = jnp.einsum('bsr,rhe->bshe', c_q, w_uq)
    q_nope, q_rope = q[..., :B_NOPE], q[..., B_NOPE:]
    c_kv = rmsnorm(c_kv_raw, g_kv)
    k_nope = jnp.einsum('bsr,rhe->bshe', c_kv, w_uk)
    v = jnp.einsum('bsr,rhe->bshe', c_kv, w_uv)
    pos = jnp.arange(S, dtype=jnp.float32)
    inv_freq = ROPE_THETA ** (-jnp.arange(0, B_ROPE, 2, dtype=jnp.float32) / B_ROPE)
    ang = pos[:, None] * inv_freq[None, :]
    cos, sin = jnp.cos(ang), jnp.sin(ang)
    q_rope = rope(q_rope, cos[None, :, None], sin[None, :, None])
    k_rope = rope(k_rope_raw, cos[None], sin[None])
    scale = (B_NOPE + B_ROPE) ** -0.5
    nb = S // B_QBLOCK
    qn = q_nope.reshape(B, nb, B_QBLOCK, B_HEADS, B_NOPE).transpose(1, 0, 2, 3, 4)
    qr = q_rope.reshape(B, nb, B_QBLOCK, B_HEADS, B_ROPE).transpose(1, 0, 2, 3, 4)

    def attend(blk):
        qn_b, qr_b = blk
        s = (jnp.einsum('bqhe,bkhe->bhqk', qn_b, k_nope)
             + jnp.einsum('bqhe,bke->bhqk', qr_b, k_rope)).astype(jnp.float32) * scale
        p = jax.nn.softmax(s, axis=-1)
        return jnp.einsum('bhqk,bkhe->bqhe', p.astype(v.dtype), v)

    o = lax.map(attend, (qn, qr))
    return o.transpose(1, 0, 2, 3, 4).reshape(B, S, B_WIDTH)

def moe(h, w_router, b_router, w_gu, b_gu, w_down, b_down):
    B, S, D = h.shape
    T = B * S
    xt = h.reshape(T, D)
    logits = (xt @ w_router + b_router).astype(jnp.float32)
    top_v, top_i = lax.top_k(logits, TOP_K)
    gates = jax.nn.softmax(top_v, axis=-1)
    N = T * TOP_K
    e_flat = top_i.reshape(N).astype(jnp.int32)
    tok_flat = (jnp.arange(N, dtype=jnp.int32) // TOP_K).astype(jnp.int32)
    g_flat = gates.reshape(N)
    order = jnp.argsort(e_flat)
    e_sorted = e_flat[order]
    counts = jnp.bincount(e_flat, length=N_EXPERTS).astype(jnp.int32)
    padded = (counts + MOE_BLOCK - 1) // MOE_BLOCK * MOE_BLOCK
    start = jnp.cumsum(counts) - counts
    pend = jnp.cumsum(padded)
    pstart = pend - padded
    rank = jnp.arange(N, dtype=jnp.int32) - start[e_sorted]
    dest = pstart[e_sorted] + rank
    NP = N + N_EXPERTS * MOE_BLOCK
    row_tok = jnp.full((NP,), T, dtype=jnp.int32).at[dest].set(tok_flat[order])
    row_w = jnp.zeros((NP,), jnp.float32).at[dest].set(g_flat[order])
    nblk = NP // MOE_BLOCK
    blk_start = jnp.arange(nblk, dtype=jnp.int32) * MOE_BLOCK
    blk_e = jnp.minimum(jnp.sum(pend[None, :] <= blk_start[:, None], axis=1), N_EXPERTS - 1).astype(jnp.int32)
    x_pad = jnp.concatenate([xt, jnp.zeros((1, D), xt.dtype)], axis=0)
    xb = x_pad[row_tok].reshape(nblk, MOE_BLOCK, D)

    def expert_block(args):
        xblk, e = args
        gu = xblk @ w_gu[e] + b_gu[e]
        gate = jnp.minimum(gu[:, :D_EXPERT], SWIGLU_LIMIT)
        up = jnp.clip(gu[:, D_EXPERT:], -SWIGLU_LIMIT, SWIGLU_LIMIT)
        act = (up + 1.0) * (gate * jax.nn.sigmoid(SWIGLU_ALPHA * gate))
        return act @ w_down[e] + b_down[e]

    yb = lax.map(expert_block, (xb, blk_e)).reshape(NP, D)
    out = jnp.zeros((T + 1, D), jnp.float32).at[row_tok].add(row_w[:, None] * yb.astype(jnp.float32))
    return out[:T].reshape(B, S, D).astype(h.dtype)

def setup_inputs(seed: int = 0) -> dict:
    key = jax.random.key(seed)
    ks = jax.random.split(key, 20)
    n = jax.random.normal
    f = jnp.float32
    return {
        "x": n(ks[0], (BATCH, SEQ, D_MODEL), f),
        "norm1_g": 1.0 + 0.02 * n(ks[1], (DEPTH, D_MODEL), f),
        "w_in": n(ks[2], (DEPTH, D_MODEL, IN_COLS), f) * D_MODEL ** -0.5,
        "q_a_norm_g": 1.0 + 0.02 * n(ks[3], (DEPTH, Q_LORA), f),
        "kv_a_norm_g": 1.0 + 0.02 * n(ks[4], (DEPTH, KV_LORA), f),
        "w_uq": n(ks[5], (DEPTH, Q_LORA, B_HEADS, B_NOPE + B_ROPE), f) * Q_LORA ** -0.5,
        "w_uk": n(ks[6], (DEPTH, KV_LORA, B_HEADS, B_NOPE), f) * KV_LORA ** -0.5,
        "w_uv": n(ks[7], (DEPTH, KV_LORA, B_HEADS, B_V), f) * KV_LORA ** -0.5,
        "w_a_out": n(ks[8], (DEPTH, A_WIDTH, D_MODEL), f) * A_WIDTH ** -0.5,
        "w_b_out": n(ks[9], (DEPTH, B_WIDTH, D_MODEL), f) * B_WIDTH ** -0.5,
        "w_o": n(ks[10], (DEPTH, D_MODEL, D_MODEL), f) * D_MODEL ** -0.5,
        "norm2_g": 1.0 + 0.02 * n(ks[11], (DEPTH, D_MODEL), f),
        "w_router": n(ks[12], (DEPTH, D_MODEL, N_EXPERTS), f) * D_MODEL ** -0.5,
        "b_router": 0.01 * n(ks[13], (DEPTH, N_EXPERTS), f),
        "w_gate_up": n(ks[14], (DEPTH, N_EXPERTS, D_MODEL, 2 * D_EXPERT), f) * D_MODEL ** -0.5,
        "b_gate_up": 0.02 * n(ks[15], (DEPTH, N_EXPERTS, 2 * D_EXPERT), f),
        "w_down": n(ks[16], (DEPTH, N_EXPERTS, D_EXPERT, D_MODEL), f) * D_EXPERT ** -0.5,
        "b_down": 0.02 * n(ks[17], (DEPTH, N_EXPERTS, D_MODEL), f),
        "final_g": 1.0 + 0.02 * n(ks[18], (D_MODEL,), f),
    }

def reference(x, norm1_g, w_in, q_a_norm_g, kv_a_norm_g, w_uq, w_uk, w_uv, w_a_out, w_b_out, w_o,
              norm2_g, w_router, b_router, w_gate_up, b_gate_up, w_down, b_down, final_g):
    B, S, D = x.shape
    for l in range(DEPTH):
        h = rmsnorm(x, norm1_g[l])
        z = h @ w_in[l]
        qa = z[..., OFF_QA:OFF_KA].reshape(B, S, A_HEADS, A_HEAD_DIM)
        ka = z[..., OFF_KA:OFF_VA].reshape(B, S, A_HEADS, A_HEAD_DIM)
        va = z[..., OFF_VA:OFF_CQ].reshape(B, S, A_HEADS, A_HEAD_DIM)
        o_a = dilated_mixture(qa, ka, va)
        o_b = mla(z[..., OFF_CQ:OFF_CKV], z[..., OFF_CKV:OFF_KR], z[..., OFF_KR:OFF_GA],
                  q_a_norm_g[l], kv_a_norm_g[l], w_uq[l], w_uk[l], w_uv[l])
        gate_a = jax.nn.sigmoid(z[..., OFF_GA:OFF_GB])
        gate_b = jax.nn.sigmoid(z[..., OFF_GB:IN_COLS])
        merged = gate_a * (o_a @ w_a_out[l]) + gate_b * (o_b @ w_b_out[l])
        x = x + merged @ w_o[l]
        h2 = rmsnorm(x, norm2_g[l])
        x = x + moe(h2, w_router[l], b_router[l], w_gate_up[l], b_gate_up[l], w_down[l], b_down[l])
    return rmsnorm(x, final_g)


_drawn_inputs = setup_inputs


def setup_inputs(seed=0):
    import zlib

    import numpy as np

    out = dict(_drawn_inputs(seed))
    spreads = {}
    factors = {'q_a_norm_g': 8.0,
     'kv_a_norm_g': 5.21,
     'b_gate_up': 5.153,
     'b_down': 24.136,
     'final_g': 24.584,
     'norm2_g': 3.252,
     'b_router': 4.075}
    for name, (base, spread) in spreads.items():
        noise = np.random.default_rng([zlib.crc32(name.encode()), seed]).standard_normal(out[name].shape)
        drawn = base * np.exp(spread * noise) if base else spread * noise
        out[name] = __import__('jax').numpy.asarray(drawn.astype(out[name].dtype))
    for name, factor in factors.items():
        out[name] = (out[name] * factor).astype(out[name].dtype)
    return out
```

```python
import math
from contextlib import ExitStack

import numpy as np

import concourse.bass as bass
from concourse import mybir

F32 = mybir.dt.float32
I32 = mybir.dt.int32
ALU = mybir.AluOpType
ACT = mybir.ActivationFunctionType
AX_X = mybir.AxisListType.X

P = 128
D = 1024
SEQ = 256
TT = SEQ // P
KT = D // P
EPS = 1e-5

HEADS = 8
HD = 64
AW = HEADS * HD
NOPE, ROPE = 64, 32
QK_B = NOPE + ROPE
Q_RANK, KV_RANK = 256, 128
LATENT = Q_RANK + KV_RANK + ROPE
OFF_LATENT = 3 * AW
OFF_GATES = OFF_LATENT + LATENT
SCALE_A = HD ** -0.5
SCALE_B = QK_B ** -0.5
PATTERNS = ((128, 1), (512, 4), (2048, 16))
NEG = -1e30
BIG = 3e38

E = 32
TOP = 4
F = D
LIMIT, ALPHA = 7.0, 1.702
CAP = 64
ROUNDS = SEQ // CAP
BANK = 512

SLOT = 2048
RING = 16
FRONT = [("latent", 2), ("qk", 4), ("v", 2), ("uq", 1), ("uk", 1), ("uv", 1), ("gates", 8), ("out", 4), ("wo", 4)]
FIRST = {}
for _name, _n in FRONT:
    FIRST[_name] = sum(n for _, n in FRONT[:len(FIRST)])
N_FRONT = sum(n for _, n in FRONT)
UP_SLOTS = KT
DOWN_SLOTS = KT // 2
PER_EXPERT = UP_SLOTS + DOWN_SLOTS
UNROLL = RING // math.gcd(RING, PER_EXPERT)
TURNS = UNROLL * PER_EXPERT // RING


def constants():
    p = np.arange(P)
    ident = np.eye(P)
    inv = 10000.0 ** (-np.arange(0, ROPE, 2, dtype=np.float32) / ROPE)
    ang = np.arange(SEQ, dtype=np.float32)[:, None] * inv[None, :].astype(np.float32)
    cos, sin = np.cos(ang), np.sin(ang)
    rope_cos = np.concatenate([cos, cos], 1).reshape(TT, P, ROPE).transpose(1, 0, 2).reshape(P, -1)
    rope_sin = np.concatenate([sin, -sin], 1).reshape(TT, P, ROPE).transpose(1, 0, 2).reshape(P, -1)
    slot = np.arange(CAP)
    none = np.full(CAP, -5 * SEQ)
    slots = np.tile(np.concatenate([slot, none, none, slot]), (P, 1))
    before = (p[:, None] < p[None, :]).astype(np.float32)
    ones = np.ones((P, P))
    fold = np.tile(np.eye(E), (P // E, 1))
    delta = p[:, None] - (np.arange(SEQ + P)[None, :] - P)
    dist = np.abs(delta)
    count = sum(((delta % d == 0) & (dist <= w // 2)).astype(int) for w, d in PATTERNS)
    log_count = np.where(count > 0, np.log(np.maximum(count, 1)), NEG)
    parts = {"ident": ident, "cos": rope_cos, "sin": rope_sin, "slots": slots, "before": before,
             "ones": ones, "fold": fold, "dist": dist, "log_count": log_count}
    at, place = 0, {}
    for name, a in parts.items():
        place[name] = (at, a.shape[1])
        at += a.shape[1]
    return np.concatenate([a.astype(np.float32) for a in parts.values()], 1), place


def build(nc, x, norm1_g, w_in, q_a_norm_g, kv_a_norm_g, w_uq, w_uk, w_uv, w_a_out, w_b_out, w_o,
          norm2_g, w_router, b_router, w_gate_up, b_gate_up, w_down, b_down, final_g, table, out):
    place = constants()[1]
    table_width = sum(n for _, n in place.values())
    fixed_width = place["dist"][0]

    with ExitStack() as ctx:
        def sb(name, shape, dt=F32):
            return ctx.enter_context(nc.sbuf_tensor(name, shape, dt))

        def sem(name):
            return ctx.enter_context(nc.semaphore(name))

        ring = sb("ring", [P, RING, SLOT])
        xrow = sb("xrow", [P, TT, D])
        const = sb("const", [P, fixed_width])
        g1 = sb("g1", [P, KT])
        gq = sb("gq", [P, Q_RANK // P])
        gkv = sb("gkv", [P, 1])
        router_w = sb("router_w", [P, KT, E])
        router_b = sb("router_b", [P, E])
        eps = sb("eps", [P, 8])
        sums = sb("sums", [P, 16])
        soft = sb("soft", [P, 2, 8])
        logits = sb("logits", [P, TT, E + TOP])
        struck = sb("struck", [P, TT, E + TOP])
        best = sb("best", [P, TT, 8])
        strike = sb("strike", [P, TT, 8])
        chosen = sb("chosen", [P, TT, E])
        expo = sb("expo", [P, TT, E])
        routing = sb("routing", [P, TT, 2 * E])
        places = sb("places", [P, TT, ROUNDS * E])
        over = sb("over", [1, ROUNDS * E + 1], I32)
        areas = {"h": 2048, "a": 4096, "g": 4096 + TT * ROPE, "s": 3072, "o": 2048, "t": 2 * (SEQ + P)}
        arena = {n: sb(f"area_{n}", [P, w]) for n, w in areas.items()}

        def view(area, at, *shape):
            n = int(np.prod(shape))
            v = arena[area][:, at:at + n]
            if len(shape) == 2:
                v = v.rearrange("p (a b) -> p a b", a=shape[0])
            if len(shape) == 3:
                v = v.rearrange("p (a b c) -> p a b c", a=shape[0], b=shape[1])
            return v

        hT = view("h", 0, KT, SEQ)
        xs = view("a", 0, TT, D)
        qmT = view("a", 0, HEADS, SEQ)
        kT = view("a", 2048, HEADS // 2, SEQ)
        va = view("a", 3072, TT, AW)
        qTb = view("a", 0, HEADS, SEQ)
        kTb = view("a", 2048, HEADS, SEQ)
        qb = xrow[:, :, 0:HEADS * QK_B]
        kcat = view("g", 0, TT, HEADS, QK_B)
        cn = view("g", 1536, TT, Q_RANK + KV_RANK)
        cT = view("g", 2304, 3, SEQ)
        rope_a = view("g", 3072, TT, HEADS, ROPE)
        rope_b = view("g", 3584, TT, HEADS, ROPE)
        kr = view("g", 4096, TT, ROPE)
        gateT = view("g", 0, 2 * KT, SEQ)
        vb = view("s", 0, TT, AW)
        probs = view("s", 1024, 2, TT, SEQ)
        probsT = view("s", 2048, 2, TT, SEQ)
        oT = view("o", 0, HEADS, SEQ)
        kr_b, kr_c = sb("kr_b", [P, TT, ROPE]), sb("kr_c", [P, TT, ROPE])
        h2 = view("h", 0, TT, D)
        up_bias = view("a", 0, 2 * F)
        down_bias = view("a", 2048, D)
        g2 = view("a", 3072, D)
        h2T = view("g", 0, KT, SEQ)
        gate_c, up_c, sig, act_v = (view("g", 512 * n, BANK) for n in range(4))
        x_e = view("g", 2048, BANK)
        xT_e = view("g", 2560, 2, BANK)
        actT = view("g", 3584, BANK)
        gf = view("s", 0, D)
        y_e = view("s", 1024, BANK)
        pick = view("s", 1536, 2, TT, CAP)
        expert_row = view("s", 1792, 2, CAP)
        routT = view("s", 1920, SEQ)
        part_rows = view("s", 2176, SEQ)
        gated = view("o", 0, 2, TT, 4 * CAP)
        gatedT = view("o", 1024, 2, 4, P)
        dist = arena["t"][:, 0:SEQ + P]
        log_count = arena["t"][:, SEQ + P:2 * (SEQ + P)]

        def cst(name):
            a, n = place[name]
            return const[:, a:a + n]
        ident = cst("ident")
        cos2 = cst("cos").rearrange("p (t n) -> p t n", t=TT)
        sin2 = cst("sin").rearrange("p (t n) -> p t n", t=TT)
        slots, before, ones, fold = (cst(n) for n in ("slots", "before", "ones", "fold"))

        ps = ctx.enter_context(nc.psum_tensor("ps", [P, 8, BANK], F32))
        GATE, UP, Y, MIX = 4, 5, 6, 7

        s_x, s_const, s_tab, s_small, s_mid = sem("x_loaded"), sem("const_loaded"), sem("table_loaded"), sem("small_loaded"), sem("mid_loaded")
        s_xagain = sem("x_again")
        s_bias = sem("bias_loaded")
        loaded = [sem(f"slot_loaded{s}") for s in range(RING)]
        freed = sem("ring_freed")
        squares, power, ms = sem("squares"), sem("power"), sem("mean_squares")
        xs_ready, hT_ps, hT_v, hT_a = sem("xs_ready"), sem("hT_ps"), sem("hT_vector"), sem("hT_scalar")
        zeroed, cleared = sem("zeroed"), sem("cleared")
        lat_sq, cn_ready, kr_ready = sem("latent_squares"), sem("cn_ready"), sem("kr_ready")
        q_ready, k_ready = sem("q_ready"), sem("k_ready")
        cT_ps, cT_ready = sem("cT_ps"), sem("cT_ready")
        va_ready = sem("va_ready")
        uq_half, qb_ready, kvb_ready = sem("uq_half"), sem("qb_ready"), sem("kvb_ready")
        roped, rope_step = sem("roped"), sem("rope_step")
        s_done, max_ready, dve_step = sem("scores_done"), sem("max_ready"), sem("dve_step")
        exp_done, probs_ready = sem("exp_done"), sem("probs_ready")
        pT_ps, pT_ready, pv_done, o_ready = sem("probsT_ps"), sem("probsT_ready"), sem("pv_done"), sem("o_ready")
        bT_ps, bq_ready, bk_ready = sem("bT_ps"), sem("bq_ready"), sem("bk_ready")
        gz_ready, gates_on = sem("gate_z_ready"), sem("gates_on")
        ab_done, merged = sem("ab_done"), sem("merged")
        x2_ready, x2_sq, h2_ready = sem("x2_ready"), sem("x2_squares"), sem("h2_ready")
        h2T_ps, h2T_v, h2T_a = sem("h2T_ps"), sem("h2T_vector"), sem("h2T_scalar")
        part_done, part_ready, logit_done, top_ready, expo_ready = sem("part_done"), sem("part_ready"), sem("logit_done"), sem("top_ready"), sem("expo_ready")
        chosen_ready, rout_ready, count_done, routT_ps, routT_ready = sem("chosen_ready"), sem("rout_ready"), sem("count_done"), sem("routT_ps"), sem("routT_ready")
        over_ready, moe_zero = sem("over_ready"), sem("moe_zero")
        pick_ready, gathered, xe_ready, xT_done, xT_ready = (sem(n) for n in ("pick_ready", "gathered", "xe_ready", "xT_done", "xT_ready"))
        gT_done, gT_ready, up_done, clamped, sig_ready = (sem(n) for n in ("gatedT_done", "gatedT_ready", "up_done", "clamped", "sig_ready"))
        act_ready, actT_done, actT_ready, y_ready = (sem(n) for n in ("act_ready", "actT_done", "actT_ready", "y_ready"))
        clamped2, raised, scattered = sem("clamped_up"), sem("raised"), sem("scattered")
        v_loaded, v_pick, v_gathered, v_xe, v_xTd, v_xT, v_gTd, v_gT = (sem("over_" + n) for n in (
            "loaded", "pick", "gathered", "xe", "xT_done", "xT", "gatedT_done", "gatedT"))
        v_up, v_cl, v_sig, v_act, v_aTd, v_aT, v_yd, v_y = (sem("over_" + n) for n in (
            "up_done", "clamped", "sig", "act", "actT_done", "actT", "y_done", "y"))
        v_cl2, v_raised = sem("over_clamped_up"), sem("over_raised")
        total, fin_sq, fin_ready, s_out = sem("total"), sem("fin_squares"), sem("fin_ready"), sem("stored")

        x_rows = x[0].rearrange("(t p) d -> p t d", p=P)
        out_rows = out[0].rearrange("(t p) d -> p t d", p=P)
        win = w_in[0].rearrange("(k p) n -> p k n", p=P)
        up_rows = w_gate_up[0].rearrange("e (k p) n -> p (e k) n", p=P)
        down_rows = w_down[0].rearrange("e (k p) n -> p (e k) n", p=P)
        ab_rows = [w[0].rearrange("(k p) n -> p k n", p=P) for w in (w_a_out, w_b_out)]
        wo_rows = w_o[0].rearrange("(k p) n -> p k n", p=P)

        def slot(n, *shape):
            v = ring[:, n % RING, 0:int(np.prod(shape))]
            if len(shape) == 2:
                v = v.rearrange("p (a b) -> p a b", a=shape[0])
            return v

        def through(name):
            return FIRST[name] + dict(FRONT)[name]

        block = ctx.enter_context(nc.Block())

        @block.sync
        def _(sp):
            front = []
            for n in range(2):
                front.append((slot(n, 4, LATENT), win[:, 4 * n:4 * n + 4, OFF_LATENT:OFF_GATES]))
            for n in range(4):
                front.append((slot(FIRST["qk"] + n, 2, 2 * AW), win[:, 2 * n:2 * n + 2, 0:2 * AW]))
            for n in range(2):
                front.append((slot(FIRST["v"] + n, 4, AW), win[:, 4 * n:4 * n + 4, 2 * AW:3 * AW]))
            front.append((slot(FIRST["uq"], 2, HEADS * QK_B), w_uq[0].rearrange("(k p) h e -> p k (h e)", p=P)))
            front.append((slot(FIRST["uk"], HEADS * NOPE), w_uk[0].rearrange("p h e -> p (h e)")))
            front.append((slot(FIRST["uv"], HEADS * HD), w_uv[0].rearrange("p h e -> p (h e)")))
            for n in range(8):
                a = OFF_GATES + n * 2 * P
                front.append((slot(FIRST["gates"] + n, KT, 2 * P), win[:, :, a:a + 2 * P]))
            for half in range(2):
                for m in range(2):
                    front.append((slot(FIRST["out"] + 2 * half + m, 4, BANK),
                                  ab_rows[m][:, :, half * BANK:(half + 1) * BANK]))
            for n in range(4):
                front.append((slot(FIRST["wo"] + n, 2, D), wo_rows[:, 2 * n:2 * n + 2, :]))
            sp.dma_start(xrow[:, :, :], x_rows).then_inc(s_x, 16)
            for n, (dst, src) in enumerate(front):
                if n >= RING:
                    sp.wait_ge(freed, n - RING + 1)
                sp.dma_start(dst, src).then_inc(loaded[n % RING], 16)
            with sp.Fori(0, E // UNROLL) as i:
                for u in range(UNROLL):
                    for j in range(PER_EXPERT):
                        n = N_FRONT + u * PER_EXPERT + j
                        sp.wait_ge(freed, i * (UNROLL * PER_EXPERT) + (n - RING + 1))
                        if j < UP_SLOTS:
                            dst = ring[:, n % RING:n % RING + 1, :]
                            src = up_rows[:, bass.ds(i * (UNROLL * KT) + (u * KT + j), 1), :]
                        else:
                            dst = slot(n, 2, D)
                            src = down_rows[:, bass.ds(i * (UNROLL * KT) + (u * KT + 2 * (j - UP_SLOTS)), 2), :]
                        sp.dma_start(dst, src).then_inc(loaded[n % RING], 16)

            sp.wait_ge(freed, N_FRONT + E * PER_EXPERT)
            sp.wait_ge(over_ready, 1)
            any_over = sp.value_load(over[0:1, ROUNDS * E:ROUNDS * E + 1])
            with sp.If(any_over > 0):
                done = sp.alloc_register("over_done_sp")
                sp.reg_mov(done, 0)
                with sp.Fori(1, ROUNDS) as r:
                    with sp.Fori(0, E) as e:
                        need = sp.value_load(over[0:1, bass.ds(r * E + e, 1)])
                        with sp.If(need > 0):
                            k = sp.snap(done)
                            row = sp.snap(e * KT)
                            sp.reg_add(done, done, 1)
                            sp.wait_ge(scattered, k + 1)
                            for j in range(UP_SLOTS):
                                sp.dma_start(ring[:, j:j + 1, :], up_rows[:, bass.ds(row + j, 1), :]).then_inc(v_loaded, 16)
                            for j in range(DOWN_SLOTS):
                                sp.dma_start(slot(UP_SLOTS + j, 2, D), down_rows[:, bass.ds(row + 2 * j, 2), :]).then_inc(v_loaded, 16)
                        sp.nop()
                sp.nop()
            sp.nop()

        @block.gpsimd
        def _(pool):
            pool.memset(eps[:, :], -0.5).then_inc(zeroed, 1)
            pool.wait_ge(zeroed, 1)
            pool.wait_ge(ms, 1)
            pool.tensor_tensor(sums[:, 2:4], sums[:, 2:4], eps[:, 0:2], ALU.pow).then_inc(power, 1)
            pool.wait_ge(hT_ps, 4)
            pool.memset(qmT, 0.0).then_inc(cleared, 1)
            pool.wait_ge(ms, 2)
            pool.tensor_tensor(sums[:, 8:12], sums[:, 8:12], eps[:, 0:4], ALU.pow).then_inc(power, 1)
            steps = 0

            def turn(rows, a, b, heads):
                nonlocal steps
                half = ROPE // 2
                if heads:
                    c, s = (t.unsqueeze(2).to_broadcast([P, TT, HEADS, ROPE]) for t in (cos2, sin2))
                else:
                    c, s = cos2, sin2
                pool.tensor_tensor(a, rows, c, ALU.mult).then_inc(rope_step, 1)
                pool.tensor_tensor(b, rows, s, ALU.mult).then_inc(rope_step, 1)
                steps += 2
                pool.wait_ge(rope_step, steps)
                if heads:
                    pool.tensor_tensor(rows[:, :, :, 0:half], a[:, :, :, 0:half], b[:, :, :, half:ROPE], ALU.add)
                    return pool.tensor_tensor(rows[:, :, :, half:ROPE], a[:, :, :, half:ROPE], b[:, :, :, 0:half], ALU.add)
                pool.tensor_tensor(rows[:, :, 0:half], a[:, :, 0:half], b[:, :, half:ROPE], ALU.add)
                return pool.tensor_tensor(rows[:, :, half:ROPE], a[:, :, half:ROPE], b[:, :, 0:half], ALU.add)

            pool.wait_ge(kr_ready, 1)
            turn(kr, kr_c[:, :, :], kr_b[:, :, :], False).then_inc(rope_step, 1)
            steps += 1
            pool.wait_ge(rope_step, steps)
            pool.tensor_copy(kcat[:, :, :, NOPE:QK_B], kr.unsqueeze(2).to_broadcast([P, TT, HEADS, ROPE])).then_inc(roped, 1)
            pool.wait_ge(qb_ready, 2)
            turn(qb.rearrange("p t (h e) -> p t h e", h=HEADS)[:, :, :, NOPE:QK_B], rope_a, rope_b, True).then_inc(roped, 1)
            pool.wait_ge(s_done, 2 * HEADS)
            pool.memset(arena["a"][:, 0:2048 + D], 0.0).then_inc(cleared, 1)
            pool.wait_ge(pv_done, HEADS)
            pool.memset(y_e, 0.0).then_inc(y_ready, 1)
            pool.memset(routT, 0.0).then_inc(moe_zero, 1)
            pool.memset(routing[:, :, :], 0.0).then_inc(moe_zero, 1)
            pool.memset(logits[:, :, E:E + TOP], BIG).then_inc(moe_zero, 1)
            pool.memset(strike[:, :, TOP:8], BIG).then_inc(moe_zero, 1)
            pool.wait_ge(ab_done, KT)
            pool.memset(gatedT[:, 1], 0.0).then_inc(moe_zero, 1)
            pool.wait_ge(ms, 3)
            pool.tensor_tensor(sums[:, 2:4], sums[:, 2:4], eps[:, 0:2], ALU.pow).then_inc(power, 1)
            pool.wait_ge(ms, 4)
            pool.tensor_tensor(sums[:, 2:4], sums[:, 2:4], eps[:, 0:2], ALU.pow).then_inc(power, 1)

        @block.scalar
        def _(act):
            nc.scalar.dma_start(const[:, :], table[:, 0:fixed_width]).then_inc(s_const, 16)
            with nc.allow_non_contiguous_dma(reason="norm weights as columns, 1.4k words"):
                act.dma_start(g1[:, :], norm1_g[0].rearrange("(k p) -> p k", p=P)).then_inc(s_small, 16)
                act.dma_start(gq[:, :], q_a_norm_g[0].rearrange("(k p) -> p k", p=P)).then_inc(s_small, 16)
                act.dma_start(gkv[:, :], kv_a_norm_g[0].rearrange("(k p) -> p k", p=P)).then_inc(s_small, 16)
            act.dma_start(arena["t"][:, :], table[:, fixed_width:table_width]).then_inc(s_tab, 16)
            act.dma_start(router_w[:, :, :], w_router[0].rearrange("(k p) e -> p k e", p=P)).then_inc(s_mid, 16)
            act.dma_start(router_b[:, :], b_router[0:1, :].to_broadcast([P, E])).then_inc(s_mid, 16)

            act.wait_ge(s_x, 16)
            for t in range(TT):
                act.activation(arena["h"][:, t * D:(t + 1) * D], xrow[:, t, :], ACT.Square, accum_out=sums[:, t:t + 1]).then_inc(squares, 1)
            act.wait_ge(s_small, 48)
            act.wait_ge(squares, TT)
            for j in (2, 3):
                act.wait_ge(hT_ps, j + 1)
                for k in range(2):
                    last = act.activation(hT[:, 2 * j + k, :], ps[:, j, k * SEQ:(k + 1) * SEQ], ACT.Copy,
                                          scale=g1[:, 2 * j + k:2 * j + k + 1])
                last.then_inc(hT_a, 1)
            for t in range(TT):
                act.wait_ge(freed, through("latent"))
                act.activation(cn[:, t, 0:Q_RANK], ps[:, 4 + t, 0:Q_RANK], ACT.Square, accum_out=sums[:, 4 + t:5 + t])
                act.activation(cn[:, t, Q_RANK:], ps[:, 4 + t, Q_RANK:Q_RANK + KV_RANK], ACT.Square,
                               accum_out=sums[:, 6 + t:7 + t]).then_inc(lat_sq, 1)
            act.wait_ge(freed, through("qk"))
            act.wait_ge(hT_ps, 4)
            for j in range(2):
                last = act.activation(kT[:, 2 * j:2 * j + 2, :], ps[:, 2 + j, :].rearrange("p (a b) -> p a b", a=2), ACT.Copy)
            last.then_inc(k_ready, 1)

            def exps(k):
                act.wait_ge(max_ready, k + 1)
                for t in range(TT):
                    src, scale = (probs[:, k % 2, t, :], 1.0) if k < HEADS else (ps[:, k % 2, t * SEQ:(t + 1) * SEQ], SCALE_B)
                    last = act.activation(probs[:, k % 2, t, :], src, ACT.Exp, bias=soft[:, k % 2, t:t + 1], scale=scale,
                                          accum_out=soft[:, k % 2, 2 + t:3 + t])
                last.then_inc(exp_done, 1)

            def take_probsT(k):
                act.wait_ge(pT_ps, k + 1)
                act.activation(probsT[:, k % 2], ps[:, 2 + k % 2, :].rearrange("p (a b) -> p a b", a=TT), ACT.Copy).then_inc(pT_ready, 1)

            exps(0)
            exps(1)
            act.wait_ge(freed, through("v"))
            for t in range(TT):
                last = act.activation(va[:, t, :], ps[:, 6 + t, :], ACT.Copy)
            last.then_inc(va_ready, 1)
            take_probsT(0)
            exps(2)
            for t in range(TT):
                if t == 0:
                    act.wait_ge(uq_half, 1)
                else:
                    act.wait_ge(freed, through("uq"))
                act.activation(qb[:, t, 0:5 * QK_B], ps[:, 4 + 2 * t, 0:5 * QK_B], ACT.Copy)
                act.activation(qb[:, t, 5 * QK_B:], ps[:, 5 + 2 * t, 0:3 * QK_B], ACT.Copy).then_inc(qb_ready, 1)
            take_probsT(1)
            exps(3)
            act.wait_ge(freed, through("uv"))
            for t in range(TT):
                act.activation(kcat[:, t, :, 0:NOPE], ps[:, 4 + t, :].rearrange("p (h e) -> p h e", h=HEADS), ACT.Copy)
                last = act.activation(vb[:, t, :], ps[:, 6 + t, :], ACT.Copy)
            last.then_inc(kvb_ready, 1)
            for k in range(2, HEADS):
                take_probsT(k)
                if k + 2 < HEADS:
                    exps(k + 2)
            for p in range(HEADS // 2):
                act.wait_ge(bT_ps, 2 * p + 1)
                act.activation(qTb[0:QK_B, 2 * p:2 * p + 2, :], ps[0:QK_B, 4 + (2 * p) % 4, :].rearrange("p (a b) -> p a b", a=2),
                               ACT.Copy).then_inc(bq_ready, 1)
            act.wait_ge(bT_ps, HEADS)
            act.dma_start(xrow[:, :, :], x_rows).then_inc(s_xagain, 16)
            exps(HEADS)
            exps(HEADS + 1)
            for k in range(HEADS, 2 * HEADS):
                take_probsT(k)
                if k + 2 < 2 * HEADS:
                    exps(k + 2)
            act.wait_ge(cleared, 2)
            act.dma_start(up_bias[0:E, :], b_gate_up[0]).then_inc(s_bias, 16)
            act.dma_start(down_bias[0:E, :], b_down[0]).then_inc(s_bias, 16)
            act.dma_start(g2[:, :], norm2_g[0:1, :].to_broadcast([P, D])).then_inc(s_bias, 16)
            act.wait_ge(pv_done, HEADS)
            act.dma_start(gf[:, :], final_g.rearrange("(a d) -> a d", a=1).to_broadcast([P, D])).then_inc(s_bias, 16)
            for n in range(4):
                act.wait_ge(gz_ready, 8)
                act.activation(gateT[:, n:2 * KT:4, :], gateT[:, n:2 * KT:4, :], ACT.Sigmoid).then_inc(gates_on, 1)
            for t in range(TT):
                act.wait_ge(x2_ready, t + 1)
                act.activation(arena["g"][:, 2048 + t * D:2048 + (t + 1) * D], xrow[:, t, :], ACT.Square, accum_out=sums[:, t:t + 1]).then_inc(x2_sq, 1)
            for j in (2, 3):
                act.wait_ge(h2T_ps, j + 1)
                act.activation(h2T[:, 2 * j:2 * j + 2, :], ps[:, 4 + j, :].rearrange("p (a b) -> p a b", a=2), ACT.Copy).then_inc(h2T_a, 1)
            act.wait_ge(top_ready, 1)
            for t in range(TT):
                last = act.activation(expo[:, t, :], logits[:, t, 0:E], ACT.Exp, bias=sums[:, 12 + t:13 + t])
            last.then_inc(expo_ready, 1)

            def take_mix(dst):
                return act.activation(dst, ps[:, MIX, :], ACT.Copy)

            act.wait_ge(gathered, 1)
            take_mix(x_e).then_inc(xe_ready, 1)
            act.wait_ge(xT_done, 1)
            take_mix(xT_e[:, 0]).then_inc(xT_ready, 1)
            with act.Fori(0, E // UNROLL) as i:
                for u in range(UNROLL):
                    e = i * UNROLL + u
                    act.wait_ge(gathered, e + 2)
                    take_mix(x_e).then_inc(xe_ready, 1)
                    act.wait_ge(xT_done, e + 2)
                    take_mix(xT_e[:, (u + 1) % 2]).then_inc(xT_ready, 1)
                    act.wait_ge(gT_done, e + 1)
                    take_mix(gatedT[:, u % 2].rearrange("p a b -> p (a b)")).then_inc(gT_ready, 1)
                    act.wait_ge(clamped, e + 1)
                    act.activation(sig, gate_c, ACT.Sigmoid, scale=ALPHA).then_inc(sig_ready, 1)
                    act.wait_ge(freed, i * (UNROLL * PER_EXPERT) + (N_FRONT + (u + 1) * PER_EXPERT))
                    act.activation(y_e, ps[:, Y, :], ACT.Copy).then_inc(y_ready, 1)

            act.wait_ge(over_ready, 1)
            any_over = act.value_load(over[0:1, ROUNDS * E:ROUNDS * E + 1])
            with act.If(any_over > 0):
                done = act.alloc_register("over_done_act")
                act.reg_mov(done, 0)
                with act.Fori(1, ROUNDS) as r:
                    with act.Fori(0, E) as e:
                        need = act.value_load(over[0:1, bass.ds(r * E + e, 1)])
                        with act.If(need > 0):
                            k = act.snap(done)
                            act.wait_ge(v_gathered, k + 1)
                            take_mix(x_e).then_inc(v_xe, 1)
                            act.wait_ge(v_xTd, k + 1)
                            take_mix(xT_e[:, 0]).then_inc(v_xT, 1)
                            act.wait_ge(v_gTd, k + 1)
                            take_mix(gatedT[:, 0].rearrange("p a b -> p (a b)")).then_inc(v_gT, 1)
                            act.wait_ge(v_cl, k + 1)
                            act.activation(sig, gate_c, ACT.Sigmoid, scale=ALPHA).then_inc(v_sig, 1)
                            act.wait_ge(v_yd, k + 1)
                            act.activation(y_e, ps[:, Y, :], ACT.Copy).then_inc(v_y, 1)
                            act.reg_add(done, done, 1)
                        act.nop()
                act.nop()
            for t in range(TT):
                act.wait_ge(total, t + 1)
                act.activation(h2[:, t, :], xrow[:, t, :], ACT.Square, accum_out=sums[:, t:t + 1]).then_inc(fin_sq, 1)
            for t in range(TT):
                act.wait_ge(fin_ready, t + 1)
                act.dma_start(out_rows[:, t:t + 1, :], xrow[:, t:t + 1, :]).then_inc(s_out, 16)
            act.wait_ge(s_out, 16 * TT)

        @block.vector
        def _(dve):
            step = [0]

            def step_wait():
                dve.wait_ge(dve_step, step[0])

            def stepped(ins):
                ins.then_inc(dve_step, 1)
                step[0] += 1

            dve.wait_ge(squares, TT)
            dve.tensor_scalar(sums[:, 2:4], sums[:, 0:2], 1.0 / D, EPS, ALU.mult, ALU.add).then_inc(ms, 1)
            dve.wait_ge(power, 1)
            dve.wait_ge(s_x, 16)
            for t in range(TT):
                dve.tensor_scalar(xs[:, t, :], xrow[:, t, :], sums[:, 2 + t:3 + t], None, ALU.mult).then_inc(xs_ready, 1)
            dve.wait_ge(s_small, 48)
            for j in (0, 1):
                dve.wait_ge(hT_ps, j + 1)
                dve.tensor_tensor(hT[:, 2 * j:2 * j + 2, :], ps[:, j, :].rearrange("p (a b) -> p a b", a=2),
                                  g1[:, 2 * j:2 * j + 2].unsqueeze(2).to_broadcast([P, 2, SEQ]), ALU.mult).then_inc(hT_v, 1)
            dve.wait_ge(lat_sq, TT)
            stepped(dve.tensor_scalar(sums[:, 8:10], sums[:, 4:6], 1.0 / Q_RANK, EPS, ALU.mult, ALU.add))
            dve.tensor_scalar(sums[:, 10:12], sums[:, 6:8], 1.0 / KV_RANK, EPS, ALU.mult, ALU.add).then_inc(ms, 1)
            for t in range(TT):
                last = dve.tensor_copy(kr[:, t, :], ps[:, 4 + t, Q_RANK + KV_RANK:LATENT])
            last.then_inc(kr_ready, 1)
            dve.wait_ge(power, 2)
            for t in range(TT):
                dve.tensor_scalar(cn[:, t, 0:Q_RANK], ps[:, 4 + t, 0:Q_RANK], sums[:, 8 + t:9 + t], None, ALU.mult)
                last = dve.tensor_scalar(cn[:, t, Q_RANK:], ps[:, 4 + t, Q_RANK:Q_RANK + KV_RANK], sums[:, 10 + t:11 + t], None, ALU.mult)
            last.then_inc(cn_ready, 1)
            dve.wait_ge(freed, through("qk"))
            dve.wait_ge(cleared, 1)
            for j in range(2):
                for o in range(2):
                    last = dve.tensor_scalar(qmT[o * HD:(o + 1) * HD, 4 * j + o:4 * j + o + 3:2, :],
                                             ps[o * HD:(o + 1) * HD, j, :].rearrange("p (a b) -> p a b", a=2), SCALE_A, None, ALU.mult)
            last.then_inc(q_ready, 1)
            dve.wait_ge(cT_ps, 1)
            dve.tensor_tensor(cT[:, 0:2, :], ps[:, 6, :].rearrange("p (a b) -> p a b", a=2),
                              gq[:, :].unsqueeze(2).to_broadcast([P, 2, SEQ]), ALU.mult)
            dve.tensor_scalar(cT[:, 2, :], ps[:, 7, 0:SEQ], gkv[:, 0:1], None, ALU.mult).then_inc(cT_ready, 1)

            def maxes(k):
                dve.wait_ge(s_done, k + 1)
                b = k % 2
                if k < HEADS:
                    slope = 2.0 ** (-8.0 * (k + 1) / HEADS)
                    for t in range(TT):
                        at = P * (TT - 1 - t)
                        stepped(dve.scalar_tensor_tensor(out=probs[:, b, t, :], in0=dist[:, at:at + SEQ], scalar=-slope,
                                                         in1=ps[:, b, t * SEQ:(t + 1) * SEQ], op0=ALU.mult, op1=ALU.add))
                    for t in range(TT):
                        at = P * (TT - 1 - t)
                        dve.wait_ge(dve_step, step[0] - (TT - 1))
                        stepped(dve.tensor_tensor_reduce(probs[:, b, t, :], probs[:, b, t, :], log_count[:, at:at + SEQ], 1.0, -BIG,
                                                         ALU.add, ALU.max, soft[:, b, 6 + t:7 + t]))
                else:
                    stepped(dve.tensor_reduce(soft[:, b, 6:8], ps[:, b, :].rearrange("p (a b) -> p a b", a=TT), AX_X, ALU.max))
                step_wait()
                dve.tensor_scalar(soft[:, b, 0:2], soft[:, b, 6:8], -1.0 if k < HEADS else -SCALE_B, None, ALU.mult).then_inc(max_ready, 1)

            def norms(k):
                b = k % 2
                dve.wait_ge(exp_done, k + 1)
                stepped(dve.reciprocal(soft[:, b, 4:6], soft[:, b, 2:4]))
                step_wait()
                for t in range(TT):
                    last = dve.tensor_scalar(probs[:, b, t, :], probs[:, b, t, :], soft[:, b, 4 + t:5 + t], None, ALU.mult)
                last.then_inc(probs_ready, 1)

            def take_o(p):
                dve.wait_ge(pv_done, p + 1)
                dve.tensor_copy(oT[:, p, :], ps[:, 4 + p % 2, 0:SEQ]).then_inc(o_ready, 1)

            def take_gates(g):
                dve.wait_ge(freed, FIRST["gates"] + g + 1)
                dve.tensor_copy(gateT[:, 2 * g:2 * g + 2, :], ps[:, 6 + g % 2, :].rearrange("p (a b) -> p a b", a=2)).then_inc(gz_ready, 1)

            dve.wait_ge(s_tab, 16)
            maxes(0)
            maxes(1)
            for k in range(HEADS):
                norms(k)
                if k + 2 < HEADS:
                    maxes(k + 2)
                if k >= 2 and k % 2 == 0:
                    take_o(k // 2 - 1)
            take_o(3)
            for p in range(HEADS // 2):
                dve.wait_ge(bT_ps, 2 * p + 2)
                dve.tensor_copy(kTb[0:QK_B, 2 * p:2 * p + 2, :], ps[0:QK_B, 4 + (2 * p + 1) % 4, :].rearrange("p (a b) -> p a b", a=2)).then_inc(bk_ready, 1)
            maxes(HEADS)
            maxes(HEADS + 1)
            take_gates(0)
            for k in range(HEADS, 2 * HEADS):
                norms(k)
                if k + 2 < 2 * HEADS:
                    maxes(k + 2)
                if k > HEADS and k % 2 == 0:
                    take_o(k // 2 - 1)
                if k - HEADS < 7:
                    take_gates(k - HEADS + 1)
            take_o(7)
            for d in range(KT):
                dve.wait_ge(ab_done, d + 1)
                dve.wait_ge(gates_on, d % 4 + 1)
                stepped(dve.tensor_tensor(gateT[:, d:d + KT + 1:KT, :], gateT[:, d:d + KT + 1:KT, :],
                                          ps[:, d % 4, :].rearrange("p (a b) -> p a b", a=2), ALU.mult))
                step_wait()
                dve.tensor_tensor(gateT[:, d, :], gateT[:, d, :], gateT[:, KT + d, :], ALU.add).then_inc(merged, 1)
            dve.wait_ge(s_xagain, 16)
            dve.wait_ge(freed, through("wo"))
            for t in range(TT):
                dve.tensor_tensor(xrow[:, t, :], xrow[:, t, :], ps[:, 4 + 2 * t:6 + 2 * t, :].rearrange("p a b -> p (a b)"), ALU.add).then_inc(x2_ready, 1)
            dve.wait_ge(x2_sq, TT)
            dve.tensor_scalar(sums[:, 2:4], sums[:, 0:2], 1.0 / D, EPS, ALU.mult, ALU.add).then_inc(ms, 1)
            dve.wait_ge(s_bias, 64)
            dve.wait_ge(power, 3)
            for t in range(TT):
                dve.scalar_tensor_tensor(out=h2[:, t, :], in0=xrow[:, t, :], scalar=sums[:, 2 + t:3 + t], in1=g2,
                                         op0=ALU.mult, op1=ALU.mult).then_inc(h2_ready, 1)
            for j in (0, 1):
                dve.wait_ge(h2T_ps, j + 1)
                dve.tensor_copy(h2T[:, 2 * j:2 * j + 2, :], ps[:, 4 + j, :].rearrange("p (a b) -> p a b", a=2)).then_inc(h2T_v, 1)
            dve.wait_ge(part_done, 1)
            dve.tensor_copy(part_rows, ps[:, 0, 0:SEQ]).then_inc(part_ready, 1)
            dve.wait_ge(s_mid, 32)
            dve.wait_ge(logit_done, 1)
            dve.wait_ge(moe_zero, 5)
            stepped(dve.tensor_tensor(logits[:, :, 0:E], ps[:, 1, 0:TT * E].rearrange("p (t e) -> p t e", t=TT),
                                      router_b[:, :].unsqueeze(1).to_broadcast([P, TT, E]), ALU.add))
            step_wait()
            for t in range(TT):
                last = dve.max(best[:, t, :], logits[:, t, 0:E])
            stepped(last)
            step_wait()
            dve.tensor_scalar(sums[:, 12:14], best[:, :, 0:1].rearrange("p t a -> p (t a)"), -1.0, None, ALU.mult).then_inc(top_ready, 1)
            stepped(dve.tensor_copy(strike[:, :, 0:TOP], best[:, :, 0:TOP]))
            step_wait()
            for t in range(TT):
                last = dve.match_replace(struck[:, t, :], strike[:, t, :], logits[:, t, :], -BIG)
            stepped(last)
            step_wait()
            dve.tensor_scalar(chosen[:, :, :], struck[:, :, 0:E], -BIG, None, ALU.is_equal).then_inc(chosen_ready, 1)
            dve.wait_ge(expo_ready, 1)
            dve.wait_ge(chosen_ready, 1)
            stepped(dve.tensor_tensor(expo[:, :, :], expo[:, :, :], chosen[:, :, :], ALU.mult))
            step_wait()
            stepped(dve.tensor_reduce(sums[:, 4:6], expo[:, :, :], AX_X, ALU.add))
            step_wait()
            stepped(dve.reciprocal(sums[:, 6:8], sums[:, 4:6]))
            step_wait()
            for t in range(TT):
                last = dve.tensor_scalar(routing[:, t, 0:E], expo[:, t, :], sums[:, 6 + t:7 + t], None, ALU.mult)
            last.then_inc(rout_ready, 1)
            dve.wait_ge(count_done, 1)
            stepped(dve.scalar_tensor_tensor(out=struck[:, :, 0:E], in0=ps[:, 2, 0:TT * E].rearrange("p (t e) -> p t e", t=TT),
                                             scalar=1.0, in1=chosen[:, :, :], op0=ALU.add, op1=ALU.mult))
            for r in range(ROUNDS):
                stepped(dve.tensor_scalar(over[0:1, r * E:(r + 1) * E], ps[0:1, 2, TT * E:(TT + 1) * E], float(CAP * r), None, ALU.is_gt))
            stepped(dve.tensor_reduce(sums[0:1, 14:15], ps[0:1, 2, TT * E:(TT + 1) * E], AX_X, ALU.max))
            step_wait()
            for r in range(ROUNDS):
                stepped(dve.tensor_scalar(places[:, :, r * E:(r + 1) * E], struck[:, :, 0:E], -float(1 + CAP * r), None, ALU.add))
            dve.tensor_scalar(over[0:1, ROUNDS * E:ROUNDS * E + 1], sums[0:1, 14:15], float(CAP), None, ALU.is_gt).then_inc(over_ready, 1)
            step_wait()
            dve.wait_ge(rout_ready, 1)

            def build_picks(b, e, je):
                for t in range(TT):
                    dve.tensor_scalar(pick[:, b, t, :], slots[:, 0:CAP], places[:, t, bass.ds(je, 1)], None, ALU.is_equal)
                for t in range(TT):
                    dve.tensor_scalar(gated[:, b, t, :], slots, places[:, t, bass.ds(je, 1)], routing[:, t, bass.ds(e, 1)],
                                      ALU.is_equal, ALU.mult)
                return dve.tensor_copy(expert_row[:, b, :], ident[:, bass.ds(e, 1)].to_broadcast([P, CAP]))

            def clamp_gate():
                return dve.tensor_scalar(gate_c, ps[:, GATE, :], LIMIT, None, ALU.min)

            def clamp_up():
                return dve.tensor_scalar(up_c, ps[:, UP, :], LIMIT, -LIMIT, ALU.min, ALU.max)

            build_picks(0, 0, 0).then_inc(pick_ready, 1)
            build_picks(1, 1, 1).then_inc(pick_ready, 1)
            dve.wait_ge(routT_ps, 1)
            dve.tensor_copy(routT[0:E, :], ps[0:E, 3, 0:SEQ]).then_inc(routT_ready, 1)
            with dve.Fori(0, E // UNROLL) as i:
                for u in range(UNROLL):
                    e = i * UNROLL + u
                    dve.wait_ge(up_done, e + 1)
                    clamp_gate().then_inc(clamped, 1)
                    clamp_up().then_inc(clamped2, 1)
                    dve.wait_ge(clamped, e + 1)
                    dve.wait_ge(clamped2, e + 1)
                    dve.scalar_tensor_tensor(out=up_c, in0=up_c, scalar=1.0, in1=gate_c, op0=ALU.add, op1=ALU.mult).then_inc(raised, 1)
                    dve.wait_ge(raised, e + 1)
                    dve.wait_ge(sig_ready, e + 1)
                    dve.tensor_tensor(act_v, up_c, sig, ALU.mult).then_inc(act_ready, 1)
                    dve.wait_ge(actT_done, e + 1)
                    dve.tensor_copy(actT, ps[:, MIX, :]).then_inc(actT_ready, 1)
                    build_picks(u % 2, e + 2, e + 2).then_inc(pick_ready, 1)

            dve.wait_ge(scattered, 1)
            dve.wait_ge(over_ready, 1)
            any_over = dve.value_load(over[0:1, ROUNDS * E:ROUNDS * E + 1])
            with dve.If(any_over > 0):
                done = dve.alloc_register("over_done_dve")
                dve.reg_mov(done, 0)
                with dve.Fori(1, ROUNDS) as r:
                    with dve.Fori(0, E) as e:
                        need = dve.value_load(over[0:1, bass.ds(r * E + e, 1)])
                        with dve.If(need > 0):
                            k = dve.snap(done)
                            build_picks(0, e, r * E + e).then_inc(v_pick, 1)
                            dve.wait_ge(v_up, k + 1)
                            clamp_gate().then_inc(v_cl, 1)
                            clamp_up().then_inc(v_cl2, 1)
                            dve.wait_ge(v_cl, k + 1)
                            dve.wait_ge(v_cl2, k + 1)
                            dve.scalar_tensor_tensor(out=up_c, in0=up_c, scalar=1.0, in1=gate_c, op0=ALU.add, op1=ALU.mult).then_inc(v_raised, 1)
                            dve.wait_ge(v_raised, k + 1)
                            dve.wait_ge(v_sig, k + 1)
                            dve.tensor_tensor(act_v, up_c, sig, ALU.mult).then_inc(v_act, 1)
                            dve.wait_ge(v_aTd, k + 1)
                            dve.tensor_copy(actT, ps[:, MIX, :]).then_inc(v_aT, 1)
                            dve.wait_ge(scattered, k + 2)
                            dve.reg_add(done, done, 1)
                        dve.nop()
                dve.nop()
            for t in range(TT):
                dve.tensor_tensor(xrow[:, t, :], xrow[:, t, :], ps[:, 2 * t:2 * t + 2, :].rearrange("p a b -> p (a b)"), ALU.add).then_inc(total, 1)
            dve.wait_ge(fin_sq, TT)
            dve.tensor_scalar(sums[:, 2:4], sums[:, 0:2], 1.0 / D, EPS, ALU.mult, ALU.add).then_inc(ms, 1)
            dve.wait_ge(power, 4)
            for t in range(TT):
                dve.scalar_tensor_tensor(out=xrow[:, t, :], in0=xrow[:, t, :], scalar=sums[:, 2 + t:3 + t], in1=gf,
                                         op0=ALU.mult, op1=ALU.mult).then_inc(fin_ready, 1)

        @block.tensor
        def _(pe):
            def arrived(n):
                pe.wait_ge(loaded[n % RING], 16 * (n // RING + 1))

            pe.wait_ge(s_const, 16)
            pe.wait_ge(xs_ready, TT)
            for j in range(4):
                for k in range(2):
                    for t in range(TT):
                        a = (2 * j + k) * P
                        last = pe.transpose(ps[:, j, k * SEQ + t * P:k * SEQ + (t + 1) * P], xs[:, t, a:a + P], ident)
                last.then_inc(hT_ps, 1)
            pe.wait_ge(hT_v, 2)
            pe.wait_ge(hT_a, 2)
            for k in range(KT):
                if k % 4 == 0:
                    arrived(FIRST["latent"] + k // 4)
                w = slot(FIRST["latent"] + k // 4, 4, LATENT)
                for t in range(TT):
                    last = pe.matmul(ps[:, 4 + t, 0:LATENT], hT[:, k, t * P:(t + 1) * P], w[:, k % 4, :], start=k == 0, stop=k == KT - 1)
                if k == 3:
                    last.then_inc(freed, 1)
            last.then_inc(freed, 1)
            for k in range(KT):
                if k % 2 == 0:
                    arrived(FIRST["qk"] + k // 2)
                w = slot(FIRST["qk"] + k // 2, 2, 2 * AW)
                for c in range(8):
                    last = pe.matmul(ps[:, c // 2, c % 2 * SEQ:(c % 2 + 1) * SEQ], w[:, k % 2, c * P:(c + 1) * P], hT[:, k, :],
                                     start=k == 0 and c % 2 == 0, stop=k == KT - 1, skip_group_check=True)
                if k % 2:
                    last.then_inc(freed, 1)
            pe.wait_ge(cn_ready, 1)
            for c in range(3):
                for t in range(TT):
                    b, a = (6, c * SEQ) if c < 2 else (7, 0)
                    last = pe.transpose(ps[:, b, a + t * P:a + (t + 1) * P], cn[:, t, c * P:(c + 1) * P], ident)
            last.then_inc(cT_ps, 1)

            def scores(k):
                for t in range(TT):
                    if k < HEADS:
                        q, key = qmT[:, k, t * P:(t + 1) * P], kT[:, k // 2, :]
                    else:
                        q, key = qTb[0:QK_B, k - HEADS, t * P:(t + 1) * P], kTb[0:QK_B, k - HEADS, :]
                    last = pe.matmul(ps[:, k % 2, t * SEQ:(t + 1) * SEQ], q, key, start=True, stop=True)
                last.then_inc(s_done, 1)

            def turn_probs(k):
                pe.wait_ge(probs_ready, k + 1)
                if k >= 2:
                    pe.wait_ge(pT_ready, k - 1)
                for c in range(TT):
                    for t in range(TT):
                        last = pe.transpose(ps[:, 2 + k % 2, c * SEQ + t * P:c * SEQ + (t + 1) * P], probs[:, k % 2, t, c * P:(c + 1) * P], ident)
                last.then_inc(pT_ps, 1)

            def attend(p):
                pe.wait_ge(pT_ready, 2 * p + 2)
                if p >= 2:
                    pe.wait_ge(o_ready, p - 1)
                v = va if p < HEADS // 2 else vb
                for c in range(TT):
                    for o in range(2):
                        h = (2 * p + o) % HEADS
                        last = pe.matmul(ps[o * HD:(o + 1) * HD, 4 + p % 2, 0:SEQ], v[:, c, h * HD:(h + 1) * HD], probsT[:, o, c, :],
                                         start=c == 0, stop=c == TT - 1)
                last.then_inc(pv_done, 1)

            pe.wait_ge(q_ready, 1)
            pe.wait_ge(k_ready, 1)
            scores(0)
            scores(1)
            pe.wait_ge(cT_ready, 1)
            for k in range(KT):
                if k % 4 == 0:
                    arrived(FIRST["v"] + k // 4)
                w = slot(FIRST["v"] + k // 4, 4, AW)
                for t in range(TT):
                    last = pe.matmul(ps[:, 6 + t, :], hT[:, k, t * P:(t + 1) * P], w[:, k % 4, :], start=k == 0, stop=k == KT - 1)
                if k % 4 == 3:
                    last.then_inc(freed, 1)
            turn_probs(0)
            scores(2)
            pe.wait_ge(va_ready, 1)
            arrived(FIRST["uq"])
            w = slot(FIRST["uq"], 2, HEADS * QK_B)
            for t in range(TT):
                for b, (a, z) in enumerate(((0, 5 * QK_B), (5 * QK_B, HEADS * QK_B))):
                    for c in range(2):
                        last = pe.matmul(ps[:, 4 + 2 * t + b, 0:z - a], cT[:, c, t * P:(t + 1) * P], w[:, c, a:z], start=c == 0, stop=c == 1)
                last.then_inc((uq_half, freed)[t], 1)
            turn_probs(1)
            scores(3)
            pe.wait_ge(qb_ready, TT)
            for m, name in enumerate(("uk", "uv")):
                arrived(FIRST[name])
                for t in range(TT):
                    last = pe.matmul(ps[:, 4 + 2 * m + t, :], cT[:, 2, t * P:(t + 1) * P], slot(FIRST[name], AW), start=True, stop=True)
                last.then_inc(freed, 1)
            pe.wait_ge(kvb_ready, 1)
            attend(0)
            for p in range(1, HEADS // 2):
                for k in (2 * p, 2 * p + 1):
                    turn_probs(k)
                    if k + 2 < HEADS:
                        scores(k + 2)
                attend(p)

            pe.wait_ge(roped, 2)
            pe.wait_ge(o_ready, HEADS // 2)
            qb4 = qb.rearrange("p t (h e) -> p t h e", h=HEADS)
            for p in range(HEADS // 2):
                for m, rows in enumerate((qb4, kcat)):
                    if p >= 2:
                        pe.wait_ge((bq_ready, bk_ready)[m], p - 1)
                    for o in range(2):
                        for t in range(TT):
                            last = pe.transpose(ps[0:QK_B, 4 + (2 * p + m) % 4, o * SEQ + t * P:o * SEQ + (t + 1) * P],
                                                rows[:, t, 2 * p + o, :], ident)
                    last.then_inc(bT_ps, 1)

            def gates(g):
                n = FIRST["gates"] + g
                arrived(n)
                if g >= 2:
                    pe.wait_ge(gz_ready, g - 1)
                w = slot(n, KT, 2 * P)
                for c in range(2):
                    for k in range(KT):
                        last = pe.matmul(ps[:, 6 + g % 2, c * SEQ:(c + 1) * SEQ], w[:, k, c * P:(c + 1) * P], hT[:, k, :], start=k == 0, stop=k == KT - 1)
                last.then_inc(freed, 1)

            pe.wait_ge(bq_ready, HEADS // 2)
            pe.wait_ge(bk_ready, HEADS // 2)
            scores(HEADS)
            scores(HEADS + 1)
            gates(0)
            for p in range(HEADS // 2, HEADS):
                for k in (2 * p, 2 * p + 1):
                    turn_probs(k)
                    if k + 2 < 2 * HEADS:
                        scores(k + 2)
                    if k - HEADS < 7:
                        gates(k - HEADS + 1)
                attend(p)

            for d in range(KT):
                if d % 4 == 0:
                    arrived(FIRST["out"] + d // 2)
                    arrived(FIRST["out"] + d // 2 + 1)
                if d == 0:
                    pe.wait_ge(o_ready, HEADS)
                if d >= 4:
                    pe.wait_ge(merged, d - 3)
                for m in range(2):
                    w = slot(FIRST["out"] + d // 4 * 2 + m, 4, BANK)
                    for c in range(4):
                        last = pe.matmul(ps[:, d % 4, m * SEQ:(m + 1) * SEQ], w[:, c, d % 4 * P:(d % 4 + 1) * P], oT[:, 4 * m + c, :],
                                         start=c == 0, stop=c == 3)
                    if m == 0 and d % 4 == 3:
                        last.then_inc(freed, 1)
                    if m == 0 and d == 4:
                        last.then_inc(freed, 1)
                last.then_inc(ab_done, 1)
            for k in range(KT):
                if k % 2 == 0:
                    arrived(FIRST["wo"] + k // 2)
                pe.wait_ge(merged, k + 1)
                w = slot(FIRST["wo"] + k // 2, 2, D)
                for t in range(TT):
                    for n in range(2):
                        last = pe.matmul(ps[:, 4 + 2 * t + n, :], gateT[:, k, t * P:(t + 1) * P], w[:, k % 2, n * BANK:(n + 1) * BANK],
                                         start=k == 0, stop=k == KT - 1)
                if k % 2 or k == 0:
                    last.then_inc(freed, 1)
            pe.wait_ge(h2_ready, TT)
            for j in range(4):
                for k in range(2):
                    for t in range(TT):
                        a = (2 * j + k) * P
                        last = pe.transpose(ps[:, 4 + j, k * SEQ + t * P:k * SEQ + (t + 1) * P], h2[:, t, a:a + P], ident)
                last.then_inc(h2T_ps, 1)
            pe.wait_ge(s_mid, 32)
            pe.wait_ge(h2T_v, 2)
            pe.wait_ge(h2T_a, 2)
            for k in range(KT):
                q = k % 4
                last = pe.matmul(ps[q * E:(q + 1) * E, 0, 0:SEQ], router_w[:, k, :], h2T[:, k, :], start=k < 4, stop=k >= 4)
            last.then_inc(part_done, 1)
            pe.wait_ge(part_ready, 1)
            for t in range(TT):
                last = pe.matmul(ps[:, 1, t * E:(t + 1) * E], part_rows[:, t * P:(t + 1) * P], fold, start=True, stop=True)
            last.then_inc(logit_done, 1)
            pe.wait_ge(chosen_ready, 1)
            pe.matmul(ps[:, 2, 0:E], before, chosen[:, 0, :], start=True, stop=True)
            pe.matmul(ps[:, 2, E:2 * E], ones, chosen[:, 0, :], start=True, stop=False)
            pe.matmul(ps[:, 2, E:2 * E], before, chosen[:, 1, :], start=False, stop=True)
            pe.matmul(ps[:, 2, 2 * E:3 * E], ones, chosen[:, 0, :], start=True, stop=False)
            pe.matmul(ps[:, 2, 2 * E:3 * E], ones, chosen[:, 1, :], start=False, stop=True).then_inc(count_done, 1)
            pe.wait_ge(rout_ready, 1)
            for t in range(TT):
                last = pe.transpose(ps[0:E, 3, t * P:(t + 1) * P], routing[:, t, 0:E], ident)
            last.then_inc(routT_ps, 1)

            def gather(b):
                for t in range(TT):
                    for n in range(2):
                        last = pe.matmul(ps[n * CAP:(n + 1) * CAP, MIX, :], pick[:, b, t, :], h2[:, t, n * BANK:(n + 1) * BANK],
                                         start=t == 0, stop=t == TT - 1)
                return last

            def turn(rows):
                for c in range(4):
                    last = pe.transpose(ps[:, MIX, c * P:(c + 1) * P], rows[:, c * P:(c + 1) * P], ident)
                return last

            def turn_gated(b):
                for n in range(2):
                    for t in range(TT):
                        last = pe.transpose(ps[:, MIX, (2 * n + t) * P:(2 * n + t + 1) * P], gated[:, b, t, n * P:(n + 1) * P], ident)
                return last

            def lhs(rows, k):
                a = k % 4 * P + k // 4 * CAP
                return rows[:, a:a + CAP]

            def up_tile(b, k, w):
                for bank in (GATE, UP):
                    for n in range(2):
                        a = (bank - GATE) * F + n * BANK
                        last = pe.matmul(ps[n * CAP:(n + 1) * CAP, bank, :], lhs(xT_e[:, b], k), w[:, a:a + BANK],
                                         start=k == 0, stop=False, skip_group_check=True)
                return last

            def up_biases(b):
                for bank in (GATE, UP):
                    for n in range(2):
                        a = (bank - GATE) * F + n * BANK
                        last = pe.matmul(ps[n * CAP:(n + 1) * CAP, bank, :], expert_row[:, b, :], up_bias[:, a:a + BANK],
                                         start=False, stop=True, skip_group_check=True)
                return last

            def down_tile(k, w):
                for n in range(2):
                    last = pe.matmul(ps[n * CAP:(n + 1) * CAP, Y, :], lhs(actT, k), w[:, n * BANK:(n + 1) * BANK],
                                     start=k == 0, stop=k == KT - 1, skip_group_check=True)
                return last

            def scatter(b):
                for t in range(TT):
                    for n in range(2):
                        last = pe.matmul(ps[:, 2 * t + n, :], gatedT[:, b, 2 * n + t, :], y_e, start=False, stop=False, skip_group_check=True)
                return last

            pe.wait_ge(pick_ready, 1)
            gather(0).then_inc(gathered, 1)
            pe.wait_ge(xe_ready, 1)
            turn(x_e).then_inc(xT_done, 1)
            pe.wait_ge(routT_ready, 1)
            pe.wait_ge(s_bias, 64)
            for t in range(TT):
                for n in range(2):
                    pe.matmul(ps[:, 2 * t + n, :], routT[:, t * P:(t + 1) * P], down_bias[:, n * BANK:(n + 1) * BANK],
                              start=True, stop=False, skip_group_check=True)
            pe.wait_ge(moe_zero, 5)
            pe.wait_ge(xT_ready, 1)
            with pe.Fori(0, E // UNROLL) as i:
                for u in range(UNROLL):
                    e = i * UNROLL + u
                    b = u % 2

                    def use(j):
                        n = N_FRONT + u * PER_EXPERT + j
                        pe.wait_ge(loaded[n % RING], i * (16 * TURNS) + 16 * (n // RING + 1))
                        return n

                    for k in range(KT):
                        n = use(k)
                        up_tile(b, k, ring[:, n % RING, :]).then_inc(freed, 1)
                        if k == 0:
                            pe.wait_ge(pick_ready, e + 2)
                            gather(1 - b).then_inc(gathered, 1)
                        if k == 2:
                            pe.wait_ge(xe_ready, e + 2)
                            turn(x_e).then_inc(xT_done, 1)
                        if k == 5:
                            pe.wait_ge(xT_ready, e + 2)
                            turn_gated(b).then_inc(gT_done, 1)
                    up_biases(b).then_inc(up_done, 1)
                    pe.wait_ge(y_ready, e + 1)
                    scatter(1 - b)
                    pe.wait_ge(gT_ready, e + 1)
                    pe.wait_ge(act_ready, e + 1)
                    turn(act_v).then_inc(actT_done, 1)
                    pe.wait_ge(actT_ready, e + 1)
                    for j in range(DOWN_SLOTS):
                        n = use(UP_SLOTS + j)
                        w = slot(n, 2, D)
                        down_tile(2 * j, w[:, 0, :])
                        last = down_tile(2 * j + 1, w[:, 1, :])
                        last.then_inc(freed, 1)
            pe.wait_ge(y_ready, E + 1)
            scatter((E - 1) % 2).then_inc(scattered, 1)

            pe.wait_ge(over_ready, 1)
            any_over = pe.value_load(over[0:1, ROUNDS * E:ROUNDS * E + 1])
            with pe.If(any_over > 0):
                done = pe.alloc_register("over_done_pe")
                pe.reg_mov(done, 0)
                with pe.Fori(1, ROUNDS) as r:
                    with pe.Fori(0, E) as e:
                        need = pe.value_load(over[0:1, bass.ds(r * E + e, 1)])
                        with pe.If(need > 0):
                            k = pe.snap(done)
                            pe.wait_ge(v_pick, k + 1)
                            gather(0).then_inc(v_gathered, 1)
                            pe.wait_ge(v_xe, k + 1)
                            turn(x_e).then_inc(v_xTd, 1)
                            pe.wait_ge(v_xT, k + 1)
                            turn_gated(0).then_inc(v_gTd, 1)
                            pe.wait_ge(v_loaded, k * (16 * PER_EXPERT) + 16 * PER_EXPERT)
                            for j in range(KT):
                                up_tile(0, j, ring[:, j, :])
                            up_biases(0).then_inc(v_up, 1)
                            pe.wait_ge(v_gT, k + 1)
                            pe.wait_ge(v_act, k + 1)
                            turn(act_v).then_inc(v_aTd, 1)
                            pe.wait_ge(v_aT, k + 1)
                            for j in range(KT):
                                last = down_tile(j, slot(UP_SLOTS + j // 2, 2, D)[:, j % 2, :])
                            last.then_inc(v_yd, 1)
                            pe.wait_ge(v_y, k + 1)
                            scatter(0).then_inc(scattered, 1)
                            pe.reg_add(done, done, 1)
                        pe.nop()
                pe.nop()
            pe.nop()


INPUTS = ["x", "norm1_g", "w_in", "q_a_norm_g", "kv_a_norm_g", "w_uq", "w_uk", "w_uv", "w_a_out", "w_b_out", "w_o",
          "norm2_g", "w_router", "b_router", "w_gate_up", "b_gate_up", "w_down", "b_down", "final_g"]


def kernel(**inputs):
    import concourse.bacc as bacc
    from concourse.bass_utils import run_bass_kernel_spmd

    nc = bacc.Bacc("TRN2", target_bir_lowering=False, num_devices=1)
    arrays, args = {}, []
    for name in INPUTS:
        a = np.ascontiguousarray(inputs[name])
        arrays[f"in_{name}"] = a
        args.append(nc.dram_tensor(f"in_{name}", a.shape, mybir.dt.from_np(a.dtype), kind="ExternalInput").ap())
    table = constants()[0]
    arrays["in_table"] = table
    args.append(nc.dram_tensor("in_table", table.shape, F32, kind="ExternalInput").ap())
    out = nc.dram_tensor("out", (1, SEQ, D), F32, kind="ExternalOutput").ap()
    build(nc, *args, out)
    return run_bass_kernel_spmd(nc, [arrays], core_ids=[0]).results[0]["out"]
```

```python
import math
from contextlib import ExitStack

import numpy as np

import concourse.bass as bass
from concourse import mybir

F32 = mybir.dt.float32
I32 = mybir.dt.int32
ALU = mybir.AluOpType
ACT = mybir.ActivationFunctionType
AX_X = mybir.AxisListType.X

P = 128
D = 1024
SEQ = 256
TT = SEQ // P
KT = D // P
EPS = 1e-5

HEADS = 8
HD = 64
AW = HEADS * HD
NOPE, ROPE = 64, 32
QK_B = NOPE + ROPE
Q_RANK, KV_RANK = 256, 128
LATENT = Q_RANK + KV_RANK + ROPE
OFF_LATENT = 3 * AW
OFF_GATES = OFF_LATENT + LATENT
SCALE_A = HD ** -0.5
SCALE_B = QK_B ** -0.5
PATTERNS = ((128, 1), (512, 4), (2048, 16))
NEG = -1e30
BIG = 3e38

E = 32
TOP = 4
F = D
LIMIT, ALPHA = 7.0, 1.702
CAP = 64
ROUNDS = SEQ // CAP
BANK = 512

SLOT = 2048
RING = 16
FRONT = [("latent", 2), ("qk", 4), ("v", 2), ("uq", 1), ("uk", 1), ("uv", 1), ("gates", 8), ("out", 4), ("wo", 4)]
FIRST = {}
for _name, _n in FRONT:
    FIRST[_name] = sum(n for _, n in FRONT[:len(FIRST)])
N_FRONT = sum(n for _, n in FRONT)
UP_SLOTS = KT
DOWN_SLOTS = KT // 2
PER_EXPERT = UP_SLOTS + DOWN_SLOTS
UNROLL = RING // math.gcd(RING, PER_EXPERT)
TURNS = UNROLL * PER_EXPERT // RING


def constants():
    p = np.arange(P)
    ident = np.eye(P)
    inv = 10000.0 ** (-np.arange(0, ROPE, 2, dtype=np.float32) / ROPE)
    ang = np.arange(SEQ, dtype=np.float32)[:, None] * inv[None, :].astype(np.float32)
    cos, sin = np.cos(ang), np.sin(ang)
    rope_cos = np.concatenate([cos, cos], 1).reshape(TT, P, ROPE).transpose(1, 0, 2).reshape(P, -1)
    rope_sin = np.concatenate([sin, -sin], 1).reshape(TT, P, ROPE).transpose(1, 0, 2).reshape(P, -1)
    slot = np.arange(CAP)
    none = np.full(CAP, -5 * SEQ)
    slots = np.tile(np.concatenate([slot, none, none, slot]), (P, 1))
    before = (p[:, None] < p[None, :]).astype(np.float32)
    ones = np.ones((P, P))
    fold = np.tile(np.eye(E), (P // E, 1))
    delta = p[:, None] - (np.arange(SEQ + P)[None, :] - P)
    dist = np.abs(delta)
    count = sum(((delta % d == 0) & (dist <= w // 2)).astype(int) for w, d in PATTERNS)
    log_count = np.where(count > 0, np.log(np.maximum(count, 1)), NEG)
    parts = {"ident": ident, "cos": rope_cos, "sin": rope_sin, "slots": slots, "before": before,
             "ones": ones, "fold": fold, "dist": dist, "log_count": log_count}
    at, place = 0, {}
    for name, a in parts.items():
        place[name] = (at, a.shape[1])
        at += a.shape[1]
    return np.concatenate([a.astype(np.float32) for a in parts.values()], 1), place


def build(nc, x, norm1_g, w_in, q_a_norm_g, kv_a_norm_g, w_uq, w_uk, w_uv, w_a_out, w_b_out, w_o,
          norm2_g, w_router, b_router, w_gate_up, b_gate_up, w_down, b_down, final_g, table, out):
    place = constants()[1]
    table_width = sum(n for _, n in place.values())
    fixed_width = place["dist"][0]

    with ExitStack() as ctx:
        def sb(name, shape, dt=F32):
            return ctx.enter_context(nc.sbuf_tensor(name, shape, dt))

        def sem(name):
            return ctx.enter_context(nc.semaphore(name))

        ring = sb("ring", [P, RING, SLOT])
        xrow = sb("xrow", [P, TT, D])
        const = sb("const", [P, fixed_width])
        g1 = sb("g1", [P, KT])
        gq = sb("gq", [P, Q_RANK // P])
        gkv = sb("gkv", [P, 1])
        g2_col = sb("g2_col", [P, KT])
        router_w = sb("router_w", [P, KT, E])
        router_b = sb("router_b", [P, E])
        eps = sb("eps", [P, 8])
        sums = sb("sums", [P, 16])
        warm = sb("warm", [P, 2])
        soft = sb("soft", [P, 2, 8])
        logits = sb("logits", [P, TT, E + TOP])
        struck = sb("struck", [P, TT, E + TOP])
        best = sb("best", [P, TT, 8])
        strike = sb("strike", [P, TT, 8])
        chosen = sb("chosen", [P, TT, E])
        expo = sb("expo", [P, TT, E])
        routing = sb("routing", [P, TT, 2 * E])
        places = sb("places", [P, TT, ROUNDS * E])
        over = sb("over", [1, ROUNDS * E + 1], I32)
        areas = {"h": 2048, "a": 4096, "g": 4096 + TT * ROPE, "s": 3072, "o": 2048, "t": 2 * (SEQ + P)}
        arena = {n: sb(f"area_{n}", [P, w]) for n, w in areas.items()}

        def view(area, at, *shape):
            n = int(np.prod(shape))
            v = arena[area][:, at:at + n]
            if len(shape) == 2:
                v = v.rearrange("p (a b) -> p a b", a=shape[0])
            if len(shape) == 3:
                v = v.rearrange("p (a b c) -> p a b c", a=shape[0], b=shape[1])
            return v

        hT = view("h", 0, KT, SEQ)
        xs = view("a", 0, TT, D)
        qmT = view("a", 0, HEADS, SEQ)
        kT = view("a", 2048, HEADS // 2, SEQ)
        va = view("a", 3072, TT, AW)
        qTb = view("a", 0, HEADS, SEQ)
        kTb = view("a", 2048, HEADS, SEQ)
        qb = xrow[:, :, 0:HEADS * QK_B]
        kcat = view("g", 0, TT, HEADS, QK_B)
        cn = view("g", 1536, TT, Q_RANK + KV_RANK)
        cT = view("g", 2304, 3, SEQ)
        rope_a = view("g", 3072, TT, HEADS, ROPE)
        rope_b = view("g", 3584, TT, HEADS, ROPE)
        kr = view("g", 4096, TT, ROPE)
        gateT = view("g", 0, 2 * KT, SEQ)
        vb = view("s", 0, TT, AW)
        probs = view("s", 1024, 2, TT, SEQ)
        probsT = view("s", 2048, 2, TT, SEQ)
        oT = view("o", 0, HEADS, SEQ)
        kr_b, kr_c = sb("kr_b", [P, TT, ROPE]), sb("kr_c", [P, TT, ROPE])
        h2 = view("h", 0, TT, D)
        up_bias = view("a", 0, 2 * F)
        g2 = view("a", 2048, D)
        x2T = view("g", 2048, KT, SEQ)
        gate_c, up_c, sig, act_v = (view("g", 512 * n, BANK) for n in range(4))
        x_e = view("g", 2048, BANK)
        xT_e = view("g", 2560, 2, BANK)
        actT = view("g", 3584, BANK)
        gf = view("s", 0, D)
        y_e = view("s", 1024, BANK)
        pick = view("s", 1536, 2, TT, CAP)
        expert_row = view("s", 1792, 2, CAP)
        part_rows = view("s", 1920, TT, P)
        gated = view("o", 0, 2, TT, 4 * CAP)
        gatedT = view("o", 1024, 2, 4, P)
        dist = arena["t"][:, 0:SEQ + P]
        log_count = arena["t"][:, SEQ + P:2 * (SEQ + P)]

        def cst(name):
            a, n = place[name]
            return const[:, a:a + n]
        ident = cst("ident")
        cos2 = cst("cos").rearrange("p (t n) -> p t n", t=TT)
        sin2 = cst("sin").rearrange("p (t n) -> p t n", t=TT)
        slots, before, ones, fold = (cst(n) for n in ("slots", "before", "ones", "fold"))

        ps = ctx.enter_context(nc.psum_tensor("ps", [P, 8, BANK], F32))
        GATE, UP, Y, MIX = 4, 5, 6, 7

        s_g2c = sem("g2_col_loaded")
        s_x, s_const, s_tab, s_small, s_mid = (sem("x_loaded0"), sem("x_loaded1")), sem("const_loaded"), sem("table_loaded"), sem("small_loaded"), sem("mid_loaded")
        s_xagain = sem("x_again")
        s_bias = sem("bias_loaded")
        loaded = [sem(f"slot_loaded{s}") for s in range(RING)]
        freed = sem("ring_freed")
        squares, power, ms = sem("squares"), sem("power"), sem("mean_squares")
        xs_ready, hT_ps, hT_v, hT_a = sem("xs_ready"), sem("hT_ps"), sem("hT_vector"), sem("hT_scalar")
        zeroed, cleared = sem("zeroed"), sem("cleared")
        lat_sq, cn_ready, kr_ready = sem("latent_squares"), sem("cn_ready"), sem("kr_ready")
        q_ready, k_ready = sem("q_ready"), sem("k_ready")
        cT_ps, cT_ready = sem("cT_ps"), sem("cT_ready")
        va_ready = sem("va_ready")
        uq_half, qb_ready, kvb_ready = sem("uq_half"), sem("qb_ready"), sem("kvb_ready")
        roped, rope_step = sem("roped"), sem("rope_step")
        s_done, max_ready, dve_step = sem("scores_done"), sem("max_ready"), sem("dve_step")
        exp_done, probs_ready = sem("exp_done"), sem("probs_ready")
        pT_ps, pT_ready, pv_done, o_ready = sem("probsT_ps"), sem("probsT_ready"), sem("pv_done"), sem("o_ready")
        bT_ps, bq_ready, bk_ready = sem("bT_ps"), sem("bq_ready"), sem("bk_ready")
        gz_ready, gates_on = sem("gate_z_ready"), sem("gates_on")
        ab_done, merged = sem("ab_done"), sem("merged")
        wo_half = sem("wo_half")
        x2_ready, x2_sq, h2_ready = sem("x2_ready"), sem("x2_squares"), sem("h2_ready")
        x2T_ps, x2T_v, x2T_a = sem("x2T_ps"), sem("x2T_vector"), sem("x2T_scalar")
        router_ready = sem("router_ready")
        part_done, part_ready, logit_done, top_ready, expo_ready = sem("part_done"), sem("part_ready"), sem("logit_done"), sem("top_ready"), sem("expo_ready")
        chosen_ready, rout_ready, count_done = sem("chosen_ready"), sem("rout_ready"), sem("count_done")
        first_gates, first_ps, down_bias_in = sem("first_gates"), sem("first_ps"), sem("down_bias_loaded")
        over_ready, moe_zero = sem("over_ready"), sem("moe_zero")
        pick_ready, gated_ready, gathered, xe_ready, xT_done, xT_ready = (sem(n) for n in ("pick_ready", "gated_ready", "gathered", "xe_ready", "xT_done", "xT_ready"))
        gT_done, gT_ready, up_done, clamped, sig_ready = (sem(n) for n in ("gatedT_done", "gatedT_ready", "up_done", "clamped", "sig_ready"))
        act_ready, actT_done, actT_ready, y_ready = (sem(n) for n in ("act_ready", "actT_done", "actT_ready", "y_ready"))
        first_rows = sem("first_rows")
        clamped2, raised, scattered = sem("clamped_up"), sem("raised"), sem("scattered")
        v_loaded, v_pick, v_gathered, v_xe, v_xTd, v_xT, v_gTd, v_gT = (sem("over_" + n) for n in (
            "loaded", "pick", "gathered", "xe", "xT_done", "xT", "gatedT_done", "gatedT"))
        v_up, v_cl, v_sig, v_act, v_aTd, v_aT, v_yd, v_y = (sem("over_" + n) for n in (
            "up_done", "clamped", "sig", "act", "actT_done", "actT", "y_done", "y"))
        v_cl2, v_raised = sem("over_clamped_up"), sem("over_raised")
        total, fin_sq, fin_ready, s_out = sem("total"), sem("fin_squares"), sem("fin_ready"), sem("stored")

        x_rows = x[0].rearrange("(t p) d -> p t d", p=P)
        out_rows = out[0].rearrange("(t p) d -> p t d", p=P)
        win = w_in[0].rearrange("(k p) n -> p k n", p=P)
        up_rows = w_gate_up[0].rearrange("e (k p) n -> p (e k) n", p=P)
        down_rows = w_down[0].rearrange("e (k p) n -> p (e k) n", p=P)
        ab_rows = [w[0].rearrange("(k p) n -> p k n", p=P) for w in (w_a_out, w_b_out)]
        wo_rows = w_o[0].rearrange("(k p) n -> p k n", p=P)

        def slot(n, *shape):
            v = ring[:, n % RING, 0:int(np.prod(shape))]
            if len(shape) == 2:
                v = v.rearrange("p (a b) -> p a b", a=shape[0])
            return v

        def through(name):
            return FIRST[name] + dict(FRONT)[name]

        block = ctx.enter_context(nc.Block())

        @block.sync
        def _(sp):
            front = []
            for n in range(2):
                front.append((slot(n, 4, LATENT), win[:, 4 * n:4 * n + 4, OFF_LATENT:OFF_GATES]))
            for n in range(4):
                front.append((slot(FIRST["qk"] + n, 2, 2 * AW), win[:, 2 * n:2 * n + 2, 0:2 * AW]))
            for n in range(2):
                front.append((slot(FIRST["v"] + n, 4, AW), win[:, 4 * n:4 * n + 4, 2 * AW:3 * AW]))
            front.append((slot(FIRST["uq"], 2, HEADS * QK_B), w_uq[0].rearrange("(k p) h e -> p k (h e)", p=P)))
            front.append((slot(FIRST["uk"], HEADS * NOPE), w_uk[0].rearrange("p h e -> p (h e)")))
            front.append((slot(FIRST["uv"], HEADS * HD), w_uv[0].rearrange("p h e -> p (h e)")))
            for n in range(8):
                a = OFF_GATES + n * 2 * P
                front.append((slot(FIRST["gates"] + n, KT, 2 * P), win[:, :, a:a + 2 * P]))
            for half in range(2):
                for m in range(2):
                    front.append((slot(FIRST["out"] + 2 * half + m, 4, BANK),
                                  ab_rows[m][:, :, half * BANK:(half + 1) * BANK]))
            for n in range(4):
                front.append((slot(FIRST["wo"] + n, 2, D), wo_rows[:, 2 * n:2 * n + 2, :]))
            for t in range(TT):
                sp.dma_start(xrow[:, t:t + 1, :], x_rows[:, t:t + 1, :]).then_inc(s_x[t], 16)
            for n, (dst, src) in enumerate(front):
                if n >= RING:
                    sp.wait_ge(freed, n - RING + 1)
                sp.dma_start(dst, src).then_inc(loaded[n % RING], 16)
            with sp.Fori(0, E // UNROLL) as i:
                for u in range(UNROLL):
                    for j in range(PER_EXPERT):
                        n = N_FRONT + u * PER_EXPERT + j
                        sp.wait_ge(freed, i * (UNROLL * PER_EXPERT) + (n - RING + 1))
                        if j < UP_SLOTS:
                            dst = ring[:, n % RING:n % RING + 1, :]
                            src = up_rows[:, bass.ds(i * (UNROLL * KT) + (u * KT + j), 1), :]
                        else:
                            dst = slot(n, 2, D)
                            src = down_rows[:, bass.ds(i * (UNROLL * KT) + (u * KT + 2 * (j - UP_SLOTS)), 2), :]
                        sp.dma_start(dst, src).then_inc(loaded[n % RING], 16)

            sp.wait_ge(freed, N_FRONT + E * PER_EXPERT)
            sp.wait_ge(over_ready, 1)
            any_over = sp.value_load(over[0:1, ROUNDS * E:ROUNDS * E + 1])
            with sp.If(any_over > 0):
                done = sp.alloc_register("over_done_sp")
                sp.reg_mov(done, 0)
                with sp.Fori(1, ROUNDS) as r:
                    with sp.Fori(0, E) as e:
                        need = sp.value_load(over[0:1, bass.ds(r * E + e, 1)])
                        with sp.If(need > 0):
                            k = sp.snap(done)
                            row = sp.snap(e * KT)
                            sp.reg_add(done, done, 1)
                            sp.wait_ge(scattered, k + 1)
                            for j in range(UP_SLOTS):
                                sp.dma_start(ring[:, j:j + 1, :], up_rows[:, bass.ds(row + j, 1), :]).then_inc(v_loaded, 16)
                            for j in range(DOWN_SLOTS):
                                sp.dma_start(slot(UP_SLOTS + j, 2, D), down_rows[:, bass.ds(row + 2 * j, 2), :]).then_inc(v_loaded, 16)
                        sp.nop()
                sp.nop()
            sp.nop()

        @block.gpsimd
        def _(pool):
            pool.memset(eps[:, :], -0.5).then_inc(zeroed, 1)
            pool.wait_ge(zeroed, 1)
            pool.wait_ge(ms, 1)
            pool.tensor_tensor(sums[:, 2:4], sums[:, 2:4], eps[:, 0:2], ALU.pow).then_inc(power, 1)
            pool.wait_ge(hT_ps, 4)
            pool.memset(qmT, 0.0).then_inc(cleared, 1)
            pool.wait_ge(ms, 2)
            pool.tensor_tensor(sums[:, 8:12], sums[:, 8:12], eps[:, 0:4], ALU.pow).then_inc(power, 1)
            steps = 0

            def turn(rows, a, b, heads):
                nonlocal steps
                half = ROPE // 2
                if heads:
                    c, s = (t.unsqueeze(2).to_broadcast([P, TT, HEADS, ROPE]) for t in (cos2, sin2))
                else:
                    c, s = cos2, sin2
                pool.tensor_tensor(a, rows, c, ALU.mult).then_inc(rope_step, 1)
                pool.tensor_tensor(b, rows, s, ALU.mult).then_inc(rope_step, 1)
                steps += 2
                pool.wait_ge(rope_step, steps)
                if heads:
                    pool.tensor_tensor(rows[:, :, :, 0:half], a[:, :, :, 0:half], b[:, :, :, half:ROPE], ALU.add)
                    return pool.tensor_tensor(rows[:, :, :, half:ROPE], a[:, :, :, half:ROPE], b[:, :, :, 0:half], ALU.add)
                pool.tensor_tensor(rows[:, :, 0:half], a[:, :, 0:half], b[:, :, half:ROPE], ALU.add)
                return pool.tensor_tensor(rows[:, :, half:ROPE], a[:, :, half:ROPE], b[:, :, 0:half], ALU.add)

            pool.wait_ge(kr_ready, 1)
            turn(kr, kr_c[:, :, :], kr_b[:, :, :], False).then_inc(rope_step, 1)
            steps += 1
            pool.wait_ge(rope_step, steps)
            pool.tensor_copy(kcat[:, :, :, NOPE:QK_B], kr.unsqueeze(2).to_broadcast([P, TT, HEADS, ROPE])).then_inc(roped, 1)
            pool.wait_ge(qb_ready, 2)
            turn(qb.rearrange("p t (h e) -> p t h e", h=HEADS)[:, :, :, NOPE:QK_B], rope_a, rope_b, True).then_inc(roped, 1)
            pool.wait_ge(s_done, 2 * HEADS)
            pool.memset(up_bias, 0.0).then_inc(cleared, 1)
            pool.wait_ge(pv_done, HEADS)
            pool.memset(y_e, 0.0).then_inc(cleared, 1)
            pool.memset(routing[:, :, :], 0.0).then_inc(moe_zero, 1)
            pool.memset(logits[:, :, E:E + TOP], BIG).then_inc(moe_zero, 1)
            pool.memset(strike[:, :, TOP:8], BIG).then_inc(moe_zero, 1)
            for n in range(2 * TT):
                t = n % TT
                pool.wait_ge(ms, 3 + n)
                pool.tensor_tensor(sums[:, 2 + t:3 + t], sums[:, 2 + t:3 + t], eps[:, 0:1], ALU.pow).then_inc(power, 1)
                if n == TT - 1:
                    pool.memset(gated[:, 1], 0.0).then_inc(moe_zero, 1)

        @block.scalar
        def _(act):
            nc.scalar.dma_start(const[:, :], table[:, 0:fixed_width]).then_inc(s_const, 16)
            with nc.allow_non_contiguous_dma(reason="norm weights as columns, 1.4k words"):
                act.dma_start(g1[:, :], norm1_g[0].rearrange("(k p) -> p k", p=P)).then_inc(s_small, 16)
                act.dma_start(gq[:, :], q_a_norm_g[0].rearrange("(k p) -> p k", p=P)).then_inc(s_small, 16)
                act.dma_start(gkv[:, :], kv_a_norm_g[0].rearrange("(k p) -> p k", p=P)).then_inc(s_small, 16)
                act.dma_start(g2_col[:, :], norm2_g[0].rearrange("(k p) -> p k", p=P)).then_inc(s_g2c, 16)
            act.dma_start(arena["t"][:, :], table[:, fixed_width:table_width]).then_inc(s_tab, 16)
            act.dma_start(router_w[:, :, :], w_router[0].rearrange("(k p) e -> p k e", p=P)).then_inc(s_mid, 16)
            act.dma_start(router_b[:, :], b_router[0:1, :].to_broadcast([P, E])).then_inc(s_mid, 16)

            for t in range(TT):
                act.wait_ge(s_x[t], 16)
                act.activation(arena["h"][:, t * D:(t + 1) * D], xrow[:, t, :], ACT.Square, accum_out=sums[:, t:t + 1]).then_inc(squares, 1)
            act.wait_ge(s_small, 48)
            act.wait_ge(squares, TT)
            for j in (2, 3):
                act.wait_ge(hT_ps, j + 1)
                for k in range(2):
                    last = act.activation(hT[:, 2 * j + k, :], ps[:, j, k * SEQ:(k + 1) * SEQ], ACT.Copy,
                                          scale=g1[:, 2 * j + k:2 * j + k + 1])
                last.then_inc(hT_a, 1)
            for t in range(TT):
                act.wait_ge(freed, through("latent"))
                act.activation(cn[:, t, 0:Q_RANK], ps[:, 4 + t, 0:Q_RANK], ACT.Square, accum_out=sums[:, 4 + t:5 + t])
                act.activation(cn[:, t, Q_RANK:], ps[:, 4 + t, Q_RANK:Q_RANK + KV_RANK], ACT.Square,
                               accum_out=sums[:, 6 + t:7 + t]).then_inc(lat_sq, 1)
            act.wait_ge(freed, through("qk"))
            act.wait_ge(hT_ps, 4)
            for j in range(2):
                last = act.activation(kT[:, 2 * j:2 * j + 2, :], ps[:, 2 + j, :].rearrange("p (a b) -> p a b", a=2), ACT.Copy)
            last.then_inc(k_ready, 1)

            def exps(k):
                act.wait_ge(max_ready, k + 1)
                for t in range(TT):
                    src, scale = (probs[:, k % 2, t, :], 1.0) if k < HEADS else (ps[:, k % 2, t * SEQ:(t + 1) * SEQ], SCALE_B)
                    last = act.activation(probs[:, k % 2, t, :], src, ACT.Exp, bias=soft[:, k % 2, t:t + 1], scale=scale,
                                          accum_out=soft[:, k % 2, 2 + t:3 + t])
                last.then_inc(exp_done, 1)

            def take_probsT(k):
                act.wait_ge(pT_ps, k + 1)
                act.activation(probsT[:, k % 2], ps[:, 2 + k % 2, :].rearrange("p (a b) -> p a b", a=TT), ACT.Copy).then_inc(pT_ready, 1)

            exps(0)
            exps(1)
            act.wait_ge(freed, through("v"))
            for t in range(TT):
                last = act.activation(va[:, t, :], ps[:, 6 + t, :], ACT.Copy)
            last.then_inc(va_ready, 1)
            for k in range(HEADS):
                take_probsT(k)
                if k + 2 < HEADS:
                    exps(k + 2)
                if k in (2, 3):
                    t = k - 2
                    act.wait_ge(*((uq_half, 1), (freed, through("uq")))[t])
                    act.activation(qb[:, t, 0:5 * QK_B], ps[:, 6, 0:5 * QK_B], ACT.Copy)
                    act.activation(qb[:, t, 5 * QK_B:], ps[:, 7, 0:3 * QK_B], ACT.Copy).then_inc(qb_ready, 1)
                if k in (4, 5):
                    act.wait_ge(freed, through(("uk", "uv")[k - 4]))
                    for t in range(TT):
                        if k == 4:
                            last = act.activation(kcat[:, t, :, 0:NOPE], ps[:, 6 + t, :].rearrange("p (h e) -> p h e", h=HEADS), ACT.Copy)
                        else:
                            last = act.activation(vb[:, t, :], ps[:, 6 + t, :], ACT.Copy)
                    last.then_inc(kvb_ready, 1)
            for p in range(HEADS // 2):
                act.wait_ge(bT_ps, 2 * p + 1)
                act.activation(qTb[0:QK_B, 2 * p:2 * p + 2, :], ps[0:QK_B, 4 + (2 * p) % 4, :].rearrange("p (a b) -> p a b", a=2),
                               ACT.Copy).then_inc(bq_ready, 1)
            act.wait_ge(bT_ps, HEADS)
            act.dma_start(xrow[:, :, :], x_rows).then_inc(s_xagain, 16)
            exps(HEADS)
            exps(HEADS + 1)
            for k in range(HEADS, 2 * HEADS):
                take_probsT(k)
                if k + 2 < 2 * HEADS:
                    exps(k + 2)
            act.wait_ge(cleared, 2)
            act.dma_start(up_bias[0:E, :], b_gate_up[0]).then_inc(s_bias, 16)
            act.dma_start(g2[:, :], norm2_g[0:1, :].to_broadcast([P, D])).then_inc(s_bias, 16)
            act.wait_ge(cleared, 3)
            for n in range(2):
                act.dma_start(y_e[n * CAP:n * CAP + E, :], b_down[0][:, n * BANK:(n + 1) * BANK]).then_inc(down_bias_in, 16)
            act.dma_start(gf[:, :], final_g.rearrange("(a d) -> a d", a=1).to_broadcast([P, D])).then_inc(s_bias, 16)
            for n in range(4):
                act.wait_ge(gz_ready, 8)
                act.activation(gateT[:, n:2 * KT:4, :], gateT[:, n:2 * KT:4, :], ACT.Sigmoid).then_inc(gates_on, 1)
            for t in range(TT):
                act.wait_ge(x2T_ps, 2 * t + 2)
                act.activation(x2T[:, 4:8, t * P:(t + 1) * P], ps[:, 2 * t + 1, :].rearrange("p (a b) -> p a b", a=4), ACT.Copy).then_inc(x2T_a, 1)
                for n in range(2):
                    act.wait_ge(x2_ready, 2 * t + n + 1)
                    a = (2 * t + n) * BANK
                    act.activation(arena["o"][:, a:a + BANK], xrow[:, t, n * BANK:(n + 1) * BANK], ACT.Square,
                                   accum_out=sums[:, 4 + 2 * t + n:5 + 2 * t + n]).then_inc(x2_sq, 1)
            act.wait_ge(zeroed, 1)
            act.activation(warm[:, 0:1], eps[:, 0:1], ACT.Exp)
            for t in range(TT):
                act.wait_ge(top_ready, t + 1)
                last = act.activation(expo[:, t, :], logits[:, t, 0:E], ACT.Exp, bias=sums[:, 12 + t:13 + t])
            last.then_inc(expo_ready, 1)
            act.activation(warm[:, 1:2], eps[:, 0:1], ACT.Sigmoid)

            def take_mix(dst):
                return act.activation(dst, ps[:, MIX, :], ACT.Copy)

            act.wait_ge(gathered, 1)
            take_mix(x_e).then_inc(xe_ready, 1)
            act.wait_ge(xT_done, 1)
            take_mix(xT_e[:, 0]).then_inc(xT_ready, 1)
            act.wait_ge(first_ps, 1)
            act.activation(gatedT[:, 1].rearrange("p a b -> p (a b)"), ps[:, Y, :], ACT.Copy).then_inc(y_ready, 1)
            with act.Fori(0, E // UNROLL) as i:
                for u in range(UNROLL):
                    e = i * UNROLL + u
                    act.wait_ge(gathered, e + 2)
                    take_mix(x_e).then_inc(xe_ready, 1)
                    act.wait_ge(xT_done, e + 2)
                    take_mix(xT_e[:, (u + 1) % 2]).then_inc(xT_ready, 1)
                    act.wait_ge(gT_done, e + 1)
                    take_mix(gatedT[:, u % 2].rearrange("p a b -> p (a b)")).then_inc(gT_ready, 1)
                    act.wait_ge(clamped, e + 1)
                    act.activation(sig, gate_c, ACT.Sigmoid, scale=ALPHA).then_inc(sig_ready, 1)
                    act.wait_ge(freed, i * (UNROLL * PER_EXPERT) + (N_FRONT + (u + 1) * PER_EXPERT))
                    act.activation(y_e, ps[:, Y, :], ACT.Copy).then_inc(y_ready, 1)

            act.wait_ge(over_ready, 1)
            any_over = act.value_load(over[0:1, ROUNDS * E:ROUNDS * E + 1])
            with act.If(any_over > 0):
                done = act.alloc_register("over_done_act")
                act.reg_mov(done, 0)
                with act.Fori(1, ROUNDS) as r:
                    with act.Fori(0, E) as e:
                        need = act.value_load(over[0:1, bass.ds(r * E + e, 1)])
                        with act.If(need > 0):
                            k = act.snap(done)
                            act.wait_ge(v_gathered, k + 1)
                            take_mix(x_e).then_inc(v_xe, 1)
                            act.wait_ge(v_xTd, k + 1)
                            take_mix(xT_e[:, 0]).then_inc(v_xT, 1)
                            act.wait_ge(v_gTd, k + 1)
                            take_mix(gatedT[:, 0].rearrange("p a b -> p (a b)")).then_inc(v_gT, 1)
                            act.wait_ge(v_cl, k + 1)
                            act.activation(sig, gate_c, ACT.Sigmoid, scale=ALPHA).then_inc(v_sig, 1)
                            act.wait_ge(v_yd, k + 1)
                            act.activation(y_e, ps[:, Y, :], ACT.Copy).then_inc(v_y, 1)
                            act.reg_add(done, done, 1)
                        act.nop()
                act.nop()
            for t in range(TT):
                for n in range(2):
                    act.wait_ge(total, 2 * t + n + 1)
                    act.activation(h2[:, t, n * BANK:(n + 1) * BANK], xrow[:, t, n * BANK:(n + 1) * BANK], ACT.Square,
                                   accum_out=sums[:, 4 + 2 * t + n:5 + 2 * t + n]).then_inc(fin_sq, 1)
            for m in range(2 * TT):
                t, a = m // 2, m % 2 * BANK
                act.wait_ge(fin_ready, m + 1)
                act.dma_start(out_rows[:, t:t + 1, a:a + BANK], xrow[:, t:t + 1, a:a + BANK]).then_inc(s_out, 16)
            act.wait_ge(s_out, 16 * 2 * TT)

        @block.vector
        def _(dve):
            step = [0]

            def step_wait():
                dve.wait_ge(dve_step, step[0])

            def stepped(ins):
                ins.then_inc(dve_step, 1)
                step[0] += 1

            dve.wait_ge(squares, TT)
            dve.tensor_scalar(sums[:, 2:4], sums[:, 0:2], 1.0 / D, EPS, ALU.mult, ALU.add).then_inc(ms, 1)
            dve.wait_ge(power, 1)
            for t in range(TT):
                dve.wait_ge(s_x[t], 16)
                dve.tensor_scalar(xs[:, t, :], xrow[:, t, :], sums[:, 2 + t:3 + t], None, ALU.mult).then_inc(xs_ready, 1)
            dve.wait_ge(s_small, 48)
            for j in (0, 1):
                dve.wait_ge(hT_ps, j + 1)
                dve.tensor_tensor(hT[:, 2 * j:2 * j + 2, :], ps[:, j, :].rearrange("p (a b) -> p a b", a=2),
                                  g1[:, 2 * j:2 * j + 2].unsqueeze(2).to_broadcast([P, 2, SEQ]), ALU.mult).then_inc(hT_v, 1)
            dve.wait_ge(lat_sq, TT)
            stepped(dve.tensor_scalar(sums[:, 8:10], sums[:, 4:6], 1.0 / Q_RANK, EPS, ALU.mult, ALU.add))
            dve.tensor_scalar(sums[:, 10:12], sums[:, 6:8], 1.0 / KV_RANK, EPS, ALU.mult, ALU.add).then_inc(ms, 1)
            for t in range(TT):
                last = dve.tensor_copy(kr[:, t, :], ps[:, 4 + t, Q_RANK + KV_RANK:LATENT])
            last.then_inc(kr_ready, 1)
            dve.wait_ge(power, 2)
            for t in range(TT):
                dve.tensor_scalar(cn[:, t, 0:Q_RANK], ps[:, 4 + t, 0:Q_RANK], sums[:, 8 + t:9 + t], None, ALU.mult)
                last = dve.tensor_scalar(cn[:, t, Q_RANK:], ps[:, 4 + t, Q_RANK:Q_RANK + KV_RANK], sums[:, 10 + t:11 + t], None, ALU.mult)
            last.then_inc(cn_ready, 1)
            dve.wait_ge(freed, through("qk"))
            dve.wait_ge(cleared, 1)
            for j in range(2):
                for o in range(2):
                    last = dve.tensor_scalar(qmT[o * HD:(o + 1) * HD, 4 * j + o:4 * j + o + 3:2, :],
                                             ps[o * HD:(o + 1) * HD, j, :].rearrange("p (a b) -> p a b", a=2), SCALE_A, None, ALU.mult)
            last.then_inc(q_ready, 1)
            dve.wait_ge(cT_ps, 1)
            dve.tensor_tensor(cT[:, 0:2, :], ps[:, 6, :].rearrange("p (a b) -> p a b", a=2),
                              gq[:, :].unsqueeze(2).to_broadcast([P, 2, SEQ]), ALU.mult)
            dve.tensor_scalar(cT[:, 2, :], ps[:, 7, 0:SEQ], gkv[:, 0:1], None, ALU.mult).then_inc(cT_ready, 1)

            def maxes(k):
                dve.wait_ge(s_done, k + 1)
                b = k % 2
                if k < HEADS:
                    slope = 2.0 ** (-8.0 * (k + 1) / HEADS)
                    for t in range(TT):
                        at = P * (TT - 1 - t)
                        stepped(dve.scalar_tensor_tensor(out=probs[:, b, t, :], in0=dist[:, at:at + SEQ], scalar=-slope,
                                                         in1=ps[:, b, t * SEQ:(t + 1) * SEQ], op0=ALU.mult, op1=ALU.add))
                    for t in range(TT):
                        at = P * (TT - 1 - t)
                        dve.wait_ge(dve_step, step[0] - (TT - 1))
                        stepped(dve.tensor_tensor_reduce(probs[:, b, t, :], probs[:, b, t, :], log_count[:, at:at + SEQ], 1.0, -BIG,
                                                         ALU.add, ALU.max, soft[:, b, 6 + t:7 + t]))
                else:
                    stepped(dve.tensor_reduce(soft[:, b, 6:8], ps[:, b, :].rearrange("p (a b) -> p a b", a=TT), AX_X, ALU.max))
                step_wait()
                dve.tensor_scalar(soft[:, b, 0:2], soft[:, b, 6:8], -1.0 if k < HEADS else -SCALE_B, None, ALU.mult).then_inc(max_ready, 1)

            def norms(k):
                b = k % 2
                dve.wait_ge(exp_done, k + 1)
                stepped(dve.reciprocal(soft[:, b, 4:6], soft[:, b, 2:4]))
                step_wait()
                for t in range(TT):
                    last = dve.tensor_scalar(probs[:, b, t, :], probs[:, b, t, :], soft[:, b, 4 + t:5 + t], None, ALU.mult)
                last.then_inc(probs_ready, 1)

            def take_o(p):
                dve.wait_ge(pv_done, p + 1)
                dve.tensor_copy(oT[:, p, :], ps[:, 4 + p % 2, 0:SEQ]).then_inc(o_ready, 1)

            def take_gates(g):
                dve.wait_ge(freed, FIRST["gates"] + g + 1)
                dve.tensor_copy(gateT[:, 2 * g:2 * g + 2, :], ps[:, 6 + g % 2, :].rearrange("p (a b) -> p a b", a=2)).then_inc(gz_ready, 1)

            dve.wait_ge(s_tab, 16)
            maxes(0)
            maxes(1)
            norms(0)
            norms(1)
            for k in range(2, HEADS):
                maxes(k)
                norms(k)
                if k >= 4 and k % 2 == 0:
                    take_o(k // 2 - 2)
            take_o(2)
            take_o(3)
            for p in range(HEADS // 2):
                dve.wait_ge(bT_ps, 2 * p + 2)
                dve.tensor_copy(kTb[0:QK_B, 2 * p:2 * p + 2, :], ps[0:QK_B, 4 + (2 * p + 1) % 4, :].rearrange("p (a b) -> p a b", a=2)).then_inc(bk_ready, 1)
            maxes(HEADS)
            maxes(HEADS + 1)
            norms(HEADS)
            norms(HEADS + 1)
            take_gates(0)
            dve.wait_ge(s_mid, 32)
            dve.wait_ge(s_g2c, 16)
            dve.tensor_tensor(router_w[:, :, :], router_w[:, :, :], g2_col[:, :].unsqueeze(2).to_broadcast([P, KT, E]), ALU.mult).then_inc(router_ready, 1)
            for k in range(HEADS, 2 * HEADS):
                if k + 2 < 2 * HEADS:
                    maxes(k + 2)
                    norms(k + 2)
                if k > HEADS and k % 2 == 0:
                    take_o(k // 2 - 1)
                if k - HEADS < 7:
                    take_gates(k - HEADS + 1)
            take_o(7)
            for d in range(KT):
                dve.wait_ge(ab_done, d + 1)
                dve.wait_ge(gates_on, d % 4 + 1)
                stepped(dve.tensor_tensor(gateT[:, d:d + KT + 1:KT, :], gateT[:, d:d + KT + 1:KT, :],
                                          ps[:, d % 4, :].rearrange("p (a b) -> p a b", a=2), ALU.mult))
                step_wait()
                dve.tensor_tensor(gateT[:, d, :], gateT[:, d, :], gateT[:, KT + d, :], ALU.add).then_inc(merged, 1)
            dve.wait_ge(s_xagain, 16)
            dve.wait_ge(s_bias, 48)
            dve.wait_ge(moe_zero, 3)
            for t in range(TT):
                dve.wait_ge(*((wo_half, 1), (freed, through("wo")))[t])
                for n in range(2):
                    dve.tensor_tensor(xrow[:, t, n * BANK:(n + 1) * BANK], xrow[:, t, n * BANK:(n + 1) * BANK], ps[:, 4 + 2 * t + n, :],
                                      ALU.add).then_inc(x2_ready, 1)
                dve.wait_ge(x2T_ps, 2 * t + 1)
                dve.tensor_copy(x2T[:, 0:4, t * P:(t + 1) * P], ps[:, 2 * t, :].rearrange("p (a b) -> p a b", a=4)).then_inc(x2T_v, 1)
                dve.wait_ge(x2_sq, 2 * t + 2)
                stepped(dve.tensor_tensor(sums[:, t:t + 1], sums[:, 4 + 2 * t:5 + 2 * t], sums[:, 5 + 2 * t:6 + 2 * t], ALU.add))
                step_wait()
                dve.tensor_scalar(sums[:, 2 + t:3 + t], sums[:, t:t + 1], 1.0 / D, EPS, ALU.mult, ALU.add).then_inc(ms, 1)
                dve.wait_ge(part_done, t + 1)
                dve.tensor_copy(part_rows[:, t, :], ps[:, 4, 0:P]).then_inc(part_ready, 1)
                dve.wait_ge(power, 3 + t)
                dve.wait_ge(logit_done, t + 1)
                stepped(dve.scalar_tensor_tensor(out=logits[:, t, 0:E], in0=ps[:, 5, t * E:(t + 1) * E], scalar=sums[:, 2 + t:3 + t],
                                                 in1=router_b[:, :], op0=ALU.mult, op1=ALU.add))
                step_wait()
                stepped(dve.max(best[:, t, :], logits[:, t, 0:E]))
                step_wait()
                dve.tensor_scalar(sums[:, 12 + t:13 + t], best[:, t, 0:1], -1.0, None, ALU.mult).then_inc(top_ready, 1)
                stepped(dve.tensor_copy(strike[:, t, 0:TOP], best[:, t, 0:TOP]))
                step_wait()
                stepped(dve.match_replace(struck[:, t, :], strike[:, t, :], logits[:, t, :], -BIG))
                step_wait()
                dve.tensor_scalar(chosen[:, t, :], struck[:, t, 0:E], -BIG, None, ALU.is_equal).then_inc(chosen_ready, 1)
                dve.scalar_tensor_tensor(out=h2[:, t, :], in0=xrow[:, t, :], scalar=sums[:, 2 + t:3 + t], in1=g2,
                                         op0=ALU.mult, op1=ALU.mult).then_inc(h2_ready, 1)
            dve.wait_ge(chosen_ready, TT)
            dve.wait_ge(count_done, 1)
            stepped(dve.scalar_tensor_tensor(out=struck[:, :, 0:E], in0=ps[:, 0, 0:TT * E].rearrange("p (t e) -> p t e", t=TT),
                                             scalar=1.0, in1=chosen[:, :, :], op0=ALU.add, op1=ALU.mult))
            step_wait()
            for r in range(ROUNDS):
                stepped(dve.tensor_scalar(places[:, :, r * E:(r + 1) * E], struck[:, :, 0:E], -float(1 + CAP * r), None, ALU.add))
            step_wait()
            def build_picks(b, je):
                for t in range(TT):
                    last = dve.tensor_scalar(pick[:, b, t, :], slots[:, 0:CAP], places[:, t, bass.ds(je, 1)], None, ALU.is_equal)
                return last

            def build_gated(b, e, je):
                for t in range(TT):
                    dve.tensor_scalar(gated[:, b, t, :], slots, places[:, t, bass.ds(je, 1)], routing[:, t, bass.ds(e, 1)],
                                      ALU.is_equal, ALU.mult)
                return dve.tensor_copy(expert_row[:, b, :], ident[:, bass.ds(e, 1)].to_broadcast([P, CAP]))

            def clamp_gate():
                return dve.tensor_scalar(gate_c, ps[:, GATE, :], LIMIT, None, ALU.min)

            def clamp_up():
                return dve.tensor_scalar(up_c, ps[:, UP, :], LIMIT, -LIMIT, ALU.min, ALU.max)

            for b in range(2):
                build_picks(b, b).then_inc(pick_ready, 1)
            dve.wait_ge(expo_ready, 1)
            stepped(dve.tensor_tensor(expo[:, :, :], expo[:, :, :], chosen[:, :, :], ALU.mult))
            step_wait()
            stepped(dve.tensor_reduce(sums[:, 4:6], expo[:, :, :], AX_X, ALU.add))
            step_wait()
            stepped(dve.reciprocal(sums[:, 6:8], sums[:, 4:6]))
            step_wait()
            for t in range(TT):
                last = dve.tensor_scalar(routing[:, t, 0:E], expo[:, t, :], sums[:, 6 + t:7 + t], None, ALU.mult)
            last.then_inc(rout_ready, 1)
            dve.wait_ge(rout_ready, 1)
            build_gated(0, 0, 0).then_inc(gated_ready, 1)
            dve.wait_ge(moe_zero, 4)
            for n in range(2):
                a = n * 3 * CAP
                last = dve.tensor_copy(gated[:, 1, :, a:a + E], routing[:, :, 0:E])
            last.then_inc(first_gates, 1)
            for r in range(ROUNDS):
                stepped(dve.tensor_scalar(over[0:1, r * E:(r + 1) * E], ps[0:1, 0, TT * E:(TT + 1) * E], float(CAP * r), None, ALU.is_gt))
            stepped(dve.tensor_reduce(sums[0:1, 14:15], ps[0:1, 0, TT * E:(TT + 1) * E], AX_X, ALU.max))
            step_wait()
            dve.tensor_scalar(over[0:1, ROUNDS * E:ROUNDS * E + 1], sums[0:1, 14:15], float(CAP), None, ALU.is_gt).then_inc(over_ready, 1)
            dve.wait_ge(first_ps, 1)
            build_gated(1, 1, 1).then_inc(gated_ready, 1)
            with dve.Fori(0, E // UNROLL) as i:
                for u in range(UNROLL):
                    e = i * UNROLL + u
                    dve.wait_ge(up_done, e + 1)
                    clamp_gate().then_inc(clamped, 1)
                    clamp_up().then_inc(clamped2, 1)
                    dve.wait_ge(clamped, e + 1)
                    dve.wait_ge(clamped2, e + 1)
                    dve.scalar_tensor_tensor(out=up_c, in0=up_c, scalar=1.0, in1=gate_c, op0=ALU.add, op1=ALU.mult).then_inc(raised, 1)
                    dve.wait_ge(raised, e + 1)
                    dve.wait_ge(sig_ready, e + 1)
                    dve.tensor_tensor(act_v, up_c, sig, ALU.mult).then_inc(act_ready, 1)
                    dve.wait_ge(actT_done, e + 1)
                    dve.tensor_copy(actT, ps[:, MIX, :]).then_inc(actT_ready, 1)
                    build_picks(u % 2, e + 2).then_inc(pick_ready, 1)
                    build_gated(u % 2, e + 2, e + 2).then_inc(gated_ready, 1)

            dve.wait_ge(over_ready, 1)
            any_over = dve.value_load(over[0:1, ROUNDS * E:ROUNDS * E + 1])
            with dve.If(any_over > 0):
                dve.wait_ge(scattered, 1)
                done = dve.alloc_register("over_done_dve")
                dve.reg_mov(done, 0)
                with dve.Fori(1, ROUNDS) as r:
                    with dve.Fori(0, E) as e:
                        need = dve.value_load(over[0:1, bass.ds(r * E + e, 1)])
                        with dve.If(need > 0):
                            k = dve.snap(done)
                            build_picks(0, r * E + e)
                            build_gated(0, e, r * E + e).then_inc(v_pick, 1)
                            dve.wait_ge(v_up, k + 1)
                            clamp_gate().then_inc(v_cl, 1)
                            clamp_up().then_inc(v_cl2, 1)
                            dve.wait_ge(v_cl, k + 1)
                            dve.wait_ge(v_cl2, k + 1)
                            dve.scalar_tensor_tensor(out=up_c, in0=up_c, scalar=1.0, in1=gate_c, op0=ALU.add, op1=ALU.mult).then_inc(v_raised, 1)
                            dve.wait_ge(v_raised, k + 1)
                            dve.wait_ge(v_sig, k + 1)
                            dve.tensor_tensor(act_v, up_c, sig, ALU.mult).then_inc(v_act, 1)
                            dve.wait_ge(v_aTd, k + 1)
                            dve.tensor_copy(actT, ps[:, MIX, :]).then_inc(v_aT, 1)
                            dve.wait_ge(scattered, k + 2)
                            dve.reg_add(done, done, 1)
                        dve.nop()
                dve.nop()
            for t in range(TT):
                dve.wait_ge((first_rows, scattered)[t], 1)
                for n in range(2):
                    dve.tensor_tensor(xrow[:, t, n * BANK:(n + 1) * BANK], xrow[:, t, n * BANK:(n + 1) * BANK], ps[:, 2 * t + n, :],
                                      ALU.add).then_inc(total, 1)
            for t in range(TT):
                dve.wait_ge(fin_sq, 2 * t + 2)
                stepped(dve.tensor_tensor(sums[:, t:t + 1], sums[:, 4 + 2 * t:5 + 2 * t], sums[:, 5 + 2 * t:6 + 2 * t], ALU.add))
                step_wait()
                dve.tensor_scalar(sums[:, 2 + t:3 + t], sums[:, t:t + 1], 1.0 / D, EPS, ALU.mult, ALU.add).then_inc(ms, 1)
                dve.wait_ge(power, 5 + t)
                for n in range(2):
                    half = xrow[:, t, n * BANK:(n + 1) * BANK]
                    dve.scalar_tensor_tensor(out=half, in0=half, scalar=sums[:, 2 + t:3 + t], in1=gf[:, n * BANK:(n + 1) * BANK],
                                             op0=ALU.mult, op1=ALU.mult).then_inc(fin_ready, 1)

        @block.tensor
        def _(pe):
            def arrived(n):
                pe.wait_ge(loaded[n % RING], 16 * (n // RING + 1))

            pe.wait_ge(s_const, 16)
            pe.wait_ge(xs_ready, TT)
            for j in range(4):
                for k in range(2):
                    for t in range(TT):
                        a = (2 * j + k) * P
                        last = pe.transpose(ps[:, j, k * SEQ + t * P:k * SEQ + (t + 1) * P], xs[:, t, a:a + P], ident)
                last.then_inc(hT_ps, 1)
            pe.wait_ge(hT_v, 2)
            pe.wait_ge(hT_a, 2)
            for k in range(KT):
                if k % 4 == 0:
                    arrived(FIRST["latent"] + k // 4)
                w = slot(FIRST["latent"] + k // 4, 4, LATENT)
                for t in range(TT):
                    last = pe.matmul(ps[:, 4 + t, 0:LATENT], hT[:, k, t * P:(t + 1) * P], w[:, k % 4, :], start=k == 0, stop=k == KT - 1)
                if k == 3:
                    last.then_inc(freed, 1)
            last.then_inc(freed, 1)
            for k in range(KT):
                if k % 2 == 0:
                    arrived(FIRST["qk"] + k // 2)
                w = slot(FIRST["qk"] + k // 2, 2, 2 * AW)
                for c in range(8):
                    last = pe.matmul(ps[:, c // 2, c % 2 * SEQ:(c % 2 + 1) * SEQ], w[:, k % 2, c * P:(c + 1) * P], hT[:, k, :],
                                     start=k == 0 and c % 2 == 0, stop=k == KT - 1, skip_group_check=True)
                if k % 2:
                    last.then_inc(freed, 1)
            pe.wait_ge(cn_ready, 1)
            for c in range(3):
                for t in range(TT):
                    b, a = (6, c * SEQ) if c < 2 else (7, 0)
                    last = pe.transpose(ps[:, b, a + t * P:a + (t + 1) * P], cn[:, t, c * P:(c + 1) * P], ident)
            last.then_inc(cT_ps, 1)

            def scores(k):
                for t in range(TT):
                    if k < HEADS:
                        q, key = qmT[:, k, t * P:(t + 1) * P], kT[:, k // 2, :]
                    else:
                        q, key = qTb[0:QK_B, k - HEADS, t * P:(t + 1) * P], kTb[0:QK_B, k - HEADS, :]
                    last = pe.matmul(ps[:, k % 2, t * SEQ:(t + 1) * SEQ], q, key, start=True, stop=True)
                last.then_inc(s_done, 1)

            def turn_probs(k):
                pe.wait_ge(probs_ready, k + 1)
                if k >= 2:
                    pe.wait_ge(pT_ready, k - 1)
                for c in range(TT):
                    for t in range(TT):
                        last = pe.transpose(ps[:, 2 + k % 2, c * SEQ + t * P:c * SEQ + (t + 1) * P], probs[:, k % 2, t, c * P:(c + 1) * P], ident)
                last.then_inc(pT_ps, 1)

            def attend(p):
                pe.wait_ge(pT_ready, 2 * p + 2)
                if p >= 2:
                    pe.wait_ge(o_ready, p - 1)
                v = va if p < HEADS // 2 else vb
                for c in range(TT):
                    for o in range(2):
                        h = (2 * p + o) % HEADS
                        last = pe.matmul(ps[o * HD:(o + 1) * HD, 4 + p % 2, 0:SEQ], v[:, c, h * HD:(h + 1) * HD], probsT[:, o, c, :],
                                         start=c == 0, stop=c == TT - 1)
                last.then_inc(pv_done, 1)

            pe.wait_ge(q_ready, 1)
            pe.wait_ge(k_ready, 1)
            scores(0)
            scores(1)
            pe.wait_ge(cT_ready, 1)
            for k in range(KT):
                if k % 4 == 0:
                    arrived(FIRST["v"] + k // 4)
                w = slot(FIRST["v"] + k // 4, 4, AW)
                for t in range(TT):
                    last = pe.matmul(ps[:, 6 + t, :], hT[:, k, t * P:(t + 1) * P], w[:, k % 4, :], start=k == 0, stop=k == KT - 1)
                if k % 4 == 3:
                    last.then_inc(freed, 1)

            def latent_part(n):
                name = ("uq", "uq", "uk", "uv")[n]
                arrived(FIRST[name])
                pe.wait_ge(*((va_ready, 1), (qb_ready, 1), (qb_ready, 2), (kvb_ready, 1))[n])
                if n < 2:
                    w = slot(FIRST[name], 2, HEADS * QK_B)
                    for b, (a, z) in enumerate(((0, 5 * QK_B), (5 * QK_B, HEADS * QK_B))):
                        for c in range(2):
                            last = pe.matmul(ps[:, 6 + b, 0:z - a], cT[:, c, n * P:(n + 1) * P], w[:, c, a:z], start=c == 0, stop=c == 1)
                    last.then_inc((uq_half, freed)[n], 1)
                    return
                for t in range(TT):
                    last = pe.matmul(ps[:, 6 + t, :], cT[:, 2, t * P:(t + 1) * P], slot(FIRST[name], AW), start=True, stop=True)
                last.then_inc(freed, 1)

            for p in range(HEADS // 2):
                for k in (2 * p, 2 * p + 1):
                    turn_probs(k)
                    if k + 2 < HEADS:
                        scores(k + 2)
                    if k in (2, 3, 4, 5):
                        latent_part(k - 2)
                attend(p)

            pe.wait_ge(roped, 2)
            pe.wait_ge(kvb_ready, 2)
            pe.wait_ge(o_ready, HEADS // 2)
            qb4 = qb.rearrange("p t (h e) -> p t h e", h=HEADS)
            for p in range(HEADS // 2):
                for m, rows in enumerate((qb4, kcat)):
                    if p >= 2:
                        pe.wait_ge((bq_ready, bk_ready)[m], p - 1)
                    for o in range(2):
                        for t in range(TT):
                            last = pe.transpose(ps[0:QK_B, 4 + (2 * p + m) % 4, o * SEQ + t * P:o * SEQ + (t + 1) * P],
                                                rows[:, t, 2 * p + o, :], ident)
                    last.then_inc(bT_ps, 1)

            def gates(g):
                n = FIRST["gates"] + g
                arrived(n)
                if g >= 2:
                    pe.wait_ge(gz_ready, g - 1)
                w = slot(n, KT, 2 * P)
                for c in range(2):
                    for k in range(KT):
                        last = pe.matmul(ps[:, 6 + g % 2, c * SEQ:(c + 1) * SEQ], w[:, k, c * P:(c + 1) * P], hT[:, k, :], start=k == 0, stop=k == KT - 1)
                last.then_inc(freed, 1)

            pe.wait_ge(bq_ready, HEADS // 2)
            pe.wait_ge(bk_ready, HEADS // 2)
            scores(HEADS)
            scores(HEADS + 1)
            gates(0)
            for p in range(HEADS // 2, HEADS):
                for k in (2 * p, 2 * p + 1):
                    turn_probs(k)
                    if k + 2 < 2 * HEADS:
                        scores(k + 2)
                    if k - HEADS < 7:
                        gates(k - HEADS + 1)
                attend(p)

            for d in range(KT):
                if d % 4 == 0:
                    arrived(FIRST["out"] + d // 2)
                    arrived(FIRST["out"] + d // 2 + 1)
                if d == 0:
                    pe.wait_ge(o_ready, HEADS)
                if d >= 4:
                    pe.wait_ge(merged, d - 3)
                for m in range(2):
                    w = slot(FIRST["out"] + d // 4 * 2 + m, 4, BANK)
                    for c in range(4):
                        last = pe.matmul(ps[:, d % 4, m * SEQ:(m + 1) * SEQ], w[:, c, d % 4 * P:(d % 4 + 1) * P], oT[:, 4 * m + c, :],
                                         start=c == 0, stop=c == 3)
                    if m == 0 and d % 4 == 3:
                        last.then_inc(freed, 1)
                    if m == 0 and d == 4:
                        last.then_inc(freed, 1)
                last.then_inc(ab_done, 1)
            def turn_rows(t):
                for j in range(2):
                    pe.wait_ge(x2_ready, 2 * t + j + 1)
                    for k in range(4):
                        a = (4 * j + k) * P
                        last = pe.transpose(ps[:, 2 * t + j, k * P:(k + 1) * P], xrow[:, t, a:a + P], ident)
                    last.then_inc(x2T_ps, 1)

            def route(t):
                pe.wait_ge(router_ready, 1)
                pe.wait_ge(x2T_v, t + 1)
                pe.wait_ge(x2T_a, t + 1)
                for k in range(KT):
                    q = k % 4
                    last = pe.matmul(ps[q * E:(q + 1) * E, 4, 0:P], router_w[:, k, :], x2T[:, k, t * P:(t + 1) * P], start=k < 4, stop=k >= 4)
                last.then_inc(part_done, 1)

            def add_parts(t):
                pe.wait_ge(part_ready, t + 1)
                pe.matmul(ps[:, 5, t * E:(t + 1) * E], part_rows[:, t, :], fold, start=True, stop=True).then_inc(logit_done, 1)

            for t in range(TT):
                for k in range(KT):
                    if t == 0 and k % 2 == 0:
                        arrived(FIRST["wo"] + k // 2)
                    if t == 0:
                        pe.wait_ge(merged, k + 1)
                    w = slot(FIRST["wo"] + k // 2, 2, D)
                    for n in range(2):
                        last = pe.matmul(ps[:, 4 + 2 * t + n, :], gateT[:, k, t * P:(t + 1) * P], w[:, k % 2, n * BANK:(n + 1) * BANK],
                                         start=k == 0, stop=k == KT - 1)
                    if t == 0 and k == 0:
                        last.then_inc(freed, 1)
                    if t == 0 and k == KT - 1:
                        last.then_inc(wo_half, 1)
                    if t == 1 and k % 2:
                        last.then_inc(freed, 1)
                    if t == 1 and k == 3:
                        turn_rows(0)
                    if t == 1 and k == 5:
                        route(0)
                    if t == 1 and k == 6:
                        add_parts(0)
            turn_rows(1)
            route(1)
            add_parts(1)
            pe.wait_ge(chosen_ready, 1)
            pe.matmul(ps[:, 0, 0:E], before, chosen[:, 0, :], start=True, stop=True)
            pe.matmul(ps[:, 0, 2 * E:3 * E], ones, chosen[:, 0, :], start=True, stop=False, skip_group_check=True)
            pe.matmul(ps[:, 0, E:2 * E], ones, chosen[:, 0, :], start=False, stop=False, skip_group_check=True)
            pe.wait_ge(chosen_ready, 2)
            pe.matmul(ps[:, 0, E:2 * E], before, chosen[:, 1, :], start=False, stop=True, skip_group_check=True)
            pe.matmul(ps[:, 0, 2 * E:3 * E], ones, chosen[:, 1, :], start=False, stop=True, skip_group_check=True).then_inc(count_done, 1)

            def gather(b):
                for t in range(TT):
                    for n in range(2):
                        last = pe.matmul(ps[n * CAP:(n + 1) * CAP, MIX, :], pick[:, b, t, :], h2[:, t, n * BANK:(n + 1) * BANK],
                                         start=t == 0, stop=t == TT - 1)
                return last

            def turn(rows):
                for c in range(4):
                    last = pe.transpose(ps[:, MIX, c * P:(c + 1) * P], rows[:, c * P:(c + 1) * P], ident)
                return last

            def turn_gated(b, bank=MIX):
                for n in range(2):
                    for t in range(TT):
                        last = pe.transpose(ps[:, bank, (2 * n + t) * P:(2 * n + t + 1) * P], gated[:, b, t, n * P:(n + 1) * P], ident)
                return last

            def lhs(rows, k):
                a = k % 4 * P + k // 4 * CAP
                return rows[:, a:a + CAP]

            def up_tile(b, k, w):
                for bank in (GATE, UP):
                    for n in range(2):
                        a = (bank - GATE) * F + n * BANK
                        last = pe.matmul(ps[n * CAP:(n + 1) * CAP, bank, :], lhs(xT_e[:, b], k), w[:, a:a + BANK],
                                         start=k == 0, stop=False, skip_group_check=True)
                return last

            def up_biases(b):
                for bank in (GATE, UP):
                    for n in range(2):
                        a = (bank - GATE) * F + n * BANK
                        last = pe.matmul(ps[n * CAP:(n + 1) * CAP, bank, :], expert_row[:, b, :], up_bias[:, a:a + BANK],
                                         start=False, stop=True, skip_group_check=True)
                return last

            def down_tile(k, w):
                for n in range(2):
                    last = pe.matmul(ps[n * CAP:(n + 1) * CAP, Y, :], lhs(actT, k), w[:, n * BANK:(n + 1) * BANK],
                                     start=k == 0, stop=k == KT - 1, skip_group_check=True)
                return last

            def scatter(b, tiles=range(TT)):
                for t in tiles:
                    for n in range(2):
                        last = pe.matmul(ps[:, 2 * t + n, :], gatedT[:, b, 2 * n + t, :], y_e, start=False, stop=False, skip_group_check=True)
                return last

            pe.wait_ge(pick_ready, 1)
            pe.wait_ge(h2_ready, TT)
            gather(0).then_inc(gathered, 1)
            pe.wait_ge(xe_ready, 1)
            turn(x_e).then_inc(xT_done, 1)
            pe.wait_ge(first_gates, 1)
            turn_gated(1, Y).then_inc(first_ps, 1)
            pe.wait_ge(over_ready, 1)
            for n in range(4):
                pe.matmul(ps[:, n, 0:2], ident, routing[:, 0, E:E + 2], start=True, stop=False, skip_group_check=True)
            pe.wait_ge(down_bias_in, 32)
            pe.wait_ge(xT_ready, 1)
            with pe.Fori(0, E // UNROLL) as i:
                for u in range(UNROLL):
                    e = i * UNROLL + u
                    b = u % 2

                    def use(j):
                        n = N_FRONT + u * PER_EXPERT + j
                        pe.wait_ge(loaded[n % RING], i * (16 * TURNS) + 16 * (n // RING + 1))
                        return n

                    for k in range(KT):
                        n = use(k)
                        up_tile(b, k, ring[:, n % RING, :]).then_inc(freed, 1)
                        if k == 0:
                            pe.wait_ge(pick_ready, e + 2)
                            gather(1 - b).then_inc(gathered, 1)
                        if k == 2:
                            pe.wait_ge(xe_ready, e + 2)
                            turn(x_e).then_inc(xT_done, 1)
                        if k == 5:
                            pe.wait_ge(xT_ready, e + 2)
                            pe.wait_ge(gated_ready, e + 1)
                            turn_gated(b).then_inc(gT_done, 1)
                    up_biases(b).then_inc(up_done, 1)
                    pe.wait_ge(y_ready, e + 1)
                    scatter(1 - b)
                    pe.wait_ge(gT_ready, e + 1)
                    pe.wait_ge(act_ready, e + 1)
                    turn(act_v).then_inc(actT_done, 1)
                    pe.wait_ge(actT_ready, e + 1)
                    for j in range(DOWN_SLOTS):
                        n = use(UP_SLOTS + j)
                        w = slot(n, 2, D)
                        down_tile(2 * j, w[:, 0, :])
                        last = down_tile(2 * j + 1, w[:, 1, :])
                        last.then_inc(freed, 1)
            pe.wait_ge(y_ready, E + 1)
            for t in range(TT):
                scatter((E - 1) % 2, (t,)).then_inc((first_rows, scattered)[t], 1)

            pe.wait_ge(over_ready, 1)
            any_over = pe.value_load(over[0:1, ROUNDS * E:ROUNDS * E + 1])
            with pe.If(any_over > 0):
                done = pe.alloc_register("over_done_pe")
                pe.reg_mov(done, 0)
                with pe.Fori(1, ROUNDS) as r:
                    with pe.Fori(0, E) as e:
                        need = pe.value_load(over[0:1, bass.ds(r * E + e, 1)])
                        with pe.If(need > 0):
                            k = pe.snap(done)
                            pe.wait_ge(v_pick, k + 1)
                            gather(0).then_inc(v_gathered, 1)
                            pe.wait_ge(v_xe, k + 1)
                            turn(x_e).then_inc(v_xTd, 1)
                            pe.wait_ge(v_xT, k + 1)
                            turn_gated(0).then_inc(v_gTd, 1)
                            pe.wait_ge(v_loaded, k * (16 * PER_EXPERT) + 16 * PER_EXPERT)
                            for j in range(KT):
                                up_tile(0, j, ring[:, j, :])
                            up_biases(0).then_inc(v_up, 1)
                            pe.wait_ge(v_gT, k + 1)
                            pe.wait_ge(v_act, k + 1)
                            turn(act_v).then_inc(v_aTd, 1)
                            pe.wait_ge(v_aT, k + 1)
                            for j in range(KT):
                                last = down_tile(j, slot(UP_SLOTS + j // 2, 2, D)[:, j % 2, :])
                            last.then_inc(v_yd, 1)
                            pe.wait_ge(v_y, k + 1)
                            scatter(0).then_inc(scattered, 1)
                            pe.reg_add(done, done, 1)
                        pe.nop()
                pe.nop()
            pe.nop()


INPUTS = ["x", "norm1_g", "w_in", "q_a_norm_g", "kv_a_norm_g", "w_uq", "w_uk", "w_uv", "w_a_out", "w_b_out", "w_o",
          "norm2_g", "w_router", "b_router", "w_gate_up", "b_gate_up", "w_down", "b_down", "final_g"]


def kernel(**inputs):
    import concourse.bacc as bacc
    from concourse.bass_utils import run_bass_kernel_spmd

    nc = bacc.Bacc("TRN2", target_bir_lowering=False, num_devices=1)
    arrays, args = {}, []
    for name in INPUTS:
        a = np.ascontiguousarray(inputs[name])
        arrays[f"in_{name}"] = a
        args.append(nc.dram_tensor(f"in_{name}", a.shape, mybir.dt.from_np(a.dtype), kind="ExternalInput").ap())
    table = constants()[0]
    arrays["in_table"] = table
    args.append(nc.dram_tensor("in_table", table.shape, F32, kind="ExternalInput").ap())
    out = nc.dram_tensor("out", (1, SEQ, D), F32, kind="ExternalOutput").ap()
    build(nc, *args, out)
    return run_bass_kernel_spmd(nc, [arrays], core_ids=[0]).results[0]["out"]
```

```python
import math
from contextlib import ExitStack

import numpy as np

import concourse.bass as bass
from concourse import mybir

F32 = mybir.dt.float32
I32 = mybir.dt.int32
ALU = mybir.AluOpType
ACT = mybir.ActivationFunctionType
AX_X = mybir.AxisListType.X

P = 128
D = 1024
SEQ = 256
TT = SEQ // P
KT = D // P
EPS = 1e-5

HEADS = 8
HD = 64
AW = HEADS * HD
NOPE, ROPE = 64, 32
QK_B = NOPE + ROPE
Q_RANK, KV_RANK = 256, 128
LATENT = Q_RANK + KV_RANK + ROPE
OFF_LATENT = 3 * AW
OFF_GATES = OFF_LATENT + LATENT
SCALE_A = HD ** -0.5
SCALE_B = QK_B ** -0.5
PATTERNS = ((128, 1), (512, 4), (2048, 16))
NEG = -1e30
BIG = 3e38

E = 32
TOP = 4
F = D
LIMIT, ALPHA = 7.0, 1.702
CAP = 64
ROUNDS = SEQ // CAP
BANK = 512

SLOT = 2048
RING = 16
FRONT = [("latent", 2), ("qk", 4), ("v", 2), ("uq", 1), ("uk", 1), ("uv", 1), ("gates", 8), ("out", 4), ("wo", 4)]
FIRST = {}
for _name, _n in FRONT:
    FIRST[_name] = sum(n for _, n in FRONT[:len(FIRST)])
N_FRONT = sum(n for _, n in FRONT)
UP_SLOTS = KT
DOWN_SLOTS = KT // 2
PER_EXPERT = UP_SLOTS + DOWN_SLOTS
SPARE = (KT - 2, RING + 1, RING + 2)
UNROLL = RING // math.gcd(RING, PER_EXPERT)
TURNS = UNROLL * PER_EXPERT // RING


def constants():
    p = np.arange(P)
    ident = np.eye(P)
    inv = 10000.0 ** (-np.arange(0, ROPE, 2, dtype=np.float32) / ROPE)
    ang = np.arange(SEQ, dtype=np.float32)[:, None] * inv[None, :].astype(np.float32)
    cos, sin = np.cos(ang), np.sin(ang)
    rope_cos = np.concatenate([cos, cos], 1).reshape(TT, P, ROPE).transpose(1, 0, 2).reshape(P, -1)
    rope_sin = np.concatenate([sin, -sin], 1).reshape(TT, P, ROPE).transpose(1, 0, 2).reshape(P, -1)
    slot = np.arange(CAP)
    none = np.full(CAP, -5 * SEQ)
    slots = np.tile(np.concatenate([slot, none, none, slot]), (P, 1))
    before = (p[:, None] < p[None, :]).astype(np.float32)
    ones = np.ones((P, P))
    fold = np.tile(np.eye(E), (P // E, 1))
    delta = p[:, None] - (np.arange(SEQ + P)[None, :] - P)
    dist = np.abs(delta)
    count = sum(((delta % d == 0) & (dist <= w // 2)).astype(int) for w, d in PATTERNS)
    log_count = np.where(count > 0, np.log(np.maximum(count, 1)), NEG)
    parts = {"ident": ident, "cos": rope_cos, "sin": rope_sin, "slots": slots, "before": before,
             "ones": ones, "fold": fold, "dist": dist, "log_count": log_count}
    at, place = 0, {}
    for name, a in parts.items():
        place[name] = (at, a.shape[1])
        at += a.shape[1]
    return np.concatenate([a.astype(np.float32) for a in parts.values()], 1), place


def build(nc, x, norm1_g, w_in, q_a_norm_g, kv_a_norm_g, w_uq, w_uk, w_uv, w_a_out, w_b_out, w_o,
          norm2_g, w_router, b_router, w_gate_up, b_gate_up, w_down, b_down, final_g, table, out):
    place = constants()[1]
    table_width = sum(n for _, n in place.values())
    fixed_width = place["dist"][0]

    with ExitStack() as ctx:
        def sb(name, shape, dt=F32):
            return ctx.enter_context(nc.sbuf_tensor(name, shape, dt))

        def sem(name):
            return ctx.enter_context(nc.semaphore(name))

        ring = sb("ring", [P, RING, SLOT])
        xrow = sb("xrow", [P, TT, D])
        const = sb("const", [P, fixed_width])
        g1 = sb("g1", [P, KT])
        gq = sb("gq", [P, Q_RANK // P])
        gkv = sb("gkv", [P, 1])
        g2_col = sb("g2_col", [P, KT])
        router_w = sb("router_w", [P, KT, E])
        router_b = sb("router_b", [P, E])
        eps = sb("eps", [P, 8])
        sums = sb("sums", [P, 16])
        warm = sb("warm", [P, 2])
        soft = sb("soft", [P, 2, 8])
        logits = sb("logits", [P, TT, E + TOP])
        struck = sb("struck", [P, TT, E + TOP])
        best = sb("best", [P, TT, 8])
        strike = sb("strike", [P, TT, 8])
        chosen = sb("chosen", [P, TT, E])
        expo = sb("expo", [P, TT, E])
        routing = sb("routing", [P, TT, 2 * E])
        places = sb("places", [P, TT, ROUNDS * E])
        over = sb("over", [1, ROUNDS * E + 1], I32)
        areas = {"h": 2048, "a": 4096, "g": 4096 + TT * ROPE, "s": 3072, "o": 2048, "t": 2 * (SEQ + P)}
        arena = {n: sb(f"area_{n}", [P, w]) for n, w in areas.items()}

        def view(area, at, *shape):
            n = int(np.prod(shape))
            v = arena[area][:, at:at + n]
            if len(shape) == 2:
                v = v.rearrange("p (a b) -> p a b", a=shape[0])
            if len(shape) == 3:
                v = v.rearrange("p (a b c) -> p a b c", a=shape[0], b=shape[1])
            return v

        hT = view("h", 0, KT, SEQ)
        xs = view("a", 0, TT, D)
        qmT = view("a", 0, HEADS, SEQ)
        kT = view("a", 2048, HEADS // 2, SEQ)
        va = view("a", 3072, TT, AW)
        qTb = view("a", 0, HEADS, SEQ)
        kTb = view("a", 2048, HEADS, SEQ)
        qb = xrow[:, :, 0:HEADS * QK_B]
        kcat = view("g", 0, TT, HEADS, QK_B)
        cn = view("g", 1536, TT, Q_RANK + KV_RANK)
        cT = view("g", 2304, 3, SEQ)
        rope_a = view("g", 3072, TT, HEADS, ROPE)
        rope_b = view("g", 3584, TT, HEADS, ROPE)
        kr = view("g", 4096, TT, ROPE)
        gateT = view("g", 0, 2 * KT, SEQ)
        vb = view("s", 0, TT, AW)
        probs = view("s", 1024, 2, TT, SEQ)
        probsT = view("s", 2048, 2, TT, SEQ)
        oT = view("o", 0, HEADS, SEQ)
        kr_b, kr_c = sb("kr_b", [P, TT, ROPE]), sb("kr_c", [P, TT, ROPE])
        h2 = view("h", 0, TT, D)
        up_bias = view("a", 0, 2 * F)
        g2 = view("a", 2048, D)
        x2T = view("g", 2048, KT, SEQ)
        gate_c, up_c, sig, act_v = (view("g", 512 * n, BANK) for n in range(4))
        x_e = view("g", 2048, BANK)
        xT_e = view("g", 2560, 2, BANK)
        actT = view("g", 3584, BANK)
        gf = view("s", 0, D)
        y_e = view("s", 1024, BANK)
        pick = view("s", 1536, 2, TT, CAP)
        expert_row = view("s", 1792, 2, CAP)
        part_rows = view("s", 1920, TT, P)
        gated = view("o", 0, 2, TT, 4 * CAP)
        gatedT = view("o", 1024, 2, 4, P)
        bias_a = view("o", 1024, 2, SEQ + P)
        dist = arena["t"][:, 0:SEQ + P]
        log_count = arena["t"][:, SEQ + P:2 * (SEQ + P)]

        def cst(name):
            a, n = place[name]
            return const[:, a:a + n]
        ident = cst("ident")
        cos2 = cst("cos").rearrange("p (t n) -> p t n", t=TT)
        sin2 = cst("sin").rearrange("p (t n) -> p t n", t=TT)
        slots, before, ones, fold = (cst(n) for n in ("slots", "before", "ones", "fold"))

        spare = ((view("g", 0, D), view("g", D, D)), (view("a", 3072, D), view("s", 0, D)), (xrow[:, 0, :], xrow[:, 1, :]))

        ps = ctx.enter_context(nc.psum_tensor("ps", [P, 8, BANK], F32))
        GATE, UP, Y, MIX = 4, 5, 6, 7

        s_g1, s_g2c = sem("g1_loaded"), sem("g2_col_loaded")
        s_x, s_ident, s_const, s_tab, s_small, s_mid = (sem("x_loaded0"), sem("x_loaded1")), sem("ident_loaded"), sem("const_loaded"), sem("table_loaded"), sem("small_loaded"), sem("mid_loaded")
        s_xagain = sem("x_again")
        s_bias, s_gf = sem("bias_loaded"), sem("final_g_loaded")
        spared, opened = [sem(f"spare_loaded{n}") for n in range(len(SPARE))], sem("sums_opened")
        loaded = [sem(f"slot_loaded{s}") for s in range(RING)]
        freed = sem("ring_freed")
        squares, power, ms = sem("squares"), sem("power"), sem("mean_squares")
        xs_ready, hT_ps, hT_v, hT_a = sem("xs_ready"), sem("hT_ps"), sem("hT_vector"), sem("hT_scalar")
        zeroed, cleared = sem("zeroed"), sem("cleared")
        lat_sq, cn_ready, kr_ready = sem("latent_squares"), sem("cn_ready"), sem("kr_ready")
        q_ready, k_ready = sem("q_ready"), sem("k_ready")
        cT_ps, cT_ready = sem("cT_ps"), sem("cT_ready")
        va_ready = sem("va_ready")
        uq_half, qb_ready, kvb_ready = sem("uq_half"), sem("qb_ready"), sem("kvb_ready")
        roped, pool_step = sem("roped"), sem("pool_step")
        biased = sem("scores_bias_ready")
        s_done, max_ready, dve_step = sem("scores_done"), sem("max_ready"), sem("dve_step")
        exp_done, probs_ready = sem("exp_done"), sem("probs_ready")
        pT_ps, pT_ready, pv_done, o_ready = sem("probsT_ps"), sem("probsT_ready"), sem("pv_done"), sem("o_ready")
        bT_ps, bq_ready, bk_ready = sem("bT_ps"), sem("bq_ready"), sem("bk_ready")
        gz_ready, gates_on = sem("gate_z_ready"), sem("gates_on")
        ab_done, merged = sem("ab_done"), sem("merged")
        wo_done = sem("wo_done")
        x2_ready, x2_sq, h2_ready = sem("x2_ready"), sem("x2_squares"), sem("h2_ready")
        x2T_ps, x2T_v, x2T_a = sem("x2T_ps"), sem("x2T_vector"), sem("x2T_scalar")
        router_ready = sem("router_ready")
        part_done, part_ready, logit_done, top_ready, expo_ready = sem("part_done"), sem("part_ready"), sem("logit_done"), sem("top_ready"), sem("expo_ready")
        chosen_ready, rout_ready, count_done = sem("chosen_ready"), sem("rout_ready"), sem("count_done")
        first_gates, first_ps, down_bias_in = sem("first_gates"), sem("first_ps"), sem("down_bias_loaded")
        over_ready, moe_zero = sem("over_ready"), sem("moe_zero")
        pick_ready, gated_ready, gathered, xe_ready, xT_done, xT_ready = (sem(n) for n in ("pick_ready", "gated_ready", "gathered", "xe_ready", "xT_done", "xT_ready"))
        gT_done, gT_ready, up_done, clamped, sig_ready = (sem(n) for n in ("gatedT_done", "gatedT_ready", "up_done", "clamped", "sig_ready"))
        act_ready, actT_done, actT_ready, y_ready = (sem(n) for n in ("act_ready", "actT_done", "actT_ready", "y_ready"))
        first_banks = sem("first_banks_done")
        clamped2, raised, scattered = sem("clamped_up"), sem("raised"), sem("scattered")
        v_loaded, v_pick, v_gathered, v_xe, v_xTd, v_xT, v_gTd, v_gT = (sem("over_" + n) for n in (
            "loaded", "pick", "gathered", "xe", "xT_done", "xT", "gatedT_done", "gatedT"))
        v_up, v_cl, v_sig, v_act, v_aTd, v_aT, v_yd, v_y = (sem("over_" + n) for n in (
            "up_done", "clamped", "sig", "act", "actT_done", "actT", "y_done", "y"))
        v_gate, v_cl2, v_raised = sem("over_gate_done"), sem("over_clamped_up"), sem("over_raised")
        fin_sq, fin_ready, s_out = sem("fin_squares"), sem("fin_ready"), sem("stored")

        x_rows = x[0].rearrange("(t p) d -> p t d", p=P)
        out_rows = out[0].rearrange("(t p) d -> p t d", p=P)
        win = w_in[0].rearrange("(k p) n -> p k n", p=P)
        up_rows = w_gate_up[0].rearrange("e (k p) n -> p (e k) n", p=P)
        down_rows = w_down[0].rearrange("e (k p) n -> p (e k) n", p=P)
        ab_rows = [w[0].rearrange("(k p) n -> p k n", p=P) for w in (w_a_out, w_b_out)]
        wo_rows = w_o[0].rearrange("(k p) n -> p k n", p=P)

        def slot(n, *shape):
            v = ring[:, n % RING, 0:int(np.prod(shape))]
            if len(shape) == 2:
                v = v.rearrange("p (a b) -> p a b", a=shape[0])
            return v

        def place_of(n, first):
            r = n - sum(N_FRONT + m < n or not first for m in SPARE)
            return r % RING, r // RING + 1

        def last_in_slot(n):
            r = n - sum(N_FRONT + m < n for m in SPARE) - RING
            return next(m for m in range(n) if m - sum(N_FRONT + x < m for x in SPARE) == r and m - N_FRONT not in SPARE)

        def through(name):
            return FIRST[name] + dict(FRONT)[name]

        block = ctx.enter_context(nc.Block())

        @block.sync
        def _(sp):
            front = []
            for n in range(2):
                front.append((slot(n, 4, LATENT), win[:, 4 * n:4 * n + 4, OFF_LATENT:OFF_GATES]))
            for n in range(4):
                front.append((slot(FIRST["qk"] + n, 2, 2 * AW), win[:, 2 * n:2 * n + 2, 0:2 * AW]))
            for n in range(2):
                front.append((slot(FIRST["v"] + n, 4, AW), win[:, 4 * n:4 * n + 4, 2 * AW:3 * AW]))
            front.append((slot(FIRST["uq"], 2, HEADS * QK_B), w_uq[0].rearrange("(k p) h e -> p k (h e)", p=P)))
            front.append((slot(FIRST["uk"], HEADS * NOPE), w_uk[0].rearrange("p h e -> p (h e)")))
            front.append((slot(FIRST["uv"], HEADS * HD), w_uv[0].rearrange("p h e -> p (h e)")))
            for n in range(8):
                a = OFF_GATES + n * 2 * P
                front.append((slot(FIRST["gates"] + n, KT, 2 * P), win[:, :, a:a + 2 * P]))
            for half in range(2):
                for m in range(2):
                    front.append((slot(FIRST["out"] + 2 * half + m, 4, BANK),
                                  ab_rows[m][:, :, half * BANK:(half + 1) * BANK]))
            for n in range(4):
                front.append((slot(FIRST["wo"] + n, 2, D), wo_rows[:, 2 * n:2 * n + 2, :]))
            for t in range(TT):
                sp.dma_start(xrow[:, t:t + 1, :], x_rows[:, t:t + 1, :]).then_inc(s_x[t], 16)
            with nc.allow_non_contiguous_dma(reason="norm weights as columns, 1k words"):
                sp.dma_start(g1[:, :], norm1_g[0].rearrange("(k p) -> p k", p=P)).then_inc(s_g1, 16)
            for n, (dst, src) in enumerate(front):
                if n >= RING:
                    sp.wait_ge(freed, n - RING + 1)
                sp.dma_start(dst, src).then_inc(loaded[n % RING], 16)

            def expert_load(i, n, which=None):
                u, j = divmod(n - N_FRONT, PER_EXPERT)
                if j < UP_SLOTS:
                    src = up_rows[:, bass.ds(i * (UNROLL * KT) + (u * KT + j), 1), :]
                else:
                    src = down_rows[:, bass.ds(i * (UNROLL * KT) + (u * KT + 2 * (j - UP_SLOTS)), 2), :]
                if which is None:
                    at = place_of(n, isinstance(i, int))[0]
                    dst = ring[:, at:at + 1, :] if j < UP_SLOTS else slot(at, 2, D)
                    sp.dma_start(dst, src).then_inc(loaded[at], 16)
                else:
                    for part, dst in enumerate(spare[which]):
                        sp.dma_start(dst, src[:, 0, part * D:(part + 1) * D]).then_inc(spared[which], 16)

            before_wo = [m for m in range(RING + 1 - dict(FRONT)["wo"]) if m not in SPARE] + [SPARE[1]]
            filling = [m for m in range(RING + 1) if m not in SPARE and m not in before_wo] + [SPARE[0], SPARE[2]]
            for m in before_wo + filling + list(range(RING + 3, UNROLL * PER_EXPERT)):
                n = N_FRONT + m
                if m in SPARE:
                    which = SPARE.index(m)
                    if which == 0:
                        sp.wait_ge(freed, through("wo"))
                    if which == 1:
                        sp.wait_ge(freed, through("out"))
                    if which == 2:
                        sp.wait_ge(opened, 1)
                    expert_load(0, n, which)
                else:
                    sp.wait_ge(freed, last_in_slot(n) + 1)
                    expert_load(0, n)
            sp.wait_ge(freed, N_FRONT + SPARE[2] + 1)
            sp.dma_start(gf[:, :], final_g.rearrange("(a d) -> a d", a=1).to_broadcast([P, D])).then_inc(s_gf, 16)
            with sp.Fori(1, E // UNROLL) as i:
                for n in range(N_FRONT, N_FRONT + UNROLL * PER_EXPERT):
                    sp.wait_ge(freed, i * (UNROLL * PER_EXPERT) + (n - RING + 1))
                    expert_load(i, n)

            sp.wait_ge(freed, N_FRONT + E * PER_EXPERT)
            sp.wait_ge(over_ready, 1)
            any_over = sp.value_load(over[0:1, ROUNDS * E:ROUNDS * E + 1])
            with sp.If(any_over > 0):
                done = sp.alloc_register("over_done_sp")
                sp.reg_mov(done, 0)
                with sp.Fori(1, ROUNDS) as r:
                    with sp.Fori(0, E) as e:
                        need = sp.value_load(over[0:1, bass.ds(r * E + e, 1)])
                        with sp.If(need > 0):
                            k = sp.snap(done)
                            row = sp.snap(e * KT)
                            sp.reg_add(done, done, 1)
                            sp.wait_ge(scattered, k + 1)
                            for j in range(UP_SLOTS):
                                sp.dma_start(ring[:, j:j + 1, :], up_rows[:, bass.ds(row + j, 1), :]).then_inc(v_loaded, 16)
                            for j in range(DOWN_SLOTS):
                                sp.dma_start(slot(UP_SLOTS + j, 2, D), down_rows[:, bass.ds(row + 2 * j, 2), :]).then_inc(v_loaded, 16)
                        sp.nop()
                sp.nop()
            sp.nop()

        @block.gpsimd
        def _(pool):
            pool.memset(eps[:, :], -0.5).then_inc(zeroed, 1)
            pool.wait_ge(zeroed, 1)
            for t in range(TT):
                pool.wait_ge(ms, t + 1)
                pool.tensor_tensor(sums[:, 2 + t:3 + t], sums[:, 2 + t:3 + t], eps[:, 0:1], ALU.pow).then_inc(power, 1)
            pool.wait_ge(hT_ps, 4)
            pool.memset(qmT, 0.0).then_inc(cleared, 1)
            pool.wait_ge(ms, 3)
            pool.tensor_tensor(sums[:, 8:12], sums[:, 8:12], eps[:, 0:4], ALU.pow).then_inc(power, 1)
            steps = 0

            def turn(rows, a, b, heads):
                nonlocal steps
                half = ROPE // 2
                if heads:
                    c, s = (t.unsqueeze(2).to_broadcast([P, TT, HEADS, ROPE]) for t in (cos2, sin2))
                else:
                    c, s = cos2, sin2
                pool.tensor_tensor(a, rows, c, ALU.mult).then_inc(pool_step, 1)
                pool.tensor_tensor(b, rows, s, ALU.mult).then_inc(pool_step, 1)
                steps += 2
                pool.wait_ge(pool_step, steps)
                if heads:
                    pool.tensor_tensor(rows[:, :, :, 0:half], a[:, :, :, 0:half], b[:, :, :, half:ROPE], ALU.add)
                    return pool.tensor_tensor(rows[:, :, :, half:ROPE], a[:, :, :, half:ROPE], b[:, :, :, 0:half], ALU.add)
                pool.tensor_tensor(rows[:, :, 0:half], a[:, :, 0:half], b[:, :, half:ROPE], ALU.add)
                return pool.tensor_tensor(rows[:, :, half:ROPE], a[:, :, half:ROPE], b[:, :, 0:half], ALU.add)

            pool.wait_ge(s_const, 16)
            pool.wait_ge(kr_ready, 1)
            turn(kr, kr_c[:, :, :], kr_b[:, :, :], False).then_inc(pool_step, 1)
            steps += 1
            pool.wait_ge(pool_step, steps)
            pool.tensor_copy(kcat[:, :, :, NOPE:QK_B], kr.unsqueeze(2).to_broadcast([P, TT, HEADS, ROPE])).then_inc(roped, 1)
            pool.wait_ge(s_tab, 16)
            for k in range(HEADS):
                if k >= 2:
                    pool.wait_ge(max_ready, k - 1)
                pool.tensor_scalar(bias_a[:, k % 2, :], dist, -2.0 ** (-8.0 * (k + 1) / HEADS), None, ALU.mult).then_inc(pool_step, 1)
                steps += 1
                pool.wait_ge(pool_step, steps)
                pool.tensor_tensor(bias_a[:, k % 2, :], bias_a[:, k % 2, :], log_count, ALU.add).then_inc(biased, 1)
            pool.wait_ge(qb_ready, 2)
            turn(qb.rearrange("p t (h e) -> p t h e", h=HEADS)[:, :, :, NOPE:QK_B], rope_a, rope_b, True).then_inc(roped, 1)
            pool.wait_ge(s_done, 2 * HEADS)
            pool.memset(up_bias, 0.0).then_inc(cleared, 1)
            pool.wait_ge(pv_done, HEADS)
            pool.memset(y_e, 0.0).then_inc(cleared, 1)
            pool.memset(routing[:, :, :], 0.0).then_inc(moe_zero, 1)
            pool.memset(logits[:, :, E:E + TOP], BIG).then_inc(moe_zero, 1)
            pool.memset(strike[:, :, TOP:8], BIG).then_inc(moe_zero, 1)
            for n in range(2 * TT):
                t = n % TT
                pool.wait_ge(ms, 4 + n)
                pool.tensor_tensor(sums[:, 2 + t:3 + t], sums[:, 2 + t:3 + t], eps[:, 0:1], ALU.pow).then_inc(power, 1)
                if n == TT - 1:
                    pool.memset(gated[:, 1], 0.0).then_inc(moe_zero, 1)

        @block.scalar
        def _(act):
            act.dma_start(ident, table[:, 0:P]).then_inc(s_ident, 16)
            for t in range(TT):
                act.wait_ge(s_x[t], 16)
                act.activation(arena["h"][:, t * D:t * D + BANK], xrow[:, t, 0:BANK], ACT.Square, scale=D ** -0.5,
                               accum_out=sums[:, 12 + 2 * t:13 + 2 * t]).then_inc(squares, 1)
            act.wait_ge(s_g1, 16)
            act.wait_ge(squares, TT)
            for j in (2, 3):
                act.wait_ge(hT_ps, j + 1)
                for k in range(2):
                    last = act.activation(hT[:, 2 * j + k, :], ps[:, j, k * SEQ:(k + 1) * SEQ], ACT.Copy,
                                          scale=g1[:, 2 * j + k:2 * j + k + 1])
                last.then_inc(hT_a, 1)
            with nc.allow_non_contiguous_dma(reason="norm weights as columns, 1.4k words"):
                act.dma_start(gq[:, :], q_a_norm_g[0].rearrange("(k p) -> p k", p=P)).then_inc(s_small, 16)
                act.dma_start(gkv[:, :], kv_a_norm_g[0].rearrange("(k p) -> p k", p=P)).then_inc(s_small, 16)
                act.dma_start(g2_col[:, :], norm2_g[0].rearrange("(k p) -> p k", p=P)).then_inc(s_g2c, 16)
            act.dma_start(const[:, P:fixed_width], table[:, P:fixed_width]).then_inc(s_const, 16)
            act.dma_start(arena["t"][:, :], table[:, fixed_width:table_width]).then_inc(s_tab, 16)
            act.dma_start(router_w[:, :, :], w_router[0].rearrange("(k p) e -> p k e", p=P)).then_inc(s_mid, 16)
            act.dma_start(router_b[:, :], b_router[0:1, :].to_broadcast([P, E])).then_inc(s_mid, 16)
            for t in range(TT):
                act.wait_ge(freed, through("latent"))
                act.activation(cn[:, t, 0:Q_RANK], ps[:, 4 + t, 0:Q_RANK], ACT.Square, accum_out=sums[:, 4 + t:5 + t])
                act.activation(cn[:, t, Q_RANK:], ps[:, 4 + t, Q_RANK:Q_RANK + KV_RANK], ACT.Square,
                               accum_out=sums[:, 6 + t:7 + t]).then_inc(lat_sq, 1)
            act.wait_ge(freed, through("qk"))
            act.wait_ge(hT_ps, 4)
            for j in range(2):
                last = act.activation(kT[:, 2 * j:2 * j + 2, :], ps[:, 2 + j, :].rearrange("p (a b) -> p a b", a=2), ACT.Copy)
            last.then_inc(k_ready, 1)

            def exps(k):
                act.wait_ge(max_ready, k + 1)
                for t in range(TT):
                    src, scale = (probs[:, k % 2, t, :], 1.0) if k < HEADS else (ps[:, k % 2, t * SEQ:(t + 1) * SEQ], SCALE_B)
                    last = act.activation(probs[:, k % 2, t, :], src, ACT.Exp, bias=soft[:, k % 2, t:t + 1], scale=scale,
                                          accum_out=soft[:, k % 2, 2 + t:3 + t])
                last.then_inc(exp_done, 1)

            def take_probsT(k):
                act.wait_ge(pT_ps, k + 1)
                act.activation(probsT[:, k % 2], ps[:, 2 + k % 2, :].rearrange("p (a b) -> p a b", a=TT), ACT.Copy).then_inc(pT_ready, 1)

            exps(0)
            exps(1)
            act.wait_ge(freed, through("v"))
            for t in range(TT):
                last = act.activation(va[:, t, :], ps[:, 6 + t, :], ACT.Copy)
            last.then_inc(va_ready, 1)
            for p in range(HEADS // 2):
                for k in (2 * p, 2 * p + 1):
                    take_probsT(k)
                if p < HEADS // 2 - 1:
                    for k in (2 * p + 2, 2 * p + 3):
                        exps(k)
                if p < 2:
                    act.wait_ge(*((uq_half, 1), (freed, through("uq")))[p])
                    act.activation(qb[:, p, 0:5 * QK_B], ps[:, 6, 0:5 * QK_B], ACT.Copy)
                    act.activation(qb[:, p, 5 * QK_B:], ps[:, 7, 0:3 * QK_B], ACT.Copy).then_inc(qb_ready, 1)
                else:
                    act.wait_ge(freed, through(("uk", "uv")[p - 2]))
                    for t in range(TT):
                        if p == 2:
                            last = act.activation(kcat[:, t, :, 0:NOPE], ps[:, 6 + t, :].rearrange("p (h e) -> p h e", h=HEADS), ACT.Copy)
                        else:
                            last = act.activation(vb[:, t, :], ps[:, 6 + t, :], ACT.Copy)
                    last.then_inc(kvb_ready, 1)
            for p in range(HEADS // 2):
                act.wait_ge(bT_ps, 2 * p + 1)
                act.activation(qTb[0:QK_B, 2 * p:2 * p + 2, :], ps[0:QK_B, 4 + (2 * p + 2) % 4, :].rearrange("p (a b) -> p a b", a=2),
                               ACT.Copy).then_inc(bq_ready, 1)
            act.wait_ge(bT_ps, HEADS)
            act.dma_start(xrow[:, :, :], x_rows).then_inc(s_xagain, 16)
            exps(HEADS)
            exps(HEADS + 1)
            for k in range(HEADS, 2 * HEADS):
                take_probsT(k)
                if k + 2 < 2 * HEADS:
                    exps(k + 2)
            act.wait_ge(cleared, 2)
            act.dma_start(up_bias[0:E, :], b_gate_up[0]).then_inc(s_bias, 16)
            act.dma_start(g2[:, :], norm2_g[0:1, :].to_broadcast([P, D])).then_inc(s_bias, 16)
            act.wait_ge(cleared, 3)
            for n in range(2):
                act.dma_start(y_e[n * CAP:n * CAP + E, :], b_down[0][:, n * BANK:(n + 1) * BANK]).then_inc(down_bias_in, 16)
            for n in range(4):
                act.wait_ge(gz_ready, 8)
                act.activation(gateT[:, n:2 * KT:4, :], gateT[:, n:2 * KT:4, :], ACT.Sigmoid).then_inc(gates_on, 1)
            for t in range(TT):
                for n in range(2):
                    act.wait_ge(x2_ready, 2 * t + n + 1)
                    a = (2 * t + n) * BANK
                    act.activation(arena["o"][:, a:a + BANK], xrow[:, t, n * BANK:(n + 1) * BANK], ACT.Square, scale=D ** -0.5,
                                   accum_out=sums[:, 4 + 2 * t + n:5 + 2 * t + n]).then_inc(x2_sq, 1)
                act.wait_ge(x2T_ps, 2 * t + 2)
                act.activation(x2T[:, 4:8, t * P:(t + 1) * P], ps[:, 2 * t + 1, :].rearrange("p (a b) -> p a b", a=4), ACT.Copy).then_inc(x2T_a, 1)
            act.wait_ge(zeroed, 1)
            act.activation(warm[:, 0:1], eps[:, 0:1], ACT.Exp)
            for t in range(TT):
                act.wait_ge(top_ready, t + 1)
                last = act.activation(expo[:, t, :], logits[:, t, 0:E], ACT.Exp, bias=sums[:, 12 + t:13 + t])
            last.then_inc(expo_ready, 1)
            act.activation(warm[:, 1:2], eps[:, 0:1], ACT.Sigmoid)

            def take_mix(dst):
                return act.activation(dst, ps[:, MIX, :], ACT.Copy)

            act.wait_ge(gathered, 1)
            take_mix(x_e).then_inc(xe_ready, 1)
            act.wait_ge(xT_done, 1)
            take_mix(xT_e[:, 0]).then_inc(xT_ready, 1)
            act.wait_ge(first_ps, 1)
            act.activation(gatedT[:, 1].rearrange("p a b -> p (a b)"), ps[:, Y, :], ACT.Copy).then_inc(y_ready, 1)

            def experts(i, first=False):
                for u in range(UNROLL):
                    e = i * UNROLL + u

                    def next_tokens():
                        act.wait_ge(gathered, e + 2)
                        take_mix(x_e).then_inc(xe_ready, 1)
                        act.wait_ge(xT_done, e + 2)
                        take_mix(xT_e[:, (u + 1) % 2]).then_inc(xT_ready, 1)

                    if not first:
                        next_tokens()
                    act.wait_ge(gT_done, e + 1)
                    take_mix(gatedT[:, u % 2].rearrange("p a b -> p (a b)")).then_inc(gT_ready, 1)
                    act.wait_ge(clamped, e + 1)
                    act.activation(sig, gate_c, ACT.Sigmoid, scale=ALPHA).then_inc(sig_ready, 1)
                    if first:
                        next_tokens()
                    act.wait_ge(freed, i * (UNROLL * PER_EXPERT) + (N_FRONT + (u + 1) * PER_EXPERT))
                    act.activation(y_e, ps[:, Y, :], ACT.Copy).then_inc(y_ready, 1)

            experts(0, first=True)
            with act.Fori(1, E // UNROLL) as i:
                experts(i)

            act.wait_ge(over_ready, 1)
            any_over = act.value_load(over[0:1, ROUNDS * E:ROUNDS * E + 1])
            with act.If(any_over > 0):
                done = act.alloc_register("over_done_act")
                act.reg_mov(done, 0)
                with act.Fori(1, ROUNDS) as r:
                    with act.Fori(0, E) as e:
                        need = act.value_load(over[0:1, bass.ds(r * E + e, 1)])
                        with act.If(need > 0):
                            k = act.snap(done)
                            act.wait_ge(v_gathered, k + 1)
                            take_mix(x_e).then_inc(v_xe, 1)
                            act.wait_ge(v_xTd, k + 1)
                            take_mix(xT_e[:, 0]).then_inc(v_xT, 1)
                            act.wait_ge(v_gTd, k + 1)
                            take_mix(gatedT[:, 0].rearrange("p a b -> p (a b)")).then_inc(v_gT, 1)
                            act.wait_ge(v_cl, k + 1)
                            act.activation(sig, gate_c, ACT.Sigmoid, scale=ALPHA).then_inc(v_sig, 1)
                            act.wait_ge(v_yd, k + 1)
                            act.activation(y_e, ps[:, Y, :], ACT.Copy).then_inc(v_y, 1)
                            act.wait_ge(scattered, k + 2)
                            act.reg_add(done, done, 1)
                        act.nop()
                act.nop()
            for t in range(TT):
                for n in range(2):
                    act.wait_ge(*((first_banks, 1), (first_banks, 2), (first_banks, 3), (scattered, 1))[2 * t + n])
                    act.activation(h2[:, t, n * BANK:(n + 1) * BANK], ps[:, 2 * t + n, :], ACT.Square, scale=D ** -0.5,
                                   accum_out=sums[:, 4 + 2 * t + n:5 + 2 * t + n]).then_inc(fin_sq, 1)
            for m in range(2 * TT):
                t, a = m // 2, m % 2 * BANK
                act.wait_ge(fin_ready, m + 1)
                act.dma_start(out_rows[:, t:t + 1, a:a + BANK], xrow[:, t:t + 1, a:a + BANK]).then_inc(s_out, 16)
            act.wait_ge(s_out, 16 * 2 * TT)

        @block.vector
        def _(dve):
            step = [0]

            def step_wait():
                dve.wait_ge(dve_step, step[0])

            def stepped(ins):
                ins.then_inc(dve_step, 1)
                step[0] += 1

            for t in range(TT):
                dve.wait_ge(s_x[t], 16)
                stepped(dve.tensor_tensor_reduce(arena["h"][:, t * D + BANK:(t + 1) * D], xrow[:, t, BANK:D], xrow[:, t, BANK:D], 1.0 / D, 0.0,
                                                 ALU.mult, ALU.add, sums[:, 13 + 2 * t:14 + 2 * t]))
                step_wait()
                dve.wait_ge(squares, t + 1)
                dve.scalar_tensor_tensor(out=sums[:, 2 + t:3 + t], in0=sums[:, 12 + 2 * t:13 + 2 * t], scalar=EPS,
                                         in1=sums[:, 13 + 2 * t:14 + 2 * t], op0=ALU.add, op1=ALU.add).then_inc(ms, 1)
                dve.wait_ge(power, t + 1)
                dve.tensor_scalar(xs[:, t, :], xrow[:, t, :], sums[:, 2 + t:3 + t], None, ALU.mult).then_inc(xs_ready, 1)
            dve.wait_ge(s_g1, 16)
            for j in (0, 1):
                dve.wait_ge(hT_ps, j + 1)
                dve.tensor_tensor(hT[:, 2 * j:2 * j + 2, :], ps[:, j, :].rearrange("p (a b) -> p a b", a=2),
                                  g1[:, 2 * j:2 * j + 2].unsqueeze(2).to_broadcast([P, 2, SEQ]), ALU.mult).then_inc(hT_v, 1)
            dve.wait_ge(lat_sq, TT)
            stepped(dve.tensor_scalar(sums[:, 8:10], sums[:, 4:6], 1.0 / Q_RANK, EPS, ALU.mult, ALU.add))
            dve.tensor_scalar(sums[:, 10:12], sums[:, 6:8], 1.0 / KV_RANK, EPS, ALU.mult, ALU.add).then_inc(ms, 1)
            for t in range(TT):
                last = dve.tensor_copy(kr[:, t, :], ps[:, 4 + t, Q_RANK + KV_RANK:LATENT])
            last.then_inc(kr_ready, 1)
            dve.wait_ge(power, 3)
            for t in range(TT):
                dve.tensor_scalar(cn[:, t, 0:Q_RANK], ps[:, 4 + t, 0:Q_RANK], sums[:, 8 + t:9 + t], None, ALU.mult)
                last = dve.tensor_scalar(cn[:, t, Q_RANK:], ps[:, 4 + t, Q_RANK:Q_RANK + KV_RANK], sums[:, 10 + t:11 + t], None, ALU.mult)
            last.then_inc(cn_ready, 1)
            dve.wait_ge(freed, through("qk"))
            dve.wait_ge(cleared, 1)
            for j in range(2):
                for o in range(2):
                    last = dve.tensor_scalar(qmT[o * HD:(o + 1) * HD, 4 * j + o:4 * j + o + 3:2, :],
                                             ps[o * HD:(o + 1) * HD, j, :].rearrange("p (a b) -> p a b", a=2), SCALE_A, None, ALU.mult)
            last.then_inc(q_ready, 1)
            dve.wait_ge(s_small, 32)
            dve.wait_ge(cT_ps, 1)
            dve.tensor_tensor(cT[:, 0:2, :], ps[:, 4, :].rearrange("p (a b) -> p a b", a=2),
                              gq[:, :].unsqueeze(2).to_broadcast([P, 2, SEQ]), ALU.mult)
            dve.tensor_scalar(cT[:, 2, :], ps[:, 5, 0:SEQ], gkv[:, 0:1], None, ALU.mult).then_inc(cT_ready, 1)

            def maxes(k):
                dve.wait_ge(s_done, k + 1)
                b = k % 2
                if k < HEADS:
                    dve.wait_ge(biased, k + 1)
                    for t in range(TT):
                        at = P * (TT - 1 - t)
                        stepped(dve.tensor_tensor_reduce(probs[:, b, t, :], ps[:, b, t * SEQ:(t + 1) * SEQ], bias_a[:, b, at:at + SEQ], 1.0, -BIG,
                                                         ALU.add, ALU.max, soft[:, b, 6 + t:7 + t]))
                else:
                    stepped(dve.tensor_reduce(soft[:, b, 6:8], ps[:, b, :].rearrange("p (a b) -> p a b", a=TT), AX_X, ALU.max))
                step_wait()
                dve.tensor_scalar(soft[:, b, 0:2], soft[:, b, 6:8], -1.0 if k < HEADS else -SCALE_B, None, ALU.mult).then_inc(max_ready, 1)

            def norms(k):
                b = k % 2
                dve.wait_ge(exp_done, k + 1)
                stepped(dve.reciprocal(soft[:, b, 4:6], soft[:, b, 2:4]))
                step_wait()
                for t in range(TT):
                    last = dve.tensor_scalar(probs[:, b, t, :], probs[:, b, t, :], soft[:, b, 4 + t:5 + t], None, ALU.mult)
                last.then_inc(probs_ready, 1)

            def take_o(p):
                dve.wait_ge(pv_done, p + 1)
                dve.tensor_copy(oT[:, p, :], ps[:, 4 + p % 2, 0:SEQ]).then_inc(o_ready, 1)

            def take_gates(g):
                dve.wait_ge(freed, FIRST["gates"] + g + 1)
                dve.tensor_copy(gateT[:, 2 * g:2 * g + 2, :], ps[:, 6 + g % 2, :].rearrange("p (a b) -> p a b", a=2)).then_inc(gz_ready, 1)

            for p in range(HEADS // 2):
                for k in (2 * p, 2 * p + 1):
                    maxes(k)
                for k in (2 * p, 2 * p + 1):
                    norms(k)
                if p:
                    take_o(p - 1)
            take_o(3)
            for p in range(HEADS // 2):
                dve.wait_ge(bT_ps, 2 * p + 2)
                dve.tensor_copy(kTb[0:QK_B, 2 * p:2 * p + 2, :], ps[0:QK_B, 4 + (2 * p + 3) % 4, :].rearrange("p (a b) -> p a b", a=2)).then_inc(bk_ready, 1)
            maxes(HEADS)
            maxes(HEADS + 1)
            norms(HEADS)
            norms(HEADS + 1)
            take_gates(0)
            dve.wait_ge(s_mid, 32)
            dve.wait_ge(s_g2c, 16)
            dve.tensor_tensor(router_w[:, :, :], router_w[:, :, :], g2_col[:, :].unsqueeze(2).to_broadcast([P, KT, E]), ALU.mult).then_inc(router_ready, 1)
            for k in range(HEADS, 2 * HEADS):
                if k + 2 < 2 * HEADS:
                    maxes(k + 2)
                    norms(k + 2)
                if k > HEADS and k % 2 == 0:
                    take_o(k // 2 - 1)
                if k - HEADS < 7:
                    take_gates(k - HEADS + 1)
            take_o(7)
            for d in range(KT):
                dve.wait_ge(ab_done, d + 1)
                dve.wait_ge(gates_on, d % 4 + 1)
                stepped(dve.tensor_tensor(gateT[:, d:d + KT + 1:KT, :], gateT[:, d:d + KT + 1:KT, :],
                                          ps[:, d % 4, :].rearrange("p (a b) -> p a b", a=2), ALU.mult))
                step_wait()
                dve.tensor_tensor(gateT[:, d, :], gateT[:, d, :], gateT[:, KT + d, :], ALU.add).then_inc(merged, 1)
            dve.wait_ge(s_const, 16)
            dve.wait_ge(s_xagain, 16)
            dve.wait_ge(s_bias, 32)
            dve.wait_ge(moe_zero, 3)
            counts = ps[:, GATE, P:P + (TT + 1) * E]

            def residual(t, n):
                dve.wait_ge(*((wo_done, 1), (wo_done, 1), (wo_done, 2), (freed, through("wo")))[2 * t + n])
                dve.tensor_tensor(xrow[:, t, n * BANK:(n + 1) * BANK], xrow[:, t, n * BANK:(n + 1) * BANK], ps[:, 4 + 2 * t + n, :],
                                  ALU.add).then_inc(x2_ready, 1)

            def take_x2T(t):
                dve.wait_ge(x2T_ps, 2 * t + 1)
                dve.tensor_copy(x2T[:, 0:4, t * P:(t + 1) * P], ps[:, 2 * t, :].rearrange("p (a b) -> p a b", a=4)).then_inc(x2T_v, 1)

            def mean_square(t):
                return dve.scalar_tensor_tensor(out=sums[:, 2 + t:3 + t], in0=sums[:, 4 + 2 * t:5 + 2 * t], scalar=EPS,
                                                in1=sums[:, 5 + 2 * t:6 + 2 * t], op0=ALU.add, op1=ALU.add)

            def choose(t):
                dve.wait_ge(part_done, t + 1)
                dve.tensor_copy(part_rows[:, t, :], ps[:, 4, 0:P]).then_inc(part_ready, 1)
                dve.wait_ge(power, 4 + t)
                dve.wait_ge(logit_done, t + 1)
                stepped(dve.scalar_tensor_tensor(out=logits[:, t, 0:E], in0=ps[:, 5, t * E:(t + 1) * E], scalar=sums[:, 2 + t:3 + t],
                                                 in1=router_b[:, :], op0=ALU.mult, op1=ALU.add))
                step_wait()
                stepped(dve.max(best[:, t, :], logits[:, t, 0:E]))
                step_wait()
                stepped(dve.tensor_copy(strike[:, t, 0:TOP], best[:, t, 0:TOP]))
                dve.tensor_scalar(sums[:, 12 + t:13 + t], best[:, t, 0:1], -1.0, None, ALU.mult).then_inc(top_ready, 1)
                step_wait()
                stepped(dve.match_replace(struck[:, t, :], strike[:, t, :], logits[:, t, :], -BIG))
                step_wait()
                dve.tensor_scalar(chosen[:, t, :], struck[:, t, 0:E], -BIG, None, ALU.is_equal).then_inc(chosen_ready, 1)

            def normed(t, n):
                a = n * BANK
                dve.scalar_tensor_tensor(out=h2[:, t, a:a + BANK], in0=xrow[:, t, a:a + BANK], scalar=sums[:, 2 + t:3 + t], in1=g2[:, a:a + BANK],
                                         op0=ALU.mult, op1=ALU.mult).then_inc(h2_ready, 1)

            residual(0, 0)
            residual(0, 1)
            take_x2T(0)
            dve.wait_ge(x2_sq, 2)
            mean_square(0).then_inc(ms, 1)
            choose(0)
            residual(1, 0)
            normed(0, 0)
            take_x2T(1)
            normed(0, 1)
            residual(1, 1)
            dve.wait_ge(x2_sq, 4)
            mean_square(1).then_inc(ms, 1)
            choose(1)
            normed(1, 0)
            dve.wait_ge(chosen_ready, TT)
            dve.wait_ge(count_done, 1)
            stepped(dve.scalar_tensor_tensor(out=struck[:, :, 0:E], in0=counts[:, 0:TT * E].rearrange("p (t e) -> p t e", t=TT),
                                             scalar=1.0, in1=chosen[:, :, :], op0=ALU.add, op1=ALU.mult))
            step_wait()

            def build_places(r):
                return dve.tensor_scalar(places[:, :, r * E:(r + 1) * E], struck[:, :, 0:E], -float(1 + CAP * r), None, ALU.add)

            def build_picks(b, je):
                for t in range(TT):
                    last = dve.tensor_scalar(pick[:, b, t, :], slots[:, 0:CAP], places[:, t, bass.ds(je, 1)], None, ALU.is_equal)
                return last

            def build_gated(b, e, je):
                for t in range(TT):
                    dve.tensor_scalar(gated[:, b, t, :], slots, places[:, t, bass.ds(je, 1)], routing[:, t, bass.ds(e, 1)],
                                      ALU.is_equal, ALU.mult)
                return dve.tensor_copy(expert_row[:, b, :], ident[:, bass.ds(e, 1)].to_broadcast([P, CAP]))

            def clamp_gate():
                return dve.tensor_scalar(gate_c, ps[:, GATE, :], LIMIT, None, ALU.min)

            def clamp_up():
                return dve.tensor_scalar(up_c, ps[:, UP, :], LIMIT, -LIMIT, ALU.min, ALU.max)

            stepped(build_places(0))
            step_wait()
            build_picks(0, 0).then_inc(pick_ready, 1)
            normed(1, 1)
            build_picks(1, 1).then_inc(pick_ready, 1)
            for r in range(1, ROUNDS):
                stepped(build_places(r))
            for r in range(ROUNDS):
                stepped(dve.tensor_scalar(over[0:1, r * E:(r + 1) * E], counts[0:1, TT * E:(TT + 1) * E], float(CAP * r), None, ALU.is_gt))
            stepped(dve.tensor_reduce(sums[0:1, 14:15], counts[0:1, TT * E:(TT + 1) * E], AX_X, ALU.max))
            step_wait()
            dve.tensor_scalar(over[0:1, ROUNDS * E:ROUNDS * E + 1], sums[0:1, 14:15], float(CAP), None, ALU.is_gt).then_inc(over_ready, 1)
            dve.wait_ge(expo_ready, 1)
            stepped(dve.tensor_tensor(expo[:, :, :], expo[:, :, :], chosen[:, :, :], ALU.mult))
            step_wait()
            stepped(dve.tensor_reduce(sums[:, 4:6], expo[:, :, :], AX_X, ALU.add))
            step_wait()
            stepped(dve.reciprocal(sums[:, 6:8], sums[:, 4:6]))
            step_wait()
            for t in range(TT):
                last = dve.tensor_scalar(routing[:, t, 0:E], expo[:, t, :], sums[:, 6 + t:7 + t], None, ALU.mult)
            last.then_inc(rout_ready, 1)
            dve.wait_ge(rout_ready, 1)
            dve.wait_ge(moe_zero, 4)
            for n in range(2):
                a = n * 3 * CAP
                last = dve.tensor_copy(gated[:, 1, :, a:a + E], routing[:, :, 0:E])
            last.then_inc(first_gates, 1)
            build_gated(0, 0, 0).then_inc(gated_ready, 1)
            dve.wait_ge(first_ps, 1)
            build_gated(1, 1, 1).then_inc(gated_ready, 1)
            with dve.Fori(0, E // UNROLL) as i:
                for u in range(UNROLL):
                    e = i * UNROLL + u
                    dve.wait_ge(up_done, e + 1)
                    clamp_up().then_inc(clamped2, 1)
                    dve.wait_ge(freed, i * (UNROLL * PER_EXPERT) + (N_FRONT + u * PER_EXPERT + UP_SLOTS))
                    clamp_gate().then_inc(clamped, 1)
                    dve.wait_ge(clamped, e + 1)
                    dve.wait_ge(clamped2, e + 1)
                    dve.scalar_tensor_tensor(out=up_c, in0=up_c, scalar=1.0, in1=gate_c, op0=ALU.add, op1=ALU.mult).then_inc(raised, 1)
                    dve.wait_ge(raised, e + 1)
                    dve.wait_ge(sig_ready, e + 1)
                    dve.tensor_tensor(act_v, up_c, sig, ALU.mult).then_inc(act_ready, 1)
                    dve.wait_ge(actT_done, e + 1)
                    dve.tensor_copy(actT, ps[:, MIX, :]).then_inc(actT_ready, 1)
                    build_picks(u % 2, e + 2).then_inc(pick_ready, 1)
                    build_gated(u % 2, e + 2, e + 2).then_inc(gated_ready, 1)

            dve.wait_ge(over_ready, 1)
            any_over = dve.value_load(over[0:1, ROUNDS * E:ROUNDS * E + 1])
            with dve.If(any_over > 0):
                dve.wait_ge(scattered, 1)
                done = dve.alloc_register("over_done_dve")
                dve.reg_mov(done, 0)
                with dve.Fori(1, ROUNDS) as r:
                    with dve.Fori(0, E) as e:
                        need = dve.value_load(over[0:1, bass.ds(r * E + e, 1)])
                        with dve.If(need > 0):
                            k = dve.snap(done)
                            build_picks(0, r * E + e)
                            build_gated(0, e, r * E + e).then_inc(v_pick, 1)
                            dve.wait_ge(v_up, k + 1)
                            clamp_up().then_inc(v_cl2, 1)
                            dve.wait_ge(v_gate, k + 1)
                            clamp_gate().then_inc(v_cl, 1)
                            dve.wait_ge(v_cl, k + 1)
                            dve.wait_ge(v_cl2, k + 1)
                            dve.scalar_tensor_tensor(out=up_c, in0=up_c, scalar=1.0, in1=gate_c, op0=ALU.add, op1=ALU.mult).then_inc(v_raised, 1)
                            dve.wait_ge(v_raised, k + 1)
                            dve.wait_ge(v_sig, k + 1)
                            dve.tensor_tensor(act_v, up_c, sig, ALU.mult).then_inc(v_act, 1)
                            dve.wait_ge(v_aTd, k + 1)
                            dve.tensor_copy(actT, ps[:, MIX, :]).then_inc(v_aT, 1)
                            dve.wait_ge(scattered, k + 2)
                            dve.reg_add(done, done, 1)
                        dve.nop()
                dve.nop()
            def last_norm(t, n):
                dve.wait_ge(power, 6 + t)
                dve.scalar_tensor_tensor(out=xrow[:, t, n * BANK:(n + 1) * BANK], in0=ps[:, 2 * t + n, :], scalar=sums[:, 2 + t:3 + t],
                                         in1=gf[:, n * BANK:(n + 1) * BANK], op0=ALU.mult, op1=ALU.mult).then_inc(fin_ready, 1)

            dve.wait_ge(s_gf, 16)
            dve.wait_ge(fin_sq, 2)
            mean_square(0).then_inc(ms, 1)
            last_norm(0, 0)
            dve.wait_ge(fin_sq, 4)
            mean_square(1).then_inc(ms, 1)
            last_norm(0, 1)
            last_norm(1, 0)
            last_norm(1, 1)

        @block.tensor
        def _(pe):
            def arrived(n):
                pe.wait_ge(loaded[n % RING], 16 * (n // RING + 1))

            pe.wait_ge(s_ident, 16)
            for t in range(TT):
                pe.wait_ge(xs_ready, t + 1)
                for k in range(KT):
                    last = pe.transpose(ps[:, k // 2, k % 2 * SEQ + t * P:k % 2 * SEQ + (t + 1) * P], xs[:, t, k * P:(k + 1) * P], ident)
                    if t == TT - 1 and k % 2:
                        last.then_inc(hT_ps, 1)
            for k in range(KT):
                if k % 2 == 0:
                    pe.wait_ge((hT_v, hT_a)[k // 4], k // 2 % 2 + 1)
                if k % 4 == 0:
                    arrived(FIRST["latent"] + k // 4)
                w = slot(FIRST["latent"] + k // 4, 4, LATENT)
                for t in range(TT):
                    last = pe.matmul(ps[:, 4 + t, 0:LATENT], hT[:, k, t * P:(t + 1) * P], w[:, k % 4, :], start=k == 0, stop=k == KT - 1)
                if k == 3:
                    last.then_inc(freed, 1)
            last.then_inc(freed, 1)
            for k in range(KT):
                if k % 2 == 0:
                    arrived(FIRST["qk"] + k // 2)
                w = slot(FIRST["qk"] + k // 2, 2, 2 * AW)
                for c in range(8):
                    last = pe.matmul(ps[:, c // 2, c % 2 * SEQ:(c % 2 + 1) * SEQ], w[:, k % 2, c * P:(c + 1) * P], hT[:, k, :],
                                     start=k == 0 and c % 2 == 0, stop=k == KT - 1, skip_group_check=True)
                if k % 2:
                    last.then_inc(freed, 1)
            pe.wait_ge(cn_ready, 1)
            for c in range(3):
                for t in range(TT):
                    b, a = (4, c * SEQ) if c < 2 else (5, 0)
                    last = pe.transpose(ps[:, b, a + t * P:a + (t + 1) * P], cn[:, t, c * P:(c + 1) * P], ident)
            last.then_inc(cT_ps, 1)

            def scores(k):
                for t in range(TT):
                    if k < HEADS:
                        q, key = qmT[:, k, t * P:(t + 1) * P], kT[:, k // 2, :]
                    else:
                        q, key = qTb[0:QK_B, k - HEADS, t * P:(t + 1) * P], kTb[0:QK_B, k - HEADS, :]
                    last = pe.matmul(ps[:, k % 2, t * SEQ:(t + 1) * SEQ], q, key, start=True, stop=True)
                last.then_inc(s_done, 1)

            def turn_probs(k):
                pe.wait_ge(probs_ready, k + 1)
                if k >= 2:
                    pe.wait_ge(pT_ready, k - 1)
                for c in range(TT):
                    for t in range(TT):
                        last = pe.transpose(ps[:, 2 + k % 2, c * SEQ + t * P:c * SEQ + (t + 1) * P], probs[:, k % 2, t, c * P:(c + 1) * P], ident)
                last.then_inc(pT_ps, 1)

            def attend(p):
                pe.wait_ge(pT_ready, 2 * p + 2)
                if p >= 2:
                    pe.wait_ge(o_ready, p - 1)
                v = va if p < HEADS // 2 else vb
                for c in range(TT):
                    for o in range(2):
                        h = (2 * p + o) % HEADS
                        last = pe.matmul(ps[o * HD:(o + 1) * HD, 4 + p % 2, 0:SEQ], v[:, c, h * HD:(h + 1) * HD], probsT[:, o, c, :],
                                         start=c == 0, stop=c == TT - 1)
                last.then_inc(pv_done, 1)

            for k in range(KT):
                if k == 2:
                    pe.wait_ge(q_ready, 1)
                    pe.wait_ge(k_ready, 1)
                    scores(0)
                    scores(1)
                if k % 4 == 0:
                    arrived(FIRST["v"] + k // 4)
                w = slot(FIRST["v"] + k // 4, 4, AW)
                for t in range(TT):
                    last = pe.matmul(ps[:, 6 + t, :], hT[:, k, t * P:(t + 1) * P], w[:, k % 4, :], start=k == 0, stop=k == KT - 1)
                if k % 4 == 3:
                    last.then_inc(freed, 1)

            def latent_part(n):
                name = ("uq", "uq", "uk", "uv")[n]
                arrived(FIRST[name])
                pe.wait_ge(*((va_ready, 1), (qb_ready, 1), (qb_ready, 2), (kvb_ready, 1))[n])
                if n < 2:
                    w = slot(FIRST[name], 2, HEADS * QK_B)
                    for b, (a, z) in enumerate(((0, 5 * QK_B), (5 * QK_B, HEADS * QK_B))):
                        for c in range(2):
                            last = pe.matmul(ps[:, 6 + b, 0:z - a], cT[:, c, n * P:(n + 1) * P], w[:, c, a:z], start=c == 0, stop=c == 1)
                    last.then_inc((uq_half, freed)[n], 1)
                    return
                for t in range(TT):
                    last = pe.matmul(ps[:, 6 + t, :], cT[:, 2, t * P:(t + 1) * P], slot(FIRST[name], AW), start=True, stop=True)
                last.then_inc(freed, 1)

            for p in range(HEADS // 2):
                for k in (2 * p, 2 * p + 1):
                    turn_probs(k)
                    if k + 2 < HEADS:
                        scores(k + 2)
                if p == 0:
                    pe.wait_ge(cT_ready, 1)
                latent_part(p)
                attend(p)

            pe.wait_ge(roped, 2)
            pe.wait_ge(kvb_ready, 2)
            qb4 = qb.rearrange("p t (h e) -> p t h e", h=HEADS)
            for p in range(HEADS // 2):
                if p == 1:
                    pe.wait_ge(o_ready, HEADS // 2)
                for m, rows in enumerate((qb4, kcat)):
                    if p >= 2:
                        pe.wait_ge((bq_ready, bk_ready)[m], p - 1)
                    for o in range(2):
                        for t in range(TT):
                            last = pe.transpose(ps[0:QK_B, 4 + (2 * p + m + 2) % 4, o * SEQ + t * P:o * SEQ + (t + 1) * P],
                                                rows[:, t, 2 * p + o, :], ident)
                    last.then_inc(bT_ps, 1)

            def gates(g):
                n = FIRST["gates"] + g
                arrived(n)
                if g >= 2:
                    pe.wait_ge(gz_ready, g - 1)
                w = slot(n, KT, 2 * P)
                for c in range(2):
                    for k in range(KT):
                        last = pe.matmul(ps[:, 6 + g % 2, c * SEQ:(c + 1) * SEQ], w[:, k, c * P:(c + 1) * P], hT[:, k, :], start=k == 0, stop=k == KT - 1)
                last.then_inc(freed, 1)

            pe.wait_ge(bq_ready, 1)
            pe.wait_ge(bk_ready, 1)
            scores(HEADS)
            scores(HEADS + 1)
            pe.wait_ge(bq_ready, HEADS // 2)
            pe.wait_ge(bk_ready, HEADS // 2)
            gates(0)
            def mix_out(d, m):
                w = slot(FIRST["out"] + d // 4 * 2 + m, 4, BANK)
                for c in range(4):
                    last = pe.matmul(ps[:, d % 4, m * SEQ:(m + 1) * SEQ], w[:, c, d % 4 * P:(d % 4 + 1) * P], oT[:, 4 * m + c, :],
                                     start=c == 0, stop=c == 3)
                return last

            for p in range(HEADS // 2, HEADS):
                for k in (2 * p, 2 * p + 1):
                    turn_probs(k)
                    if k + 2 < 2 * HEADS:
                        scores(k + 2)
                    if k - HEADS < 7:
                        gates(k - HEADS + 1)
                if p == HEADS - 1:
                    arrived(FIRST["out"])
                    mix_out(0, 0)
                    mix_out(1, 0)
                attend(p)
            mix_out(2, 0)
            mix_out(3, 0).then_inc(freed, 1)
            pe.wait_ge(o_ready, HEADS)
            arrived(FIRST["out"] + 1)
            for d in range(4):
                mix_out(d, 1).then_inc(ab_done, 1)
            arrived(FIRST["out"] + 2)
            arrived(FIRST["out"] + 3)
            for d in range(4, KT):
                pe.wait_ge(merged, d - 3)
                last = mix_out(d, 0)
                if d in (4, 7):
                    last.then_inc(freed, 1)
                mix_out(d, 1).then_inc(ab_done, 1)

            def turn_rows(t, j):
                pe.wait_ge(x2_ready, 2 * t + j + 1)
                for k in range(4):
                    a = (4 * j + k) * P
                    last = pe.transpose(ps[:, 2 * t + j, k * P:(k + 1) * P], xrow[:, t, a:a + P], ident)
                last.then_inc(x2T_ps, 1)

            def route(t, j):
                pe.wait_ge((x2T_v, x2T_a)[j], t + 1)
                for q in range(4):
                    k = 4 * j + q
                    last = pe.matmul(ps[q * E:(q + 1) * E, 4, 0:P], router_w[:, k, :], x2T[:, k, t * P:(t + 1) * P], start=j == 0, stop=j == 1)
                if j == 1:
                    last.then_inc(part_done, 1)

            def add_parts(t):
                pe.wait_ge(part_ready, t + 1)
                pe.matmul(ps[:, 5, t * E:(t + 1) * E], part_rows[:, t, :], fold, start=True, stop=True).then_inc(logit_done, 1)

            def open_sums(t, n):
                return pe.matmul(ps[:, 2 * t + n, :], ident, xrow[:, t, n * BANK:(n + 1) * BANK], start=True, stop=False, skip_group_check=True)

            def project(t, k, n):
                w = slot(FIRST["wo"] + k // 2, 2, D)
                return pe.matmul(ps[:, 4 + 2 * t + n, :], gateT[:, k, t * P:(t + 1) * P], w[:, k % 2, n * BANK:(n + 1) * BANK],
                                 start=k == 0, stop=k == KT - 1)

            for k in range(KT):
                if k % 2 == 0:
                    arrived(FIRST["wo"] + k // 2)
                pe.wait_ge(merged, k + 1)
                for n in range(2):
                    last = project(0, k, n)
                if k == 0:
                    last.then_inc(freed, 1)
            last.then_inc(wo_done, 1)
            pe.wait_ge(router_ready, 1)
            pe.wait_ge(s_const, 16)
            for k in range(KT):
                last = project(1, k, 0)
                if k == 3:
                    turn_rows(0, 0)
                    turn_rows(0, 1)
                if k == 5:
                    route(0, 0)
                    route(0, 1)
            last.then_inc(wo_done, 1)
            add_parts(0)
            for k in range(KT):
                last = project(1, k, 1)
                if k % 2:
                    last.then_inc(freed, 1)
                if k == 3:
                    turn_rows(1, 0)
            open_sums(0, 0)
            turn_rows(1, 1)
            route(1, 0)
            route(1, 1)
            counts = ps[:, GATE, P:P + (TT + 1) * E]
            pe.wait_ge(chosen_ready, 1)
            add_parts(1)
            pe.matmul(counts[:, 0:E], before, chosen[:, 0, :], start=True, stop=True, skip_group_check=True)
            pe.matmul(counts[:, 2 * E:3 * E], ones, chosen[:, 0, :], start=True, stop=False, skip_group_check=True)
            pe.matmul(counts[:, E:2 * E], ones, chosen[:, 0, :], start=False, stop=False, skip_group_check=True)
            open_sums(0, 1)
            pe.wait_ge(chosen_ready, 2)
            pe.matmul(counts[:, E:2 * E], before, chosen[:, 1, :], start=False, stop=True, skip_group_check=True)
            pe.matmul(counts[:, 2 * E:3 * E], ones, chosen[:, 1, :], start=False, stop=True, skip_group_check=True).then_inc(count_done, 1)
            open_sums(1, 0)

            def gather(b, first=False):
                for t in range(TT):
                    if first:
                        pe.wait_ge(h2_ready, 2 * t + 2)
                    for n in range(2):
                        last = pe.matmul(ps[n * CAP:(n + 1) * CAP, MIX, :], pick[:, b, t, :], h2[:, t, n * BANK:(n + 1) * BANK],
                                         start=t == 0, stop=t == TT - 1)
                return last

            def turn(rows):
                for c in range(4):
                    last = pe.transpose(ps[:, MIX, c * P:(c + 1) * P], rows[:, c * P:(c + 1) * P], ident)
                return last

            def turn_gated(b, bank=MIX):
                for n in range(2):
                    for t in range(TT):
                        last = pe.transpose(ps[:, bank, (2 * n + t) * P:(2 * n + t + 1) * P], gated[:, b, t, n * P:(n + 1) * P], ident)
                return last

            def lhs(rows, k):
                a = k % 4 * P + k // 4 * CAP
                return rows[:, a:a + CAP]

            def halves(at):
                return ring[:, at, 0:F], ring[:, at, F:2 * F]

            def up_tile(b, k, w, up_sem):
                for bank in (UP, GATE):
                    for n in range(2):
                        last = pe.matmul(ps[n * CAP:(n + 1) * CAP, bank, :], lhs(xT_e[:, b], k), w[bank - GATE][:, n * BANK:(n + 1) * BANK],
                                         start=k == 0, stop=k == KT - 1, skip_group_check=True)
                    if bank == UP and k == KT - 1:
                        last.then_inc(up_sem, 1)
                return last

            def up_biases(b):
                for bank in (GATE, UP):
                    for n in range(2):
                        a = (bank - GATE) * F + n * BANK
                        pe.matmul(ps[n * CAP:(n + 1) * CAP, bank, :], expert_row[:, b, :], up_bias[:, a:a + BANK],
                                         start=False, stop=False, skip_group_check=True)

            def down_tile(k, w):
                for n in range(2):
                    last = pe.matmul(ps[n * CAP:(n + 1) * CAP, Y, :], lhs(actT, k), w[:, n * BANK:(n + 1) * BANK],
                                     start=k == 0, stop=k == KT - 1, skip_group_check=True)
                return last

            def scatter(b, n):
                t, half = divmod(n, 2)
                return pe.matmul(ps[:, n, :], gatedT[:, b, 2 * half + t, :], y_e, start=False, stop=False, skip_group_check=True)

            pe.wait_ge(pick_ready, 1)
            gather(0, first=True).then_inc(gathered, 1)
            open_sums(1, 1).then_inc(opened, 1)
            pe.wait_ge(xe_ready, 1)
            turn(x_e).then_inc(xT_done, 1)
            pe.wait_ge(first_gates, 1)
            turn_gated(1, Y).then_inc(first_ps, 1)
            pe.wait_ge(over_ready, 1)
            pe.wait_ge(down_bias_in, 32)
            pe.wait_ge(xT_ready, 1)
            def experts(i, first=False):
                for u in range(UNROLL):
                    e = i * UNROLL + u
                    b = u % 2

                    def use(j):
                        n = N_FRONT + u * PER_EXPERT + j
                        if first and n - N_FRONT in SPARE:
                            which = SPARE.index(n - N_FRONT)
                            pe.wait_ge(spared[which], 32)
                            return spare[which]
                        at, count = place_of(n, first)
                        pe.wait_ge(loaded[at], i * (16 * TURNS) + 16 * count)
                        return halves(at)

                    def next_rows():
                        pe.wait_ge(pick_ready, e + 2)
                        gather(1 - b).then_inc(gathered, 1)

                    def turn_next():
                        pe.wait_ge(xe_ready, e + 2)
                        turn(x_e).then_inc(xT_done, 1)

                    for k in range(KT):
                        up_tile(b, k, use(k), up_done).then_inc(freed, 1)
                        if k == 1 and not first:
                            next_rows()
                        if k == 3 and not first:
                            turn_next()
                        if k == 5:
                            if not first:
                                pe.wait_ge(xT_ready, e + 2)
                            pe.wait_ge(gated_ready, e + 1)
                            turn_gated(b).then_inc(gT_done, 1)
                        if k == 6:
                            up_biases(b)
                    pe.wait_ge(y_ready, e + 1)
                    for n in range(3):
                        scatter(1 - b, n)
                    pe.wait_ge(gT_ready, e + 1)
                    pe.wait_ge(act_ready, e + 1)
                    turn(act_v).then_inc(actT_done, 1)
                    scatter(1 - b, 3)
                    pe.wait_ge(actT_ready, e + 1)
                    for j in range(DOWN_SLOTS):
                        w = use(UP_SLOTS + j)
                        if j == 2 and first:
                            next_rows()
                        if j == 3 and first:
                            turn_next()
                        down_tile(2 * j, w[0])
                        down_tile(2 * j + 1, w[1]).then_inc(freed, 1)
                    if first:
                        pe.wait_ge(xT_ready, e + 2)

            experts(0, first=True)
            with pe.Fori(1, E // UNROLL) as i:
                experts(i)
            pe.wait_ge(y_ready, E + 1)
            for n in range(2 * TT):
                scatter((E - 1) % 2, n).then_inc(first_banks if n < 3 else scattered, 1)

            pe.wait_ge(over_ready, 1)
            any_over = pe.value_load(over[0:1, ROUNDS * E:ROUNDS * E + 1])
            with pe.If(any_over > 0):
                done = pe.alloc_register("over_done_pe")
                pe.reg_mov(done, 0)
                with pe.Fori(1, ROUNDS) as r:
                    with pe.Fori(0, E) as e:
                        need = pe.value_load(over[0:1, bass.ds(r * E + e, 1)])
                        with pe.If(need > 0):
                            k = pe.snap(done)
                            pe.wait_ge(v_pick, k + 1)
                            gather(0).then_inc(v_gathered, 1)
                            pe.wait_ge(v_xe, k + 1)
                            turn(x_e).then_inc(v_xTd, 1)
                            pe.wait_ge(v_xT, k + 1)
                            turn_gated(0).then_inc(v_gTd, 1)
                            pe.wait_ge(v_loaded, k * (16 * PER_EXPERT) + 16 * PER_EXPERT)
                            for j in range(KT):
                                last = up_tile(0, j, halves(j), v_up)
                                if j == 0:
                                    up_biases(0)
                            last.then_inc(v_gate, 1)
                            pe.wait_ge(v_gT, k + 1)
                            pe.wait_ge(v_act, k + 1)
                            turn(act_v).then_inc(v_aTd, 1)
                            pe.wait_ge(v_aT, k + 1)
                            for j in range(KT):
                                last = down_tile(j, slot(UP_SLOTS + j // 2, 2, D)[:, j % 2, :])
                            last.then_inc(v_yd, 1)
                            pe.wait_ge(v_y, k + 1)
                            for n in range(2 * TT):
                                last = scatter(0, n)
                            last.then_inc(scattered, 1)
                            pe.reg_add(done, done, 1)
                        pe.nop()
                pe.nop()
            pe.nop()


INPUTS = ["x", "norm1_g", "w_in", "q_a_norm_g", "kv_a_norm_g", "w_uq", "w_uk", "w_uv", "w_a_out", "w_b_out", "w_o",
          "norm2_g", "w_router", "b_router", "w_gate_up", "b_gate_up", "w_down", "b_down", "final_g"]


def kernel(**inputs):
    import concourse.bacc as bacc
    from concourse.bass_utils import run_bass_kernel_spmd

    nc = bacc.Bacc("TRN2", target_bir_lowering=False, num_devices=1)
    arrays, args = {}, []
    for name in INPUTS:
        a = np.ascontiguousarray(inputs[name])
        arrays[f"in_{name}"] = a
        args.append(nc.dram_tensor(f"in_{name}", a.shape, mybir.dt.from_np(a.dtype), kind="ExternalInput").ap())
    table = constants()[0]
    arrays["in_table"] = table
    args.append(nc.dram_tensor("in_table", table.shape, F32, kind="ExternalInput").ap())
    out = nc.dram_tensor("out", (1, SEQ, D), F32, kind="ExternalOutput").ap()
    build(nc, *args, out)
    return run_bass_kernel_spmd(nc, [arrays], core_ids=[0]).results[0]["out"]
```
